# Optimizing a Trainium2 kernel written in Bass

```python
import math
import jax, jax.numpy as jnp
from jax import lax
import numpy as np

D_MODEL = 1024
BATCH = 1
SEQ = 512
DEPTH = 2

GRID_W = 64
CTX_LEN = 256
N_MIXERS = 3
CHUNK = 64
CONV_K = 3
Q_BLOCK = 128
ROPE_BASE = 10000.0
EPS = 1e-6
ADA_CHUNKS = 6

GDN_HEADS = 8
GDN_HEAD_K = 128
GDN_HEAD_V = 128
GDN_KW = GDN_HEADS * GDN_HEAD_K
GDN_VW = GDN_HEADS * GDN_HEAD_V
GDN_IN = 2 * GDN_KW + 2 * GDN_VW + 4 * GDN_HEADS

SSD_INNER = 2 * D_MODEL
SSD_HEAD_DIM = 64
SSD_HEADS = SSD_INNER // SSD_HEAD_DIM
SSD_GROUPS = 8
SSD_STATE = 128
SSD_GN = SSD_GROUPS * SSD_STATE
SSD_CONV_CH = SSD_INNER + 2 * SSD_GN
SSD_IN = SSD_INNER + SSD_CONV_CH + 2 * SSD_HEADS

MLA_HEADS = 16
MLA_NOPE = 64
MLA_ROPE = 32
MLA_V = 64
MLA_Q_RANK = 768
MLA_KV_RANK = 256
MLA_IN = MLA_Q_RANK + MLA_KV_RANK + MLA_ROPE

N_EXPERTS = 16
EXPERT_FF = 1024
EC_CAPACITY = 2


F32 = jnp.float32

def rms_norm(x, g):
    xf = x.astype(F32)
    y = xf * lax.rsqrt(jnp.mean(xf * xf, axis=-1, keepdims=True) + EPS)
    return (y * g.astype(F32)).astype(x.dtype)

def _l2norm(x):
    xf = x.astype(F32)
    return (xf * lax.rsqrt(jnp.sum(xf * xf, axis=-1, keepdims=True) + EPS)).astype(x.dtype)

def _rev(a):
    return jnp.flip(a, axis=1)

def depthwise_conv(x, w):
    k = w.shape[0]
    return lax.conv_general_dilated(
        x, w[:, None, :].astype(x.dtype), window_strides=(1,), padding=[((k - 1) // 2, k // 2)],
        dimension_numbers=('NWC', 'WIO', 'NWC'), feature_group_count=x.shape[-1])

def ada_chunks(cvec, w, b):
    m = jax.nn.silu(cvec) @ w + b
    return jnp.split(m, ADA_CHUNKS, axis=-1)

def modulate(h, shift, scale):
    return h * (1 + scale) + shift

def axial_rope(x, rows, cols):
    def rot(xp, pos):
        d = xp.shape[-1]
        half = d // 2
        inv = ROPE_BASE ** (-jnp.arange(half, dtype=F32) * 2.0 / d)
        ang = pos.astype(F32)[:, None] * inv[None, :]
        cos = jnp.cos(ang)[None, :, None, :]
        sin = jnp.sin(ang)[None, :, None, :]
        x1 = xp[..., :half].astype(F32)
        x2 = xp[..., half:].astype(F32)
        return jnp.concatenate([x1 * cos - x2 * sin, x1 * sin + x2 * cos], -1).astype(xp.dtype)
    r = x.shape[-1] // 2
    return jnp.concatenate([rot(x[..., :r], rows), rot(x[..., r:], cols)], -1)

def gated_delta_scan(q, k, v, g, beta, s0):
    b, t, h, dk = q.shape
    dv = v.shape[-1]
    n = t // CHUNK

    def chunk(a):
        a = a.astype(F32).reshape((b, n, CHUNK) + a.shape[2:])
        return jnp.swapaxes(jnp.swapaxes(a, 0, 1), 2, 3)

    qc = chunk(q) * (dk ** -0.5)
    kc, vc, gc, bc = chunk(k), chunk(v), chunk(g), chunk(beta)
    gcum = jnp.cumsum(gc, axis=-1)
    tril = jnp.tril(jnp.ones((CHUNK, CHUNK), bool))
    strict = jnp.tril(jnp.ones((CHUNK, CHUNK), bool), -1)
    decay = jnp.exp(jnp.where(tril, gcum[..., :, None] - gcum[..., None, :], -jnp.inf))
    kb = kc * bc[..., None]
    lower = jnp.where(strict, jnp.einsum('nbhid,nbhjd->nbhij', kb, kc) * decay, 0.0)
    eye = jnp.broadcast_to(jnp.eye(CHUNK, dtype=F32), lower.shape)
    rhs = jnp.concatenate([vc * bc[..., None], kb * jnp.exp(gcum)[..., None]], axis=-1)
    sol = lax.linalg.triangular_solve(eye + lower, rhs, left_side=True, lower=True, unit_diagonal=True)
    u, w = sol[..., :dv], sol[..., dv:]
    attn = jnp.where(tril, jnp.einsum('nbhid,nbhjd->nbhij', qc, kc) * decay, 0.0)

    def step(S, inp):
        q_i, k_i, u_i, w_i, a_i, g_i = inp
        v_new = u_i - jnp.einsum('bhck,bhkv->bhcv', w_i, S)
        o = (jnp.einsum('bhck,bhkv->bhcv', q_i * jnp.exp(g_i)[..., None], S)
             + jnp.einsum('bhij,bhjv->bhiv', a_i, v_new))
        g_last = g_i[..., -1]
        S = (S * jnp.exp(g_last)[..., None, None]
             + jnp.einsum('bhck,bhcv->bhkv', k_i * jnp.exp(g_last[..., None] - g_i)[..., None], v_new))
        return S, o

    S, o = lax.scan(step, s0, (qc, kc, u, w, attn, gcum))
    o = jnp.swapaxes(jnp.swapaxes(o, 2, 3), 0, 1).reshape(b, t, h, dv)
    return o, S

def gdn_mixer(hx, hc, w_in, conv_w, a_log, dt_bias, norm_g, w_out):
    neg_a = -jnp.exp(a_log.astype(F32))

    def project(h):
        b, t, _ = h.shape
        p = h @ w_in
        qkv = jax.nn.silu(depthwise_conv(p[..., :2 * GDN_KW + GDN_VW], conv_w))
        q = _l2norm(qkv[..., :GDN_KW].reshape(b, t, GDN_HEADS, GDN_HEAD_K))
        k = _l2norm(qkv[..., GDN_KW:2 * GDN_KW].reshape(b, t, GDN_HEADS, GDN_HEAD_K))
        v = qkv[..., 2 * GDN_KW:].reshape(b, t, GDN_HEADS, GDN_HEAD_V)
        off = 2 * GDN_KW + GDN_VW
        z = p[..., off:off + GDN_VW].reshape(b, t, GDN_HEADS, GDN_HEAD_V)
        off += GDN_VW
        beta = jax.nn.sigmoid(p[..., off:off + 2 * GDN_HEADS].astype(F32)).reshape(b, t, 2, GDN_HEADS)
        off += 2 * GDN_HEADS
        g = neg_a * jax.nn.softplus(p[..., off:].astype(F32).reshape(b, t, 2, GDN_HEADS) + dt_bias.astype(F32))
        return q, k, v, z, g, beta

    def mix(h, s0f, s0b):
        b, t, _ = h.shape
        q, k, v, z, g, beta = project(h)
        of, sf = gated_delta_scan(q, k, v, g[:, :, 0], beta[:, :, 0], s0f)
        ob, sb = gated_delta_scan(_rev(q), _rev(k), _rev(v), _rev(g[:, :, 1]), _rev(beta[:, :, 1]), s0b)
        o = (of + _rev(ob)).astype(h.dtype)
        o = rms_norm(o, norm_g) * jax.nn.silu(z)
        return o.reshape(b, t, GDN_VW) @ w_out, sf, sb

    s0 = jnp.zeros((hc.shape[0], GDN_HEADS, GDN_HEAD_K, GDN_HEAD_V), F32)
    oc, sf, sb = mix(hc, s0, s0)
    ox, _, _ = mix(hx, sf, sb)
    return ox, oc

def ssd_scan(xs, dt, A, bm, cm, h0):
    b, t = xs.shape[:2]
    n = t // CHUNK

    def chunk(a):
        return jnp.swapaxes(a.astype(F32).reshape((b, n, CHUNK) + a.shape[2:]), 0, 1)

    tril = jnp.tril(jnp.ones((CHUNK, CHUNK), bool))[None, :, :, None, None]

    def step(h, inp):
        x_i, dt_i, b_i, c_i = inp
        acs = jnp.cumsum(dt_i * A, axis=1)
        seg = jnp.where(tril, acs[:, :, None] - acs[:, None, :], -jnp.inf)
        wts = jnp.einsum('btgn,bsgn->btsg', c_i, b_i)[..., None] * jnp.exp(seg) * dt_i[:, None]
        y = (jnp.einsum('btsgr,bsgrp->btgrp', wts, x_i)
             + jnp.einsum('btgn,bgrpn->btgrp', c_i, h) * jnp.exp(acs)[..., None])
        to_end = jnp.exp(acs[:, -1:] - acs) * dt_i
        h = (h * jnp.exp(acs[:, -1])[..., None, None]
             + jnp.einsum('bsgn,bsgr,bsgrp->bgrpn', b_i, to_end, x_i))
        return h, y

    h, y = lax.scan(step, h0, (chunk(xs), chunk(dt), chunk(bm), chunk(cm)))
    return jnp.swapaxes(y, 0, 1).reshape(xs.shape), h

def ssd_mixer(hx, hc, w_in, conv_w, conv_b, a_log, dt_bias, d_skip, norm_g, w_out):
    r = SSD_HEADS // SSD_GROUPS
    A = -jnp.exp(a_log.astype(F32)).reshape(2, SSD_GROUPS, r)

    def project(h):
        b, t, _ = h.shape
        p = h @ w_in
        z = p[..., :SSD_INNER]
        xbc = jax.nn.silu(depthwise_conv(p[..., SSD_INNER:SSD_INNER + SSD_CONV_CH], conv_w) + conv_b)
        dt = jax.nn.softplus((p[..., SSD_INNER + SSD_CONV_CH:] + dt_bias.reshape(-1)).astype(F32))
        dt = dt.reshape(b, t, 2, SSD_GROUPS, r)
        xs = xbc[..., :SSD_INNER].reshape(b, t, SSD_GROUPS, r, SSD_HEAD_DIM)
        bm = xbc[..., SSD_INNER:SSD_INNER + SSD_GN].reshape(b, t, SSD_GROUPS, SSD_STATE)
        cm = xbc[..., SSD_INNER + SSD_GN:].reshape(b, t, SSD_GROUPS, SSD_STATE)
        return z, xs, bm, cm, dt

    def mix(h, h0f, h0b):
        b, t, _ = h.shape
        z, xs, bm, cm, dt = project(h)
        yf, hf = ssd_scan(xs, dt[:, :, 0], A[0], bm, cm, h0f)
        yb, hb = ssd_scan(_rev(xs), _rev(dt[:, :, 1]), A[1], _rev(bm), _rev(cm), h0b)
        y = yf + _rev(yb) + d_skip.astype(F32).reshape(SSD_GROUPS, r)[..., None] * xs.astype(F32)
        y = y.reshape(b, t, SSD_INNER).astype(h.dtype) * jax.nn.silu(z)
        return rms_norm(y, norm_g) @ w_out, hf, hb

    h0 = jnp.zeros((hc.shape[0], SSD_GROUPS, r, SSD_HEAD_DIM, SSD_STATE), F32)
    oc, hf, hb = mix(hc, h0, h0)
    ox, _, _ = mix(hx, hf, hb)
    return ox, oc

def block_attention(q_nope, q_rope, k_nope, k_rope, v):
    b, t, h, _ = q_nope.shape
    nb = t // Q_BLOCK
    scale = (MLA_NOPE + MLA_ROPE) ** -0.5

    def blocks(a):
        return jnp.swapaxes(a.reshape((b, nb, Q_BLOCK) + a.shape[2:]), 0, 1)

    def one(args):
        qn, qr = args
        s = (jnp.einsum('bqhd,bkhd->bhqk', qn, k_nope).astype(F32)
             + jnp.einsum('bqhr,bkr->bhqk', qr, k_rope).astype(F32)) * scale
        p = jax.nn.softmax(s, axis=-1).astype(v.dtype)
        return jnp.einsum('bhqk,bkhd->bqhd', p, v)

    o = lax.map(one, (blocks(q_nope), blocks(q_rope)))
    return jnp.swapaxes(o, 0, 1).reshape(b, t, h, v.shape[-1])

def mla_mixer(hx, hc, w_in, q_norm_g, w_uq, kv_norm_g, w_ukv, w_out, rows, cols):
    def project(h, positioned):
        b, t, _ = h.shape
        p = h @ w_in
        cq = p[..., :MLA_Q_RANK]
        ckv = p[..., MLA_Q_RANK:MLA_Q_RANK + MLA_KV_RANK]
        kr = p[..., MLA_Q_RANK + MLA_KV_RANK:][:, :, None, :]
        q = (rms_norm(cq, q_norm_g) @ w_uq).reshape(b, t, MLA_HEADS, MLA_NOPE + MLA_ROPE)
        kv = (rms_norm(ckv, kv_norm_g) @ w_ukv).reshape(b, t, MLA_HEADS, MLA_NOPE + MLA_V)
        q_nope, q_rope = q[..., :MLA_NOPE], q[..., MLA_NOPE:]
        k_nope, v = kv[..., :MLA_NOPE], kv[..., MLA_NOPE:]
        if positioned:
            q_rope = axial_rope(q_rope, rows, cols)
            kr = axial_rope(kr, rows, cols)
        return q_nope, q_rope, k_nope, kr[:, :, 0], v

    qn_c, qr_c, kn_c, kr_c, v_c = project(hc, False)
    qn_x, qr_x, kn_x, kr_x, v_x = project(hx, True)
    oc = block_attention(qn_c, qr_c, kn_c, kr_c, v_c)
    ox = block_attention(qn_x, qr_x,
                         jnp.concatenate([kn_c, kn_x], axis=1),
                         jnp.concatenate([kr_c, kr_x], axis=1),
                         jnp.concatenate([v_c, v_x], axis=1))
    bx, tx = hx.shape[:2]
    bc, tc = hc.shape[:2]
    return (ox.reshape(bx, tx, MLA_HEADS * MLA_V) @ w_out,
            oc.reshape(bc, tc, MLA_HEADS * MLA_V) @ w_out)

def ec_moe(h, w_router, w_gate, w_up, w_down):
    b, n, _ = h.shape
    cap = EC_CAPACITY * n // N_EXPERTS
    aff = jax.nn.softmax((h @ w_router).astype(F32), axis=-1)
    gate, idx = lax.top_k(jnp.swapaxes(aff, 1, 2), cap)
    bidx = jnp.arange(b)[:, None, None]
    xs = h[bidx, idx]
    hid = jax.nn.silu(jnp.einsum('becd,edf->becf', xs, w_gate)) * jnp.einsum('becd,edf->becf', xs, w_up)
    y = jnp.einsum('becf,efd->becd', hid, w_down) * gate.astype(h.dtype)[..., None]
    return jnp.zeros_like(h).at[bidx, idx].add(y)

def first_inputs(seed: int = 0) -> dict:
    key = jax.random.key(seed)
    ks = iter(jax.random.split(key, 40))
    n_a = len(range(0, DEPTH, N_MIXERS))
    n_b = len(range(1, DEPTH, N_MIXERS))
    n_c = len(range(2, DEPTH, N_MIXERS))

    def nrm(shape, scale):
        return jax.random.normal(next(ks), shape, F32) * scale

    def gain(shape):
        return 1.0 + nrm(shape, 0.05)

    def a_log(shape):
        return jnp.log(jax.random.uniform(next(ks), shape, F32, 1.0, 16.0))

    def dt_bias(shape):
        dt = jnp.exp(jax.random.uniform(next(ks), shape, F32, math.log(1e-3), math.log(1e-1)))
        return dt + jnp.log(-jnp.expm1(-dt))

    d = D_MODEL
    return {
        "x": nrm((BATCH, SEQ, d), 1.0),
        "c": nrm((BATCH, d), 1.0),
        "ctx": nrm((BATCH, CTX_LEN, d), 1.0),
        "c_ctx": nrm((d,), 1.0),
        "ada_w": nrm((DEPTH, d, ADA_CHUNKS * d), 0.5 * d ** -0.5),
        "ada_b": nrm((DEPTH, ADA_CHUNKS * d), 0.02),
        "norm1_g": gain((DEPTH, d)),
        "norm2_g": gain((DEPTH, d)),
        "router_w": nrm((DEPTH, d, N_EXPERTS), d ** -0.5),
        "moe_w_gate": nrm((DEPTH, N_EXPERTS, d, EXPERT_FF), d ** -0.5),
        "moe_w_up": nrm((DEPTH, N_EXPERTS, d, EXPERT_FF), d ** -0.5),
        "moe_w_down": nrm((DEPTH, N_EXPERTS, EXPERT_FF, d), EXPERT_FF ** -0.5),
        "gdn_w_in": nrm((n_a, d, GDN_IN), d ** -0.5),
        "gdn_conv_w": nrm((n_a, CONV_K, 2 * GDN_KW + GDN_VW), CONV_K ** -0.5),
        "gdn_a_log": a_log((n_a, 2, GDN_HEADS)),
        "gdn_dt_bias": dt_bias((n_a, 2, GDN_HEADS)),
        "gdn_norm_g": gain((n_a, GDN_HEAD_V)),
        "gdn_w_out": nrm((n_a, GDN_VW, d), GDN_VW ** -0.5),
        "ssd_w_in": nrm((n_b, d, SSD_IN), d ** -0.5),
        "ssd_conv_w": nrm((n_b, CONV_K, SSD_CONV_CH), CONV_K ** -0.5),
        "ssd_conv_b": nrm((n_b, SSD_CONV_CH), 0.02),
        "ssd_a_log": a_log((n_b, 2, SSD_HEADS)),
        "ssd_dt_bias": dt_bias((n_b, 2, SSD_HEADS)),
        "ssd_d": 1.0 + nrm((n_b, SSD_HEADS), 0.1),
        "ssd_norm_g": gain((n_b, SSD_INNER)),
        "ssd_w_out": nrm((n_b, SSD_INNER, d), SSD_INNER ** -0.5),
        "mla_w_in": nrm((n_c, d, MLA_IN), d ** -0.5),
        "mla_q_norm_g": gain((n_c, MLA_Q_RANK)),
        "mla_w_uq": nrm((n_c, MLA_Q_RANK, MLA_HEADS * (MLA_NOPE + MLA_ROPE)), MLA_Q_RANK ** -0.5),
        "mla_kv_norm_g": gain((n_c, MLA_KV_RANK)),
        "mla_w_ukv": nrm((n_c, MLA_KV_RANK, MLA_HEADS * (MLA_NOPE + MLA_V)), MLA_KV_RANK ** -0.5),
        "mla_w_out": nrm((n_c, MLA_HEADS * MLA_V, d), (MLA_HEADS * MLA_V) ** -0.5),
        "final_norm_g": gain((d,)),
    }

def first_block(x, c, ctx, c_ctx, ada_w, ada_b, norm1_g, norm2_g, router_w, moe_w_gate, moe_w_up, moe_w_down,
              gdn_w_in, gdn_conv_w, gdn_a_log, gdn_dt_bias, gdn_norm_g, gdn_w_out,
              ssd_w_in, ssd_conv_w, ssd_conv_b, ssd_a_log, ssd_dt_bias, ssd_d, ssd_norm_g, ssd_w_out,
              mla_w_in, mla_q_norm_g, mla_w_uq, mla_kv_norm_g, mla_w_ukv, mla_w_out, final_norm_g):
    t = x.shape[1]
    ROWS = t // GRID_W
    rows = jnp.repeat(jnp.arange(ROWS, dtype=jnp.int32), GRID_W)
    cols = jnp.tile(jnp.arange(GRID_W, dtype=jnp.int32), ROWS)

    for i in range(DEPTH):
        last = i == DEPTH - 1
        mx = [m[:, None, :] for m in ada_chunks(c, ada_w[i], ada_b[i])]
        mc = ada_chunks(c_ctx, ada_w[i], ada_b[i])
        hx = modulate(rms_norm(x, norm1_g[i]), mx[0], mx[1])
        hc = modulate(rms_norm(ctx, norm1_g[i]), mc[0], mc[1])
        kind = i % N_MIXERS
        j = i // N_MIXERS
        if kind == 0:
            ox, oc = gdn_mixer(hx, hc, gdn_w_in[j], gdn_conv_w[j], gdn_a_log[j], gdn_dt_bias[j],
                               gdn_norm_g[j], gdn_w_out[j])
        elif kind == 1:
            ox, oc = ssd_mixer(hx, hc, ssd_w_in[j], ssd_conv_w[j], ssd_conv_b[j], ssd_a_log[j],
                               ssd_dt_bias[j], ssd_d[j], ssd_norm_g[j], ssd_w_out[j])
        else:
            ox, oc = mla_mixer(hx, hc, mla_w_in[j], mla_q_norm_g[j], mla_w_uq[j], mla_kv_norm_g[j],
                               mla_w_ukv[j], mla_w_out[j], rows, cols)
        x = x + mx[2] * ox
        hx = modulate(rms_norm(x, norm2_g[i]), mx[3], mx[4])
        x = x + mx[5] * ec_moe(hx, router_w[i], moe_w_gate[i], moe_w_up[i], moe_w_down[i])
        if not last:
            ctx = ctx + mc[2] * oc
            hc = modulate(rms_norm(ctx, norm2_g[i]), mc[3], mc[4])
            ctx = ctx + mc[5] * ec_moe(hc, router_w[i], moe_w_gate[i], moe_w_up[i], moe_w_down[i])

    return rms_norm(x, final_norm_g)


FOX_HEADS = 8
FOX_HEAD_DIM = 64
FOX_WIDTH = FOX_HEADS * FOX_HEAD_DIM
POOL_WINDOWS = (2, 4, 8, 16)
POOL_GROUPS = len(POOL_WINDOWS)
POOL_WIDTH = D_MODEL - FOX_WIDTH
POOL_GROUP_DIM = POOL_WIDTH // POOL_GROUPS
EVEN_IN_WIDTH = 3 * FOX_WIDTH + FOX_HEADS + POOL_WIDTH
LRU_WIDTH = D_MODEL
LRU_HEADS = 4
LRU_HEAD_DIM = LRU_WIDTH // LRU_HEADS
CONV_WIDTH = 4
LRU_C = 8.0
D_FF = -(-8 * D_MODEL // (3 * 256)) * 256
RMS_EPS = 1e-6


def rmsnorm(x, g):
    xf = x.astype(jnp.float32)
    y = xf * lax.rsqrt(jnp.mean(xf * xf, axis=-1, keepdims=True) + RMS_EPS)
    return (y * g.astype(jnp.float32)).astype(x.dtype)

def swiglu(h, w_gate, w_up, w_down):
    return (jax.nn.silu(h @ w_gate) * (h @ w_up)) @ w_down

def forgetting_attention(q, k, v, log_f):
    B, S, H, Dh = q.shape
    n_blk = S // Q_BLOCK
    scale = Dh ** -0.5
    c = jnp.cumsum(log_f, axis=1).transpose(0, 2, 1)
    q_blocks = q.reshape(B, n_blk, Q_BLOCK, H, Dh).transpose(1, 0, 3, 2, 4)
    c_blocks = c.reshape(B, H, n_blk, Q_BLOCK).transpose(2, 0, 1, 3)
    k_pos = jnp.arange(S, dtype=jnp.int32)

    def one_block(args):
        qb, cb, i = args
        s = jnp.einsum('bhqd,bshd->bhqs', qb, k, preferred_element_type=jnp.float32)
        s = s * scale + cb[..., None] - c[:, :, None, :]
        q_pos = i * Q_BLOCK + jnp.arange(Q_BLOCK, dtype=jnp.int32)
        mask = k_pos[None, :] <= q_pos[:, None]
        s = jnp.where(mask, s, -jnp.inf)
        p = jax.nn.softmax(s, axis=-1)
        return jnp.einsum('bhqs,bshd->bqhd', p.astype(v.dtype), v)

    out = lax.map(one_block, (q_blocks, c_blocks, jnp.arange(n_blk, dtype=jnp.int32)))
    return out.transpose(1, 0, 2, 3, 4).reshape(B, S, H * Dh)

def multiscale_pool(u, pool_w, pool_scale):
    B, S, _ = u.shape
    uf = u.astype(jnp.float32).reshape(B, S, POOL_GROUPS, POOL_GROUP_DIM)
    cs = jnp.cumsum(uf, axis=1)
    t1 = jnp.arange(1, S + 1, dtype=jnp.float32)
    pooled = []
    for g, w in enumerate(POOL_WINDOWS):
        cg = cs[:, :, g]
        lagged = jnp.pad(cg, ((0, 0), (w, 0), (0, 0)))[:, :S]
        mean = (cg - lagged) / jnp.minimum(t1, float(w))[None, :, None]
        pooled.append(mean - uf[:, :, g])
    pooled = jnp.stack(pooled, axis=2)
    mixed = jnp.einsum('bsgd,gde->bsge', pooled, pool_w.astype(jnp.float32))
    return (mixed.reshape(B, S, POOL_WIDTH) * pool_scale.astype(jnp.float32)).astype(u.dtype)

def even_mixer(h, w_in, b_f, pool_w, pool_scale, w_out):
    B, S, _ = h.shape
    proj = h @ w_in
    q, k, v, f_logit, u = jnp.split(
        proj, [FOX_WIDTH, 2 * FOX_WIDTH, 3 * FOX_WIDTH, 3 * FOX_WIDTH + FOX_HEADS], axis=-1)
    q = q.reshape(B, S, FOX_HEADS, FOX_HEAD_DIM)
    k = k.reshape(B, S, FOX_HEADS, FOX_HEAD_DIM)
    v = v.reshape(B, S, FOX_HEADS, FOX_HEAD_DIM)
    log_f = jax.nn.log_sigmoid(f_logit.astype(jnp.float32) + b_f.astype(jnp.float32))
    attn = forgetting_attention(q, k, v, log_f)
    pool = multiscale_pool(u, pool_w, pool_scale)
    return jnp.concatenate([attn, pool.astype(attn.dtype)], axis=-1) @ w_out

def causal_depthwise_conv(x, conv_w, conv_b):
    C = x.shape[-1]
    y = lax.conv_general_dilated(
        x, conv_w[:, None, :], window_strides=(1,), padding=[(CONV_WIDTH - 1, 0)],
        dimension_numbers=('NWC', 'WIO', 'NWC'), feature_group_count=C)
    return y + conv_b

def rg_lru(x, w_a, b_a, w_x, b_x, lam):
    B, S, W = x.shape
    xf = x.astype(jnp.float32)
    xh = xf.reshape(B, S, LRU_HEADS, LRU_HEAD_DIM)
    r = jax.nn.sigmoid(jnp.einsum('bshd,hde->bshe', xh, w_a.astype(jnp.float32)).reshape(B, S, W)
                       + b_a.astype(jnp.float32))
    i = jax.nn.sigmoid(jnp.einsum('bshd,hde->bshe', xh, w_x.astype(jnp.float32)).reshape(B, S, W)
                       + b_x.astype(jnp.float32))
    log_a = -LRU_C * r * jax.nn.softplus(-lam.astype(jnp.float32))
    a = jnp.exp(log_a)
    b = jnp.sqrt(-jnp.expm1(2.0 * log_a)) * (i * xf)

    def combine(c1, c2):
        a1, b1 = c1
        a2, b2 = c2
        return a1 * a2, a2 * b1 + b2

    _, hs = lax.associative_scan(combine, (a, b), axis=1)
    return hs.astype(x.dtype)

def odd_mixer(h, w_in, conv_w, conv_b, w_a, b_a, w_x, b_x, lam, w_out):
    proj = h @ w_in
    gate, xr = jnp.split(proj, 2, axis=-1)
    xr = causal_depthwise_conv(xr, conv_w, conv_b)
    y = rg_lru(xr, w_a, b_a, w_x, b_x, lam)
    return (jax.nn.gelu(gate) * y) @ w_out

def second_inputs(seed: int = 0) -> dict:
    key = jax.random.key(seed)
    ks = jax.random.split(key, 32)
    f32 = jnp.float32
    ne = (DEPTH + 1) // 2
    no = DEPTH // 2

    def nrm(k, shape, scale):
        return jax.random.normal(k, shape, f32) * scale

    def gain(k, shape):
        return 1.0 + 0.05 * jax.random.normal(k, shape, f32)

    u = jax.random.uniform(ks[24], (no, LRU_WIDTH), f32, minval=0.9, maxval=0.999)
    s = u ** (1.0 / LRU_C)
    lam = jnp.log(s) - jnp.log1p(-s)
    return {
        "x": jax.random.normal(ks[0], (BATCH, SEQ, D_MODEL), f32),
        "mix_pre_g": gain(ks[1], (DEPTH, D_MODEL)),
        "mix_post_g": gain(ks[2], (DEPTH, D_MODEL)),
        "ffn_pre_g": gain(ks[3], (DEPTH, D_MODEL)),
        "ffn_post_g": gain(ks[4], (DEPTH, D_MODEL)),
        "ffn_w_gate": nrm(ks[5], (DEPTH, D_MODEL, D_FF), D_MODEL ** -0.5),
        "ffn_w_up": nrm(ks[6], (DEPTH, D_MODEL, D_FF), D_MODEL ** -0.5),
        "ffn_w_down": nrm(ks[7], (DEPTH, D_FF, D_MODEL), D_FF ** -0.5),
        "ev_w_in": nrm(ks[8], (ne, D_MODEL, EVEN_IN_WIDTH), D_MODEL ** -0.5),
        "ev_b_f": jax.random.uniform(ks[9], (ne, FOX_HEADS), f32, minval=1.0, maxval=6.0),
        "ev_pool_w": nrm(ks[10], (ne, POOL_GROUPS, POOL_GROUP_DIM, POOL_GROUP_DIM), POOL_GROUP_DIM ** -0.5),
        "ev_pool_scale": 1.0 + 0.1 * jax.random.normal(ks[11], (ne, POOL_WIDTH), f32),
        "ev_w_out": nrm(ks[12], (ne, D_MODEL, D_MODEL), D_MODEL ** -0.5),
        "od_w_in": nrm(ks[13], (no, D_MODEL, 2 * LRU_WIDTH), D_MODEL ** -0.5),
        "od_conv_w": nrm(ks[14], (no, CONV_WIDTH, LRU_WIDTH), CONV_WIDTH ** -0.5),
        "od_conv_b": nrm(ks[15], (no, LRU_WIDTH), 0.01),
        "od_w_a": nrm(ks[16], (no, LRU_HEADS, LRU_HEAD_DIM, LRU_HEAD_DIM), LRU_HEAD_DIM ** -0.5),
        "od_b_a": nrm(ks[17], (no, LRU_WIDTH), 0.01),
        "od_w_x": nrm(ks[18], (no, LRU_HEADS, LRU_HEAD_DIM, LRU_HEAD_DIM), LRU_HEAD_DIM ** -0.5),
        "od_b_x": nrm(ks[19], (no, LRU_WIDTH), 0.01),
        "od_lam": lam,
        "od_w_out": nrm(ks[20], (no, LRU_WIDTH, D_MODEL), LRU_WIDTH ** -0.5),
    }

def second_block(x, mix_pre_g, mix_post_g, ffn_pre_g, ffn_post_g, ffn_w_gate, ffn_w_up, ffn_w_down,
              ev_w_in, ev_b_f, ev_pool_w, ev_pool_scale, ev_w_out,
              od_w_in, od_conv_w, od_conv_b, od_w_a, od_b_a, od_w_x, od_b_x, od_lam, od_w_out):
    for layer in range(DEPTH):
        h = rmsnorm(x, mix_pre_g[layer])
        if layer % 2 == 0:
            e = layer // 2
            m = even_mixer(h, ev_w_in[e], ev_b_f[e], ev_pool_w[e], ev_pool_scale[e], ev_w_out[e])
        else:
            o = layer // 2
            m = odd_mixer(h, od_w_in[o], od_conv_w[o], od_conv_b[o], od_w_a[o], od_b_a[o],
                          od_w_x[o], od_b_x[o], od_lam[o], od_w_out[o])
        x = x + rmsnorm(m, mix_post_g[layer])
        h = rmsnorm(x, ffn_pre_g[layer])
        x = x + rmsnorm(swiglu(h, ffn_w_gate[layer], ffn_w_up[layer], ffn_w_down[layer]), ffn_post_g[layer])
    return x


def setup_inputs(seed=0):
    out = dict(first_inputs(seed))
    for name, value in second_inputs(seed + 1).items():
        if name != "x":
            out[name + "_2"] = value
    return out


def reference(
    x, c, ctx, c_ctx, ada_w, ada_b, norm1_g, norm2_g, router_w, moe_w_gate, moe_w_up,
    moe_w_down, gdn_w_in, gdn_conv_w, gdn_a_log, gdn_dt_bias, gdn_norm_g, gdn_w_out, ssd_w_in,
    ssd_conv_w, ssd_conv_b, ssd_a_log, ssd_dt_bias, ssd_d, ssd_norm_g, ssd_w_out, mla_w_in,
    mla_q_norm_g, mla_w_uq, mla_kv_norm_g, mla_w_ukv, mla_w_out, final_norm_g, mix_pre_g_2,
    mix_post_g_2, ffn_pre_g_2, ffn_post_g_2, ffn_w_gate_2, ffn_w_up_2, ffn_w_down_2, ev_w_in_2,
    ev_b_f_2, ev_pool_w_2, ev_pool_scale_2, ev_w_out_2, od_w_in_2, od_conv_w_2, od_conv_b_2,
    od_w_a_2, od_b_a_2, od_w_x_2, od_b_x_2, od_lam_2, od_w_out_2,
):
    x = first_block(
        x, c, ctx, c_ctx, ada_w, ada_b, norm1_g, norm2_g, router_w, moe_w_gate, moe_w_up,
        moe_w_down, gdn_w_in, gdn_conv_w, gdn_a_log, gdn_dt_bias, gdn_norm_g, gdn_w_out,
        ssd_w_in, ssd_conv_w, ssd_conv_b, ssd_a_log, ssd_dt_bias, ssd_d, ssd_norm_g, ssd_w_out,
        mla_w_in, mla_q_norm_g, mla_w_uq, mla_kv_norm_g, mla_w_ukv, mla_w_out, final_norm_g,
    )
    return second_block(
        x, mix_pre_g_2, mix_post_g_2, ffn_pre_g_2, ffn_post_g_2, ffn_w_gate_2, ffn_w_up_2,
        ffn_w_down_2, ev_w_in_2, ev_b_f_2, ev_pool_w_2, ev_pool_scale_2, ev_w_out_2, od_w_in_2,
        od_conv_w_2, od_conv_b_2, od_w_a_2, od_b_a_2, od_w_x_2, od_b_x_2, od_lam_2, od_w_out_2,
    )


_drawn_inputs = setup_inputs


def setup_inputs(seed=0):
    import zlib

    import numpy as np

    out = dict(_drawn_inputs(seed))
    spreads = {}
    factors = {'gdn_norm_g': 2.979,
     'ssd_conv_b': 3.357,
     'ssd_d': 3.058,
     'od_b_a_2': 58.953,
     'od_b_x_2': 25.003,
     'norm2_g': 2.932}
    for name, (base, spread) in spreads.items():
        noise = np.random.default_rng([zlib.crc32(name.encode()), seed]).standard_normal(out[name].shape)
        drawn = base * np.exp(spread * noise) if base else spread * noise
        out[name] = __import__('jax').numpy.asarray(drawn.astype(out[name].dtype))
    for name, factor in factors.items():
        out[name] = (out[name] * factor).astype(out[name].dtype)
    return out
```

```python
from contextlib import ExitStack, contextmanager

import numpy as np

import concourse.bass as bass
from concourse import mybir

F32 = mybir.dt.float32
ALU = mybir.AluOpType
ACT = mybir.ActivationFunctionType
AX = mybir.AxisListType

P = 128
D = 1024
KT = D // P
NX, NC = 512, 256
T = NX + NC
TC, TX = NC // P, NX // P
TT = TC + TX
EPS = 1e-6
SLOT = 4096

GH, GK = 8, 128
SH, SP_, SG, SN = 32, 64, 8, 128
SR = SH // SG
SI = SH * SP_
NE, FF = 16, 1024
CAPX, CAPC = 2 * NX // NE, 2 * NC // NE
CAP = CAPX + CAPC
FH, FD = 8, 64
WINDOWS = (2, 4, 8, 16)
DFF = 2816
LH, LD = 4, 256
LRU_C = 8.0

FWD, BWD = 0, 1
ORDER = (tuple(range(TT)), tuple(reversed(range(TC))) + tuple(reversed(range(TC, TT))))


class Marks:

    def __init__(self, sem, *names):
        self.sem, self.names = sem, names

    def skip_step(self, engine):
        engine.sem_inc(self.sem, len(self.names))

    def at(self, step, name):
        return step * len(self.names) + self.names.index(name) + 1


class Ring:

    def __init__(self, nc, ctx, slots):
        self.slots = slots
        self.buf = ctx.enter_context(nc.sbuf_tensor("weight_ring", [P, slots, SLOT], F32))
        self.arrived = [nc.alloc_semaphore(name=f"weights_arrived_{s}") for s in range(slots)]
        self.used = nc.alloc_semaphore(name="weights_used")
        self.loads, self.index, self.issued = [], {}, 0

    def plan(self, name, source):
        self.index[name] = len(self.loads)
        self.loads.append(source)

    def view(self, name, **dims):
        n = self.index[name]
        shape = self.loads[n].shape
        size = int(np.prod(shape[1:]))
        flat = self.buf[:, n % self.slots, 0:size]
        return flat.rearrange("p (a b) -> p a b", b=shape[2]) if len(shape) == 3 else flat

    def wait(self, pe, name):
        n = self.index[name]
        pe.wait_ge(self.arrived[n % self.slots], 16 * (n // self.slots + 1))

    def done(self, engine, name):
        engine.wait_ge(self.used, self.index[name] + 1)

    def feed(self, sp, last):
        done = 0 if last is None else self.index[last] + 1
        until = min(done + self.slots, len(self.loads))
        for n in range(self.issued, until):
            if n >= self.slots:
                sp.wait_ge(self.used, n - self.slots + 1)
            source = self.loads[n]
            size = int(np.prod(source.shape[1:]))
            target = self.buf[:, n % self.slots, 0:size]
            if len(source.shape) == 3:
                target = target.rearrange("p (a b) -> p a b", b=source.shape[2])
            sp.dma_start(target, source).then_inc(self.arrived[n % self.slots], 16)
        self.issued = max(self.issued, until)


class Core:

    def __init__(self, nc, ctx, dram):
        self.nc, self.ctx, self.dram = nc, ctx, dram
        self.bank = [ctx.enter_context(nc.psum_tensor(f"bank{i}", [P, 512], F32)) for i in range(8)]
        self.dumps, self.stages, self.buffers = None, 0, 0

    def sb(self, ctx, name, *shape):
        self.buffers += 1
        return ctx.enter_context(self.nc.sbuf_tensor(f"{name}_b{self.buffers}", [P, *shape], F32))

    @contextmanager
    def stage(self, *names):
        self.stages += 1
        sems = [self.nc.alloc_semaphore(name=f"{n}_s{self.stages}") for n in names]
        with self.nc.Block() as block:
            yield (block, *sems)
        self.nc.clear_and_free_semaphores(sems)
        self.nc.all_engine_barrier()

    def dump(self, name, ap):
        if self.dumps is None:
            return
        with self.stage("dumped") as (block, dumped):
            out = self.nc.dram_tensor("dump_" + name, list(ap.shape), F32, kind="ExternalOutput").ap()
            out, ap = out, ap
            self.dumps.append("dump_" + name)

            @block.gpsimd
            def _(pool):
                pool.dma_start(out, ap).then_inc(dumped, 16)
                pool.wait_ge(dumped, 16)



VECTORS = [("c", 1), ("c_ctx", 1), ("norm1_g", 2), ("norm2_g", 2), ("ada_b", 2), ("gdn_conv_w", 3),
           ("gdn_norm_g", 1), ("ssd_conv_w", 3), ("ssd_conv_b", 1), ("ssd_norm_g", 1),
           ("mix_pre_g_2", 2), ("ffn_pre_g_2", 2), ("ev_pool_scale_2", 1), ("od_conv_w_2", 4),
           ("od_conv_b_2", 1), ("od_b_a_2", 1), ("od_b_x_2", 1), ("od_lam_2", 1)]
HEADED = ["gdn_a_log", "gdn_dt_bias", "ssd_a_log", "ssd_dt_bias", "ssd_d", "ev_b_f_2"]
LEVELS = [1, 2, 4, 8, 16, 32, 64]


def flat_rows(ap):
    names = " ".join("abcdef"[:len(ap.shape)])
    flat = ap.rearrange(f"{names} -> ({names})") if len(ap.shape) > 1 else ap
    return flat.rearrange("(r p) -> r p", p=P)


def constants(core):
    nc, ctx, dram = core.nc, core.ctx, core.dram
    core.ident = core.sb(ctx, "ident", P)
    core.ones = core.sb(ctx, "ones", P)
    core.tri = core.sb(ctx, "tri", 2, P)
    core.strict = core.sb(ctx, "strict", 2, P)
    core.level = core.sb(ctx, "level", len(LEVELS), P)
    core.iota = core.sb(ctx, "iota", 2 * CAPX)
    core.zero = core.sb(ctx, "zero", 1)
    core.eps = core.sb(ctx, "eps", 1)
    pieces, at = {}, 0
    for name, _ in VECTORS:
        n = int(np.prod(dram[name].shape)) // P
        pieces[name] = (at, n)
        at += n
    groups = -(-at // P)
    core.cols = core.sb(ctx, "cols", groups * P)
    core.col0 = {name: first for name, (first, _) in pieces.items()}
    width = {n: int(np.prod(dram[n].shape)) for n in HEADED}
    heads = core.sb(ctx, "heads", sum(width.values()))
    core.head, first = {}, 0
    for n in HEADED:
        core.head[n] = heads[:, first:first + width[n]]
        first += width[n]
    core.c2 = core.sb(ctx, "c2", KT, 2)
    copies = []
    for name, (first, n) in pieces.items():
        source, done = flat_rows(dram[name]), 0
        while done < n:
            g, r = (first + done) // P, (first + done) % P
            k = min(n - done, P - r)
            copies.append((g, r, source[done:done + k, :]))
            done += k
    with ExitStack() as own:
        rows = core.sb(own, "vector_rows", groups, P)
        with core.stage("rows_loaded", "rows_blank", "made", "turned", "copied") as (
                block, rows_loaded, rows_blank, made, turned, copied):
            @block.sync
            def _(sp):
                sp.wait_ge(rows_blank, 1)
                for g, r, source in copies:
                    sp.dma_start(rows[r:r + source.shape[0], g, :], source).then_inc(rows_loaded, 16)
                for n in HEADED:
                    letters = " ".join("abcd"[:len(dram[n].shape)])
                    source = dram[n].rearrange(f"{letters} -> ({letters})")
                    sp.dma_start(core.head[n], source.partition_broadcast(P)).then_inc(rows_loaded, 16)
                core.ring.feed(sp, None)

            @block.gpsimd
            def _(pool):
                pool.memset(core.ident[:], 0.0)
                pool.memset(core.strict[:], 0.0)
                pool.memset(core.zero[:], 0.0)
                pool.memset(core.eps[:], EPS)
                pool.memset(core.level[:], 1.0)
                pool.memset(core.ones[:], 1.0)
                pool.memset(core.tri[:], 1.0)
                pool.iota(core.iota[:], [[1, 2 * CAPX]], base=0, channel_multiplier=0,
                          allow_small_or_imprecise_dtypes=True).then_inc(made, 1)
                pool.wait_ge(made, 1)
                pool.affine_select(out=core.ident[:], in_=core.ident[:], pattern=[[-1, P]],
                                   compare_op=ALU.not_equal, fill=1.0, base=0, channel_multiplier=1)
                for d, sign in ((FWD, 1), (BWD, -1)):
                    for t, fill in ((core.tri, 0.0), (core.strict, 1.0)):
                        pool.affine_select(out=t[:, d, :], in_=t[:, d, :], pattern=[[sign, P]],
                                           compare_op=ALU.is_ge, fill=fill, base=0, channel_multiplier=-sign)
                for n, s in enumerate(LEVELS):
                    view = core.level[:, n, :].rearrange("p (b s) -> p b s", s=2 * s)
                    last = pool.affine_select(out=view, in_=view, pattern=[[-2 * s, P // (2 * s)], [0, 2 * s]],
                                              compare_op=ALU.is_ge, fill=0.0, base=0, channel_multiplier=1)
                last.then_inc(made, 1)
                pool.wait_ge(made, 2)
                for n, s in enumerate(LEVELS):
                    view = core.level[:, n, :].rearrange("p (b s) -> p b s", s=2 * s)
                    last = pool.affine_select(out=view, in_=view, pattern=[[2 * s, P // (2 * s)], [0, 2 * s]],
                                              compare_op=ALU.is_ge, fill=0.0, base=2 * s - 1,
                                              channel_multiplier=-1)
                last.then_inc(made, 1)

            @block.vector
            def _(dve):
                dve.memset(rows[:], 0.0).then_inc(rows_blank, 1)
                dve.wait_ge(made, 3)
                for n in reversed(range(1, len(LEVELS))):
                    dve.tensor_tensor(core.level[:, n, :], core.level[:, n, :], core.level[:, n - 1, :],
                                      ALU.subtract)
                dve.tensor_tensor(core.level[:, 0, :], core.level[:, 0, :], core.ident[:], ALU.subtract)
                dve.wait_ge(turned, 1)
                dve.tensor_copy(core.cols[:], core.bank[0][:, 0:groups * P]).then_inc(copied, 1)

            @block.tensor
            def _(pe):
                pe.wait_ge(made, 3)
                pe.wait_ge(rows_loaded, 16 * (len(copies) + len(HEADED)))
                for g in range(groups):
                    last = pe.transpose(core.bank[0][:, g * P:(g + 1) * P], rows[:, g, :], core.ident[:])
                last.then_inc(turned, 1)

            @block.scalar
            def _(act):
                act.wait_ge(copied, 1)
                for i, name in enumerate(("c", "c_ctx")):
                    first = core.col0[name]
                    act.activation(core.c2[:, :, i], core.cols[:, first:first + KT], ACT.Silu)
    core.dump("cols", core.cols[:])
    core.dump("level", core.level[:])


def columns(core, name, index=0, count=KT):
    first = core.col0[name] + index * count
    return core.cols[:, first:first + count]




def ada(core, layer):
    nc = core.nc
    mod = core.mod
    tiles = 6 * D // 512
    with core.stage("m") as (block, m):
        acc = core.bank[0]

        @block.sync
        def _(sp):
            core.ring.feed(sp, f"ada{layer}_{tiles - 1}")

        @block.tensor
        def _(pe):
            for j in range(tiles):
                name = f"ada{layer}_{j}"
                core.ring.wait(pe, name)
                w = core.ring.view(name)
                for c in range(4):
                    col = 2 * (4 * j + c)
                    for k in range(KT):
                        last = pe.matmul(acc[:, col:col + 2], w[:, k, c * P:(c + 1) * P], core.c2[:, k, :],
                                         start=(k == 0), stop=(k == KT - 1))
                last.then_inc(core.ring.used, 1)

        @block.vector
        def _(dve):
            core.ring.done(dve, f"ada{layer}_{tiles - 1}")
            bias = core.cols[:, core.col0["ada_b"] + 48 * layer:core.col0["ada_b"] + 48 * layer + 48]
            dve.tensor_tensor(mod[:], acc[:, 0:96].rearrange("p (c i) -> p c i", i=2),
                              bias.unsqueeze(2).to_broadcast([P, 48, 2]), ALU.add).then_inc(m, 1)
            dve.wait_ge(m, 1)
            for n, (norm, chunk) in enumerate((("norm1_g", 1), ("norm2_g", 4))):
                g = columns(core, norm, layer).unsqueeze(2).to_broadcast([P, KT, 2])
                dve.scalar_tensor_tensor(out=core.factor[:, n, :, :], in0=mod[:, chunk * KT:(chunk + 1) * KT, :],
                                         scalar=1.0, in1=g, op0=ALU.add, op1=ALU.mult)
    core.dump(f"mod{layer}", mod[:])


def gate_rows(core, gate, chunk):
    with core.stage("spread") as (block, spread):
        @block.tensor
        def _(pe):
            for i in range(2):
                for h in range(2):
                    for k in range(4):
                        m = core.mod[:, chunk * KT + 4 * h + k, i:i + 1]
                        last = pe.matmul(core.bank[2 * i + h][:, k * P:(k + 1) * P], m.to_broadcast([P, P]),
                                         core.ident[:], start=True, stop=True)
                    last.then_inc(spread, 1)

        @block.vector
        def _(dve):
            for i in range(2):
                for h in range(2):
                    dve.wait_ge(spread, 2 * i + h + 1)
                    dve.tensor_copy(gate[:, i, h * 512:(h + 1) * 512], core.bank[2 * i + h][:])




def norm_turn(core, X, hT, tiles, factor, shift, xn, last_load):
    nt = len(tiles)
    with ExitStack() as own, core.stage("squared", "rooted", "scaled", "turned", "moved") as (
            block, squared, rooted, scaled, turned, moved):
        ss = core.sb(own, "sum_squares", nt)
        rms = core.sb(own, "rms", nt)
        inv = core.sb(own, "inverse_rms", nt)
        runs = [r for r in (tiles[0:TC], tiles[TC:]) if r] if nt == TT else [tiles]

        @block.sync
        def _(sp):
            core.ring.feed(sp, last_load)

        @block.scalar
        def _(act):
            for i, t in enumerate(tiles):
                last = act.activation(xn[:, i, :], X[:, i, :], ACT.Square, accum_out=ss[:, i:i + 1])
            last.then_inc(squared, 1)
            act.wait_ge(scaled, 1)
            act.activation(rms[:], ss[:], ACT.Sqrt).then_inc(rooted, 1)

        @block.vector
        def _(dve):
            dve.wait_ge(squared, 1)
            dve.tensor_scalar(ss[:], ss[:], 1.0 / D, EPS, ALU.mult, ALU.add).then_inc(scaled, 1)
            dve.wait_ge(rooted, 1)
            dve.reciprocal(inv[:], rms[:]).then_inc(scaled, 1)
            dve.wait_ge(scaled, 2)
            for i in range(nt):
                dve.tensor_scalar(xn[:, i, :], X[:, i, :], inv[:, i:i + 1], None, ALU.mult).then_inc(scaled, 1)
            n = 0
            for k in range(KT):
                at = 0
                for run in runs:
                    w = len(run) * P
                    dve.wait_ge(turned, n + 1)
                    b = shift(k, run[0]) if shift else core.zero[:, 0:1]
                    dve.tensor_scalar(hT[:, k, at:at + w], core.bank[n % 8][:, 0:w], factor(k, run[0]), b,
                                      ALU.mult, ALU.add).then_inc(moved, 1)
                    at += w
                    n += 1

        @block.tensor
        def _(pe):
            n = 0
            pe.wait_ge(scaled, 2 + nt)
            for k in range(KT):
                i = 0
                for run in runs:
                    if n >= 8:
                        pe.wait_ge(moved, n - 7)
                    for j in range(len(run)):
                        last = pe.transpose(core.bank[n % 8][:, j * P:(j + 1) * P],
                                            xn[:, i, k * P:(k + 1) * P], core.ident[:])
                        i += 1
                    last.then_inc(turned, 1)
                    n += 1


def load_x(core, X, source):
    with core.stage("loaded") as (block, loaded):
        @block.sync
        def _(sp):
            if source is None:
                parts = ((0, TC, core.dram["ctx"]), (TC, TT, core.dram["x"]))
                for a, b, ap in parts:
                    sp.dma_start(X[:, a:b, :], ap.rearrange("o (t p) n -> p (o t) n", p=P)).then_inc(loaded, 16)
                sp.wait_ge(loaded, 32)
            else:
                sp.dma_start(X, source).then_inc(loaded, 16)
                sp.wait_ge(loaded, 16)



CV = T + 2
SEQ0 = NC + 2


def chunk_cols(t):
    return t * P + (0 if t < TC else 2)


def conv_project(core, hT, jobs, taps, bias, last_load):
    nc = core.nc
    with ExitStack() as own, core.stage("projected", "padded", "convolved", "activated", "squared",
                                        "posted", "rooted", "link", "stored") as (
            block, projected, padded, convolved, activated, squared, posted, rooted, link, stored):
        raw = core.sb(own, "conv_in", 2, CV + 2)
        cv = core.sb(own, "conv_out", 2, CV)
        sl = core.sb(own, "conv_silu", 2, CV)
        sq = core.sb(own, "conv_square", CV)
        rt = core.sb(own, "conv_root", CV)
        half = T // 2
        N = len(jobs)
        turn_runs = ((0, 4), (4, TT))

        @block.sync
        def _(sp):
            core.ring.feed(sp, last_load)

        @block.gpsimd
        def _(pool):
            pool.memset(raw[:, :, 0:1], 0.0)
            pool.memset(raw[:, :, NC + 1:NC + 3], 0.0)
            pool.memset(raw[:, :, CV + 1:CV + 2], 0.0).then_inc(stored, 1)

        @block.tensor
        def _(pe):
            def post(n):
                _, _, _, kind, _ = jobs[n]
                if kind == "unit":
                    pe.wait_ge(squared, n + 1)
                    if n >= 2:
                        pe.wait_ge(link, 2 * (n - 1))
                    for h in range(2):
                        last = pe.matmul(core.bank[4 + 2 * (n % 2) + h][:, 0:CV // 2], core.ones[:],
                                         sq[:, h * (CV // 2):(h + 1) * (CV // 2)], start=True, stop=True)
                    last.then_inc(posted, 1)
                elif kind == "turn":
                    pe.wait_ge(activated, n + 1)
                    if n >= 2:
                        pe.wait_ge(link, 2 * (n - 1))
                    for h, (a, b) in enumerate(turn_runs):
                        for t in range(a, b):
                            last = pe.transpose(core.bank[4 + 2 * (n % 2) + h][:, (t - a) * P:(t - a + 1) * P],
                                                sl[:, n % 2, chunk_cols(t):chunk_cols(t) + P], core.ident[:])
                    last.then_inc(posted, 1)

            names = [j[0] for j in jobs]
            for n, (name, c, _, _, _) in enumerate(jobs):
                if n == 0 or names[n - 1] != name:
                    core.ring.wait(pe, name)
                w = core.ring.view(name)
                if n >= 2:
                    pe.wait_ge(padded, n - 1)
                for h in range(2):
                    acc = core.bank[2 * (n % 2) + h][:, 0:half]
                    for k in range(KT):
                        last = pe.matmul(acc, w[:, k, c * P:(c + 1) * P], hT[:, k, h * half:(h + 1) * half],
                                         start=(k == 0), stop=(k == KT - 1))
                last.then_inc(projected, 1)
                if n == N - 1 or names[n + 1] != name:
                    pe.wait_ge(projected, n + 1)
                    pe.sem_inc(core.ring.used, 1)
                if n >= 1:
                    post(n - 1)
            post(N - 1)

        @block.scalar
        def _(act):
            act.wait_ge(stored, 1)
            for n, (_, _, ch, kind, target) in enumerate(jobs):
                act.wait_ge(projected, n + 1)
                if n >= 2:
                    act.wait_ge(convolved, 3 * (n - 1))
                a, b = core.bank[2 * (n % 2)], core.bank[2 * (n % 2) + 1]
                r = raw[:, n % 2, :]
                act.activation(r[:, 1:1 + NC], a[:, 0:NC], ACT.Copy)
                act.activation(r[:, SEQ0 + 1:SEQ0 + 1 + half - NC], a[:, NC:half], ACT.Copy)
                act.activation(r[:, SEQ0 + 1 + half - NC:CV + 1], b[:, 0:half], ACT.Copy).then_inc(padded, 1)
                act.wait_ge(convolved, 3 * (n + 1))
                if n >= 2 and kind != "plain":
                    act.wait_ge(link, 2 * (n - 1))
                out = target if kind == "plain" else sl[:, n % 2, :]
                act.activation(out, cv[:, n % 2, :], ACT.Silu,
                               bias=bias(ch) if bias else 0.0).then_inc(activated, 1)
                if kind == "unit":
                    act.wait_ge(posted, n + 1)
                    if n >= 1:
                        act.wait_ge(link, 2 * n)
                    for h in range(2):
                        w = CV // 2
                        last = act.activation(rt[:, h * w:(h + 1) * w], core.bank[4 + 2 * (n % 2) + h][:, 0:w],
                                              ACT.Sqrt, bias=core.eps[:, 0:1])
                    last.then_inc(rooted, 1)

        @block.vector
        def _(dve):
            for n, (_, _, ch, kind, target) in enumerate(jobs):
                r, y = raw[:, n % 2, :], cv[:, n % 2, :]
                dve.wait_ge(padded, n + 1)
                if n >= 2:
                    dve.wait_ge(activated, n - 1)
                dve.tensor_scalar(y, r[:, 1:CV + 1], taps(1, ch), None, ALU.mult).then_inc(convolved, 1)
                dve.wait_ge(convolved, 3 * n + 1)
                dve.scalar_tensor_tensor(out=y, in0=r[:, 0:CV], scalar=taps(0, ch), in1=y, op0=ALU.mult,
                                         op1=ALU.add).then_inc(convolved, 1)
                dve.wait_ge(convolved, 3 * n + 2)
                dve.scalar_tensor_tensor(out=y, in0=r[:, 2:CV + 2], scalar=taps(2, ch), in1=y, op0=ALU.mult,
                                         op1=ALU.add).then_inc(convolved, 1)
                if kind == "unit":
                    goal, scale = target
                    x = sl[:, n % 2, :]
                    dve.wait_ge(activated, n + 1)
                    if n >= 1:
                        dve.wait_ge(posted, n)
                    dve.tensor_tensor(sq[:], x, x, ALU.mult).then_inc(squared, 1)
                    dve.wait_ge(rooted, n + 1)
                    dve.reciprocal(rt[:], rt[:]).then_inc(link, 1)
                    dve.wait_ge(link, 2 * n + 1)
                    dve.scalar_tensor_tensor(out=goal, in0=x, scalar=scale, in1=rt[:], op0=ALU.mult,
                                             op1=ALU.mult).then_inc(link, 1)
                elif kind == "turn":
                    dve.wait_ge(posted, n + 1)
                    for h, (a, b) in enumerate(turn_runs):
                        view = core.bank[4 + 2 * (n % 2) + h][:, 0:(b - a) * P]
                        dve.tensor_copy(target[:, a:b, :], view.rearrange("p (t c) -> p t c", c=P)).then_inc(link, 1)




class Decays:

    def __init__(self, core, ctx, tag, heads):
        self.heads = heads
        self.step = core.sb(ctx, f"{tag}_step", TT, 2, heads)
        self.g = core.sb(ctx, f"{tag}_g", TT, 2, heads)
        self.cum = core.sb(ctx, f"{tag}_cum", TT, 2, heads)
        self.from_start = core.sb(ctx, f"{tag}_from_start", TT, 2, heads)
        self.to_end = core.sb(ctx, f"{tag}_to_end", TT, 2, heads)
        self.whole = core.sb(ctx, f"{tag}_whole", TT, 2, heads)


def decays(core, hT, load, H, bias, a_log, dec, with_beta, last_load):
    n = 2 * H
    first = n if with_beta else 0
    width = first + n
    with ExitStack() as own, core.stage("projected", "dve_done", "act_done", "summed") as (
            block, projected, dve_done, act_done, summed):
        x = core.sb(own, "gate_x", TT, n)
        ax = core.sb(own, "gate_abs", TT, n)
        ex = core.sb(own, "gate_exp", TT, n)
        a = core.sb(own, "gate_a", n)
        acc = core.bank[0][:, 0:TT * width].rearrange("p (t n) -> p t n", n=width)
        step, g, cum = (v[:].rearrange("p t d h -> p t (d h)") for v in (dec.step, dec.g, dec.cum))
        sums = core.bank[1][:, 0:TT * n].rearrange("p (t d h) -> p t d h", d=2, h=H)
        wholes = core.bank[2][:, 0:TT * n].rearrange("p (t n) -> p t n", n=n)
        to_end, whole = (v[:].rearrange("p t d h -> p t (d h)") for v in (dec.to_end, dec.whole))

        @block.sync
        def _(sp):
            core.ring.feed(sp, last_load)

        @block.tensor
        def _(pe):
            core.ring.wait(pe, load)
            w = core.ring.view(load)
            for t in range(TT):
                for k in range(KT):
                    last = pe.matmul(acc[:, t, :], hT[:, k, t * P:(t + 1) * P], w[:, k, :],
                                     start=(k == 0), stop=(k == KT - 1))
            last.then_inc(core.ring.used, 1)
            pe.wait_ge(dve_done, 5)
            for t in range(TT):
                for d in (FWD, BWD):
                    pe.matmul(sums[:, t, d, :], core.tri[:, d, :], dec.g[:, t, d, :], start=True, stop=True)
                last = pe.matmul(wholes[:, t, :], core.ones[:], g[:, t, :], start=True, stop=True)
            last.then_inc(summed, 1)

        @block.vector
        def _(dve):
            core.ring.done(dve, load)
            dve.tensor_tensor(x[:], acc[:, :, first:width], bias.unsqueeze(1).to_broadcast([P, TT, n]),
                              ALU.add).then_inc(dve_done, 1)
            dve.wait_ge(dve_done, 1)
            dve.scalar_tensor_tensor(out=ax[:], in0=x[:], scalar=-1.0, in1=x[:], op0=ALU.mult,
                                     op1=ALU.max).then_inc(dve_done, 1)
            dve.tensor_scalar(x[:], x[:], 0.0, None, ALU.max).then_inc(dve_done, 1)
            dve.wait_ge(act_done, 3)
            dve.wait_ge(dve_done, 3)
            dve.tensor_tensor(step, x[:], ex[:], ALU.add).then_inc(dve_done, 1)
            dve.wait_ge(dve_done, 4)
            dve.scalar_tensor_tensor(out=g, in0=step, scalar=-1.0, in1=a[:].unsqueeze(1).to_broadcast([P, TT, n]),
                                     op0=ALU.mult, op1=ALU.mult).then_inc(dve_done, 1)
            dve.wait_ge(summed, 1)
            dve.tensor_copy(dec.cum[:], sums).then_inc(dve_done, 1)
            dve.wait_ge(dve_done, 6)
            dve.tensor_tensor(ex[:], wholes, cum, ALU.subtract).then_inc(dve_done, 1)

        @block.scalar
        def _(act):
            act.activation(a[:], a_log, ACT.Exp).then_inc(act_done, 1)
            act.wait_ge(dve_done, 2)
            act.activation(ex[:], ax[:], ACT.Exp, scale=-1.0).then_inc(act_done, 1)
            act.wait_ge(act_done, 2)
            act.activation(ex[:], ex[:], ACT.Ln, bias=core.ones[:, 0:1]).then_inc(act_done, 1)
            act.wait_ge(dve_done, 7)
            act.activation(dec.from_start[:], dec.cum[:], ACT.Exp)
            act.activation(to_end, ex[:], ACT.Exp)
            act.activation(whole, wholes, ACT.Exp)
            if with_beta:
                beta = dec.beta[:].rearrange("p t d h -> p t (d h)")
                act.activation(beta, acc[:, :, 0:n], ACT.Sigmoid)



GQ = 4


def delta_scan(core, qT, kT, V, O, dec, h0, last_load):
    nc = core.nc
    PEM = ["rows", "gram", "qk", "turn1"]
    for s in LEVELS[1:]:
        PEM += [f"ct{s}", f"u{s}"] + ([f"v{s}"] if s != LEVELS[-1] else [])
    PEM += ["kturn", "ks", "new", "o", "state"]
    DVM = ["ge", "low", "attn", "u1", "v1"]
    for s in LEVELS[1:]:
        DVM += [f"u{s}"] + ([f"v{s}"] if s != LEVELS[-1] else [])
    DVM += ["ub", "qs", "kend", "eks", "rest", "out", "fade", "state"]
    ACM = ["gap", "decay", "rowexp"] + [f"ct{s}" for s in LEVELS[1:]] + ["new"]
    POM = ["attn", "a1"] + [f"a{s}" for s in LEVELS[1:]]
    with ExitStack() as own, core.stage("pe_f", "pe_b", "dve_f", "dve_b", "act_f", "act_b", "pool_f", "pool_b",
                                        "cleared") as (
            block, pe_f, pe_b, dve_f, dve_b, act_f, act_b, pool_f, pool_b, cleared):
        pem = [Marks(x, *PEM) for x in (pe_f, pe_b)]
        dvm = [Marks(x, *DVM) for x in (dve_f, dve_b)]
        acm = [Marks(x, *ACM) for x in (act_f, act_b)]
        pom = [Marks(x, *POM) for x in (pool_f, pool_b)]
        E = core.sb(own, "d_decay", 2, GQ, P)
        L = core.sb(own, "d_low", 2, GQ, P)
        A = core.sb(own, "d_level", 2, 2, GQ, P)
        U = core.sb(own, "d_u", 2, GQ, P)
        W = core.sb(own, "d_v", 2, GQ, P)
        C = core.sb(own, "d_ct", 2, GQ, P)
        G = core.sb(own, "d_gap", 2, GQ, P)
        QS = core.sb(own, "d_qs", 2, GQ, P)
        KE = core.sb(own, "d_kend", 2, GQ, P)
        AT = core.sb(own, "d_attn", 2, GQ, P)
        R, NW = E, C
        S = core.sb(own, "d_state", 2, GQ, P)
        B = [[core.bank[4 * d + i][:].rearrange("p (h c) -> p h c", c=P) for i in range(4)] for d in (FWD, BWD)]
        flat = "p h c -> p (h c)"

        def wide(x, d, t):
            return x[:, t, d, h0:h0 + GQ].unsqueeze(2).to_broadcast([P, GQ, P])

        def over_heads(m):
            return m.unsqueeze(1).to_broadcast([P, GQ, P])

        def steps():
            for s in range(TT):
                yield s

        def wait(engine, marks, s, name):
            engine.wait_ge(marks.sem, marks.at(s, name))

        @block.sync
        def _(sp):
            core.ring.feed(sp, last_load)

        @block.gpsimd
        def _(pool):
            for s in steps():
                for d in (FWD, BWD):
                    wait(pool, dvm[d], s, "attn")
                    if s:
                        wait(pool, pem[d], s - 1, "o")
                    pool.tensor_tensor(AT[:, d], G[:, d], over_heads(core.tri[:, d, :]), ALU.mult) \
                        .then_inc(pom[d].sem, 1)
                for n, size in enumerate(LEVELS):
                    for d in (FWD, BWD):
                        if n > 2:
                            wait(pool, pem[d], s, f"ct{LEVELS[n - 2]}")
                        elif n == 2:
                            wait(pool, pem[d], s, "turn1")
                            wait(pool, dvm[d], s, "v1")
                        elif s:
                            wait(pool, pem[d], s - 1, f"ct{LEVELS[-1 - n]}")
                        wait(pool, dvm[d], s, "low")
                        pool.tensor_tensor(A[:, d, n % 2], L[:, d], over_heads(core.level[:, n, :]), ALU.mult) \
                            .then_inc(pom[d].sem, 1)

        @block.tensor
        def _(pe):
            def each(d, s, name, out, lhsT, rhs):
                for h in range(GQ):
                    last = pe.matmul(out[:, h, :], lhsT(h), rhs(h), start=True, stop=True)
                last.then_inc(pem[d].sem, 1)

            for s in steps():
                for d in (FWD, BWD):
                    t = ORDER[d][s]
                    if s:
                        wait(pe, acm[d], s - 1, "rowexp")
                    each(d, s, "rows", B[d][0], lambda h: dec.g[:, t, d, h0 + h:h0 + h + 1].to_broadcast([P, P]),
                         lambda h: core.tri[:, d, :])
                for d in (FWD, BWD):
                    t = ORDER[d][s]
                    cols = slice(chunk_cols(t), chunk_cols(t) + P)
                    if s:
                        wait(pe, dvm[d], s - 1, "out")
                    each(d, s, "gram", B[d][1], lambda h: kT[:, h, cols], lambda h: kT[:, h, cols])
                    each(d, s, "qk", B[d][2], lambda h: kT[:, h, cols], lambda h: qT[:, h, cols])
                for d in (FWD, BWD):
                    wait(pe, pom[d], s, "a1")
                    wait(pe, dvm[d], s, "ge")
                    for h in range(GQ):
                        last = pe.transpose(B[d][1][:, h, :], A[:, d, 0, h, :], core.ident[:])
                    last.then_inc(pem[d].sem, 1)
                for n, size in enumerate(LEVELS):
                    if n == 0:
                        continue
                    below = LEVELS[n - 1]
                    for d in (FWD, BWD):
                        wait(pe, pom[d], s, f"a{size}")
                        wait(pe, dvm[d], s, f"v{below}")
                        if n == 1:
                            wait(pe, dvm[d], s, "attn")
                        each(d, s, "ct", B[d][2], lambda h: A[:, d, n % 2, h, :], lambda h: U[:, d, h, :])
                    for d in (FWD, BWD):
                        wait(pe, acm[d], s, f"ct{size}")
                        each(d, s, "u", B[d][1], lambda h: W[:, d, h, :], lambda h: C[:, d, h, :])
                        if size != LEVELS[-1]:
                            each(d, s, "v", B[d][2], lambda h: C[:, d, h, :], lambda h: W[:, d, h, :])
                for d in (FWD, BWD):
                    t = ORDER[d][s]
                    cols = slice(chunk_cols(t), chunk_cols(t) + P)
                    for h in range(GQ):
                        last = pe.transpose(B[d][2][:, h, :], kT[:, h, cols], core.ident[:])
                    last.then_inc(pem[d].sem, 1)
                for d in (FWD, BWD):
                    t = ORDER[d][s]
                    cols = slice(chunk_cols(t), chunk_cols(t) + P)
                    if s:
                        wait(pe, dvm[d], s - 1, "state")
                    else:
                        pe.wait_ge(cleared, 1)
                    each(d, s, "ks", B[d][3], lambda h: kT[:, h, cols], lambda h: S[:, d, h, :])
                for d in (FWD, BWD):
                    wait(pe, dvm[d], s, "rest")
                    each(d, s, "new", B[d][1], lambda h: U[:, d, h, :], lambda h: R[:, d, h, :])
                for d in (FWD, BWD):
                    wait(pe, acm[d], s, "new")
                    wait(pe, pom[d], s, "attn")
                    for h in range(GQ):
                        pe.matmul(B[d][2][:, h, :], QS[:, d, h, :], S[:, d, h, :], start=True, stop=False)
                        last = pe.matmul(B[d][2][:, h, :], AT[:, d, h, :], NW[:, d, h, :], start=False, stop=True)
                    last.then_inc(pem[d].sem, 1)
                    each(d, s, "state", B[d][3], lambda h: KE[:, d, h, :], lambda h: NW[:, d, h, :])

        @block.scalar
        def _(act):
            for s in steps():
                for d in (FWD, BWD):
                    t = ORDER[d][s]
                    wait(act, pem[d], s, "rows")
                    if s:
                        wait(act, pom[d], s - 1, "attn")
                        wait(act, pem[d], s - 1, "new")
                    for h in range(GQ):
                        last = act.activation(G[:, d, h, :], B[d][0][:, h, :], ACT.Abs, scale=-1.0,
                                              bias=dec.cum[:, t, d, h0 + h:h0 + h + 1])
                    last.then_inc(acm[d].sem, 1)
                    wait(act, acm[d], s, "gap")
                    act.activation(E[:, d], G[:, d], ACT.Exp, scale=-1.0).then_inc(acm[d].sem, 1)
                    if s:
                        wait(act, pem[d], s - 1, "o")
                    act.activation(QS[:, d], B[d][0], ACT.Exp).then_inc(acm[d].sem, 1)
                for size in LEVELS[1:]:
                    for d in (FWD, BWD):
                        wait(act, pem[d], s, f"ct{size}")
                        act.activation(C[:, d], B[d][2], ACT.Copy).then_inc(acm[d].sem, 1)
                for d in (FWD, BWD):
                    wait(act, pem[d], s, "new")
                    if s:
                        wait(act, pem[d], s - 1, "state")
                    act.activation(NW[:, d], B[d][1], ACT.Copy).then_inc(acm[d].sem, 1)

        @block.vector
        def _(dve):
            dve.memset(S[:], 0.0).then_inc(cleared, 1)
            for s in steps():
                for d in (FWD, BWD):
                    t = ORDER[d][s]
                    wait(dve, acm[d], s, "decay")
                    wait(dve, pem[d], s, "gram")
                    if s:
                        wait(dve, pom[d], s - 1, f"a{LEVELS[-1]}")
                    dve.tensor_tensor(L[:, d], B[d][1], E[:, d], ALU.mult).then_inc(dvm[d].sem, 1)
                    wait(dve, dvm[d], s, "ge")
                    for h in range(GQ):
                        last = dve.scalar_tensor_tensor(out=L[:, d, h, :], in0=L[:, d, h, :],
                                                        scalar=dec.beta[:, t, d, h0 + h:h0 + h + 1],
                                                        in1=core.strict[:, d, :], op0=ALU.mult, op1=ALU.mult)
                    last.then_inc(dvm[d].sem, 1)
                    wait(dve, pem[d], s, "qk")
                    dve.tensor_tensor(G[:, d], B[d][2], E[:, d], ALU.mult).then_inc(dvm[d].sem, 1)
                for d in (FWD, BWD):
                    wait(dve, pem[d], s, "turn1")
                    if s:
                        wait(dve, pem[d], s - 1, "new")
                    dve.scalar_tensor_tensor(out=U[:, d], in0=B[d][1], scalar=-1.0, in1=over_heads(core.ident[:]),
                                             op0=ALU.mult, op1=ALU.add).then_inc(dvm[d].sem, 1)
                    wait(dve, pom[d], s, "a1")
                    dve.scalar_tensor_tensor(out=W[:, d], in0=A[:, d, 0], scalar=-1.0,
                                             in1=over_heads(core.ident[:]), op0=ALU.mult,
                                             op1=ALU.add).then_inc(dvm[d].sem, 1)
                for size in LEVELS[1:]:
                    for d in (FWD, BWD):
                        wait(dve, pem[d], s, f"u{size}")
                        wait(dve, dvm[d], s, f"v{size // 2}")
                        dve.tensor_tensor(U[:, d], U[:, d], B[d][1], ALU.subtract).then_inc(dvm[d].sem, 1)
                        if size != LEVELS[-1]:
                            wait(dve, pem[d], s, f"v{size}")
                            dve.tensor_tensor(W[:, d], W[:, d], B[d][2], ALU.subtract).then_inc(dvm[d].sem, 1)
                for d in (FWD, BWD):
                    t = ORDER[d][s]
                    cols = slice(chunk_cols(t), chunk_cols(t) + P)
                    wait(dve, dvm[d], s, f"u{LEVELS[-1]}")
                    dve.tensor_tensor(U[:, d], U[:, d], wide(dec.beta, d, t), ALU.mult).then_inc(dvm[d].sem, 1)
                    wait(dve, acm[d], s, "rowexp")
                    dve.tensor_tensor(QS[:, d], QS[:, d], qT[:, :, cols], ALU.mult).then_inc(dvm[d].sem, 1)
                    wait(dve, pem[d], s, "kturn")
                    if s:
                        wait(dve, pem[d], s - 1, "state")
                    dve.tensor_tensor(KE[:, d], B[d][2], wide(dec.to_end, d, t), ALU.mult) \
                        .then_inc(dvm[d].sem, 1)
                for d in (FWD, BWD):
                    t = ORDER[d][s]
                    wait(dve, pem[d], s, "ks")
                    if s:
                        wait(dve, pem[d], s - 1, "new")
                    dve.tensor_tensor(R[:, d], B[d][3], wide(dec.from_start, d, t), ALU.mult) \
                        .then_inc(dvm[d].sem, 1)
                    wait(dve, dvm[d], s, "eks")
                    dve.tensor_tensor(R[:, d], V[:, t], R[:, d], ALU.subtract).then_inc(dvm[d].sem, 1)
                for d in (FWD, BWD):
                    t = ORDER[d][s]
                    wait(dve, pem[d], s, "o")
                    other = ORDER[1 - d].index(t)
                    if s < other or (s == other and d == FWD):
                        dve.tensor_copy(O[:, t], B[d][2]).then_inc(dvm[d].sem, 1)
                    else:
                        wait(dve, dvm[1 - d], other, "out")
                        dve.tensor_tensor(O[:, t], O[:, t], B[d][2], ALU.add).then_inc(dvm[d].sem, 1)
                    dve.tensor_tensor(S[:, d], S[:, d], wide(dec.whole, d, t), ALU.mult).then_inc(dvm[d].sem, 1)
                    wait(dve, pem[d], s, "state")
                    wait(dve, dvm[d], s, "fade")
                    dve.tensor_tensor(S[:, d], S[:, d], B[d][3], ALU.add).then_inc(dvm[d].sem, 1)




def gemm_tokens(core, lhs, groups, tiles, evac, last_load, on_scalar=False):
    nt = len(tiles)
    with core.stage("summed", "moved", "link") as (block, summed, moved, link):
        @block.sync
        def _(sp):
            core.ring.feed(sp, last_load)

        @block.tensor
        def _(pe):
            for j, group in enumerate(groups):
                for n, (load, ks) in enumerate(group):
                    core.ring.wait(pe, load)
                    w = core.ring.view(load)
                    width = w.shape[2]
                    for i, t in enumerate(tiles):
                        b = (j * nt + i)
                        if n == 0 and b >= 8:
                            pe.wait_ge(moved, b - 7)
                        for q, k in enumerate(ks):
                            last = pe.matmul(core.bank[b % 8][:, 0:width], lhs(k, t), w[:, q, :],
                                             start=(n == 0 and q == 0), stop=(n == len(group) - 1 and q == len(ks) - 1))
                        if n == len(group) - 1 and i < nt - 1:
                            last.then_inc(summed, 1)
                    last.then_inc(core.ring.used, 1)

        @(block.scalar if on_scalar else block.vector)
        def _(dve):
            links = [0]

            def linked(instruction):
                links[0] += 1
                instruction.then_inc(link, 1)
                dve.wait_ge(link, links[0])

            for j, group in enumerate(groups):
                for i, t in enumerate(tiles):
                    if i < nt - 1:
                        dve.wait_ge(summed, j * (nt - 1) + i + 1)
                    else:
                        core.ring.done(dve, group[-1][0])
                    if not on_scalar and j * nt + i:
                        dve.wait_ge(moved, j * nt + i)
                    evac(dve, linked, j, t, core.bank[(j * nt + i) % 8]).then_inc(moved, 1)


def add_gated(X, gate, tmp, width=512):
    def evac(dve, linked, j, t, bank):
        cols = slice(j * width, (j + 1) * width)
        g = gate[:, int(t < TC), cols]
        linked(dve.tensor_tensor(tmp[:, 0:width], bank[:, 0:width], g, ALU.mult))
        return dve.tensor_tensor(X(t)[:, cols], X(t)[:, cols], tmp[:, 0:width], ALU.add)
    return evac




def swiglu_up(core, hT, hid, loads, last_load):
    with ExitStack() as own, core.stage("gated", "upped", "activated", "stored", "used") as (
            block, gated, upped, activated, stored, used):
        sl = core.sb(own, "swiglu_silu", 2, NX)
        flat = [(g, u, f0 + c, c, c == n - 1) for g, u, f0, n in loads for c in range(n)]

        @block.sync
        def _(sp):
            core.ring.feed(sp, last_load)

        @block.tensor
        def _(pe):
            for n, (g, u, f, c, ends) in enumerate(flat):
                core.ring.wait(pe, g)
                core.ring.wait(pe, u)
                if n >= 4:
                    pe.wait_ge(stored, n - 3)
                for name, bank, sem in ((g, 2 * (n % 4), gated), (u, 2 * (n % 4) + 1, upped)):
                    w = core.ring.view(name)
                    for k in range(KT):
                        last = pe.matmul(core.bank[bank][:], w[:, k, c * P:(c + 1) * P], hT[:, k, :],
                                         start=(k == 0), stop=(k == KT - 1))
                    last.then_inc(sem, 1)
                if ends:
                    pe.wait_ge(upped, n + 1)
                    pe.sem_inc(core.ring.used, 2)

        @block.scalar
        def _(act):
            for n in range(len(flat)):
                act.wait_ge(gated, n + 1)
                if n >= 2:
                    act.wait_ge(stored, n - 1)
                act.activation(sl[:, n % 2, :], core.bank[2 * (n % 4)][:], ACT.Silu).then_inc(activated, 1)

        @block.vector
        def _(dve):
            for n, (_, _, f, _, _) in enumerate(flat):
                dve.wait_ge(activated, n + 1)
                dve.wait_ge(upped, n + 1)
                dve.tensor_tensor(hid[:, f, :], sl[:, n % 2, :], core.bank[2 * (n % 4) + 1][:],
                                  ALU.mult).then_inc(stored, 1)


def project_channels(core, hT, jobs, last_load):
    with core.stage("summed", "moved") as (block, summed, moved):
        names = [j[0] for j in jobs]

        @block.sync
        def _(sp):
            core.ring.feed(sp, last_load)

        @block.tensor
        def _(pe):
            for n, (name, c, _, _) in enumerate(jobs):
                core.ring.wait(pe, name)
                w = core.ring.view(name)
                if n >= 8:
                    pe.wait_ge(moved, n - 7)
                for k in range(KT):
                    last = pe.matmul(core.bank[n % 8][:], w[:, k, c * P:(c + 1) * P], hT[:, k, :],
                                     start=(k == 0), stop=(k == KT - 1))
                last.then_inc(summed, 1)
                if n == len(jobs) - 1 or names[n + 1] != name:
                    pe.wait_ge(summed, n + 1)
                    pe.sem_inc(core.ring.used, 1)

        @block.scalar
        def _(act):
            for n, (_, _, target, function) in enumerate(jobs):
                act.wait_ge(summed, n + 1)
                act.activation(target, core.bank[n % 8][:], function).then_inc(moved, 1)


def add_normed(core, X, M, gain_source, squares):
    with ExitStack() as own, core.stage("gain_loaded", "squared", "rooted", "scaled") as (
            block, gain_loaded, squared, rooted, scaled):
        gain = core.sb(own, "gain_row", D)
        ss = core.sb(own, "sum_squares", TX)
        junk = core.sb(own, "squares", D)
        rms = core.sb(own, "rms", TX)
        inv = core.sb(own, "inverse_rms", TX)

        @block.sync
        def _(sp):
            sp.dma_start(gain[:], gain_source.partition_broadcast(P)).then_inc(gain_loaded, 16)

        @block.scalar
        def _(act):
            for i in range(TX):
                if i:
                    act.wait_ge(squared, i)
                act.activation(junk[:], M[:, i, :], ACT.Square, accum_out=ss[:, i:i + 1]).then_inc(squared, 1)
            act.wait_ge(scaled, 1)
            act.activation(rms[:], ss[:], ACT.Sqrt).then_inc(rooted, 1)

        @block.vector
        def _(dve):
            dve.wait_ge(squared, TX)
            dve.tensor_scalar(ss[:], ss[:], 1.0 / D, EPS, ALU.mult, ALU.add).then_inc(scaled, 1)
            dve.wait_ge(rooted, 1)
            dve.reciprocal(inv[:], rms[:]).then_inc(scaled, 1)
            dve.wait_ge(scaled, 2)
            dve.wait_ge(gain_loaded, 16)
            for i in range(TX):
                dve.scalar_tensor_tensor(out=M[:, i, :], in0=M[:, i, :], scalar=inv[:, i:i + 1], in1=gain[:],
                                         op0=ALU.mult, op1=ALU.mult).then_inc(scaled, 1)
            for i in range(TX):
                dve.wait_ge(scaled, 3 + i)
                dve.tensor_tensor(X[:, i, :], X[:, i, :], M[:, i, :], ALU.add)




def pool_mix(core, U, uT, last_load):
    groups, lead = len(WINDOWS), WINDOWS[-1]
    with ExitStack() as own, core.stage("made", "summed", "mixed", "counted") as (
            block, made, summed, mixed, counted):
        Ws = core.sb(own, "pool_window", 2, lead + NX)
        pooled = core.sb(own, "pooled", groups, NX)
        inv = core.sb(own, "inverse_count", groups, NX)
        t1 = core.sb(own, "token_number", NX)

        @block.sync
        def _(sp):
            core.ring.feed(sp, last_load)

        @block.gpsimd
        def _(pool):
            pool.iota(t1[:], [[1, NX]], base=1, channel_multiplier=0,
                      allow_small_or_imprecise_dtypes=True).then_inc(counted, 1)

        @block.vector
        def _(dve):
            links = [0]

            def linked(instruction):
                links[0] += 1
                instruction.then_inc(made, 1)
                dve.wait_ge(made, links[0])

            dve.wait_ge(counted, 1)
            for g, window in enumerate(WINDOWS):
                linked(dve.tensor_scalar(inv[:, g, :], t1[:], float(window), None, ALU.min))
            linked(dve.reciprocal(inv[:], inv[:]))
            for g, window in enumerate(WINDOWS):
                source, size, n = U[:, g, :], 1, 0
                while size < window:
                    target = Ws[:, n % 2, :]
                    linked(dve.tensor_copy(target[:, 0:size], source[:, 0:size]))
                    linked(dve.tensor_tensor(target[:, size:], source[:, size:], source[:, 0:lead + NX - size],
                                             ALU.add))
                    source, size, n = target, 2 * size, n + 1
                linked(dve.tensor_tensor(pooled[:, g, :], source[:, lead:], inv[:, g, :], ALU.mult))
                dve.tensor_tensor(pooled[:, g, :], pooled[:, g, :], U[:, g, lead:], ALU.subtract) \
                    .then_inc(summed, 1)
            for g in range(groups):
                if g < groups - 1:
                    dve.wait_ge(mixed, g + 1)
                else:
                    core.ring.done(dve, "ev_pool")
                scale = core.cols[:, core.col0["ev_pool_scale_2"] + g:core.col0["ev_pool_scale_2"] + g + 1]
                dve.tensor_scalar(uT[:, g, :], core.bank[g][:], scale, None, ALU.mult)

        @block.tensor
        def _(pe):
            core.ring.wait(pe, "ev_pool")
            w = core.ring.view("ev_pool")
            for g in range(groups):
                pe.wait_ge(summed, g + 1)
                last = pe.matmul(core.bank[g][:], w[:, g, :], pooled[:, g, :], start=True, stop=True)
                last.then_inc(mixed if g < groups - 1 else core.ring.used, 1)




def forget_gate(core, hT, nlf, last_load):
    bias = core.head["ev_b_f_2"]
    with ExitStack() as own, core.stage("dve_done", "act_done") as (block, dve_done, act_done):
        x = core.sb(own, "f_x", TX, FH)
        ax = core.sb(own, "f_abs", TX, FH)
        acc = core.bank[0][:, 0:TX * FH].rearrange("p (t h) -> p t h", h=FH)

        @block.sync
        def _(sp):
            core.ring.feed(sp, last_load)

        @block.tensor
        def _(pe):
            core.ring.wait(pe, "ev_f")
            w = core.ring.view("ev_f")
            for t in range(TX):
                for k in range(KT):
                    last = pe.matmul(acc[:, t, :], hT[:, k, t * P:(t + 1) * P], w[:, k, :],
                                     start=(k == 0), stop=(k == KT - 1))
            last.then_inc(core.ring.used, 1)

        @block.vector
        def _(dve):
            core.ring.done(dve, "ev_f")
            dve.tensor_tensor(x[:], acc, bias.unsqueeze(1).to_broadcast([P, TX, FH]), ALU.add).then_inc(dve_done, 1)
            dve.wait_ge(dve_done, 1)
            dve.scalar_tensor_tensor(out=ax[:], in0=x[:], scalar=-1.0, in1=x[:], op0=ALU.mult,
                                     op1=ALU.max).then_inc(dve_done, 1)
            dve.tensor_scalar(x[:], x[:], -1.0, 0.0, ALU.mult, ALU.max).then_inc(dve_done, 1)
            dve.wait_ge(act_done, 2)
            dve.wait_ge(dve_done, 3)
            dve.tensor_tensor(nlf[:], x[:], ax[:], ALU.add)

        @block.scalar
        def _(act):
            act.wait_ge(dve_done, 2)
            act.activation(ax[:], ax[:], ACT.Exp, scale=-1.0).then_inc(act_done, 1)
            act.wait_ge(act_done, 1)
            act.activation(ax[:], ax[:], ACT.Ln, bias=core.ones[:, 0:1]).then_inc(act_done, 1)


def forgetting_attention(core, QT, KT_, V, nlf, aT, last_load):
    scale = FD ** -0.5
    units = [(h, t) for h in range(FH) for t in range(TX)]
    with ExitStack() as own, core.stage("crow", "crow_moved", "scored", "dve_done", "exped", "normed", "turned",
                                        "moved", "out", "stored", "inverted") as (
            block, crow, crow_moved, scored, dve_done, exped, normed, turned, moved, out, stored, inverted):
        NCR = core.sb(own, "neg_c_rows", 2, NX)
        Sc = core.sb(own, "scores", 2, NX)
        Pr = core.sb(own, "probs", 2, NX)
        mx = core.sb(own, "row_max", 2, 1)
        nm = core.sb(own, "neg_max", 2, 1)
        sm = core.sb(own, "row_sum", 2, 1)
        ri = core.sb(own, "row_inverse", 2, 1)
        PT = core.sb(own, "probs_turned", 2, TX, NX)

        @block.sync
        def _(sp):
            core.ring.feed(sp, last_load)

        @block.tensor
        def _(pe):
            def rows(h):
                if h >= 1:
                    pe.wait_ge(crow_moved, h)
                for t in range(TX):
                    for j in range(t + 1):
                        last = pe.matmul(core.bank[0][:, t * P:(t + 1) * P],
                                         nlf[:, j, h:h + 1].to_broadcast([P, P]),
                                         core.tri[:, FWD, :] if j == t else core.ones[:],
                                         start=(j == 0), stop=(j == t))
                last.then_inc(crow, 1)

            def score(u):
                h, t = units[u]
                part = slice((h % 2) * FD, (h % 2 + 1) * FD)
                if u >= 2:
                    pe.wait_ge(dve_done, 4 * (u - 2) + 1)
                pe.matmul(core.bank[1 + u % 2][:, 0:(t + 1) * P], QT[part, h // 2, t * P:(t + 1) * P],
                          KT_[part, h // 2, 0:(t + 1) * P], start=True, stop=True).then_inc(scored, 1)

            def turn(u):
                h, t = units[u]
                pe.wait_ge(normed, u + 1)
                if u >= 2:
                    pe.wait_ge(moved, u - 1)
                for j in range(t + 1):
                    last = pe.transpose(core.bank[3 + u % 2][:, j * P:(j + 1) * P], Pr[:, u % 2, j * P:(j + 1) * P],
                                        core.ident[:])
                last.then_inc(turned, 1)

            def values(h):
                pe.wait_ge(moved, TX * (h + 1))
                if h >= 2:
                    pe.wait_ge(stored, h - 1)
                acc = core.bank[5 + h % 2][0:FD, :]
                for t in range(TX):
                    for j in range(t + 1):
                        last = pe.matmul(acc[:, t * P:(t + 1) * P], V[:, j, h * FD:(h + 1) * FD],
                                         PT[:, h % 2, j, t * P:(t + 1) * P], start=(j == 0), stop=(j == t))
                last.then_inc(out, 1)

            rows(0)
            for u in range(len(units)):
                score(u)
                if u >= 1:
                    turn(u - 1)
                if u % TX == TX - 1 and u // TX + 1 < FH:
                    rows(u // TX + 1)
                if u % TX == 1 and u >= TX:
                    values(u // TX - 1)
            turn(len(units) - 1)
            values(FH - 1)

        @block.scalar
        def _(act):
            def store(h):
                act.wait_ge(out, h + 1)
                act.activation(aT[(h % 2) * FD:(h % 2 + 1) * FD, h // 2, :], core.bank[5 + h % 2][0:FD, :],
                               ACT.Copy).then_inc(stored, 1)

            def move(u):
                h, t = units[u]
                act.wait_ge(turned, u + 1)
                if h >= 2:
                    act.wait_ge(out, h - 1)
                act.activation(PT[:, h % 2, 0:t + 1, t * P:(t + 1) * P],
                               core.bank[3 + u % 2][:, 0:(t + 1) * P].rearrange("p (j c) -> p j c", c=P),
                               ACT.Copy).then_inc(moved, 1)

            for u, (h, t) in enumerate(units):
                w = (t + 1) * P
                if t == 0:
                    act.wait_ge(crow, h + 1)
                    if h >= 2:
                        act.wait_ge(dve_done, 4 * ((h - 1) * TX - 1) + 1)
                    act.activation(NCR[:, h % 2, :], core.bank[0][:], ACT.Copy).then_inc(crow_moved, 1)
                act.wait_ge(dve_done, 4 * u + 4)
                if u >= 2:
                    act.wait_ge(turned, u - 1)
                act.activation(Pr[:, u % 2, 0:w], Sc[:, u % 2, 0:w], ACT.Exp, bias=nm[:, u % 2, :],
                               accum_out=sm[:, u % 2, :]).then_inc(exped, 1)
                if u >= 1:
                    move(u - 1)
                if u % TX == 2 and u >= TX:
                    store(u // TX - 1)
            move(len(units) - 1)
            store(FH - 1)

        @block.gpsimd
        def _(pool):
            for u, (h, t) in enumerate(units):
                pool.wait_ge(dve_done, 4 * u + 1)
                diagonal = Sc[:, u % 2, t * P:(t + 1) * P]
                pool.affine_select(out=diagonal, in_=diagonal, pattern=[[-1, P]], compare_op=ALU.is_ge,
                                   fill=-3.0e38, base=0, channel_multiplier=1).then_inc(dve_done, 1)

        @block.vector
        def _(dve):
            for u, (h, t) in enumerate(units):
                w = (t + 1) * P
                dve.wait_ge(scored, u + 1)
                dve.wait_ge(crow_moved, h + 1)
                if u >= 2:
                    dve.wait_ge(exped, u - 1)
                dve.scalar_tensor_tensor(out=Sc[:, u % 2, 0:w], in0=core.bank[1 + u % 2][:, 0:w], scalar=scale,
                                         in1=NCR[:, h % 2, 0:w], op0=ALU.mult, op1=ALU.add).then_inc(dve_done, 1)
                dve.wait_ge(dve_done, 4 * u + 2)
                dve.tensor_reduce(mx[:, u % 2, :], Sc[:, u % 2, 0:w], AX.X, ALU.max).then_inc(dve_done, 1)
                dve.wait_ge(dve_done, 4 * u + 3)
                dve.tensor_scalar(nm[:, u % 2, :], mx[:, u % 2, :], -1.0, None, ALU.mult).then_inc(dve_done, 1)
                dve.wait_ge(exped, u + 1)
                dve.reciprocal(ri[:, u % 2, :], sm[:, u % 2, :]).then_inc(inverted, 1)
                dve.wait_ge(inverted, u + 1)
                dve.tensor_scalar(Pr[:, u % 2, 0:w], Pr[:, u % 2, 0:w], ri[:, u % 2, :], None,
                                  ALU.mult).then_inc(normed, 1)




def lru_conv(core, raw, xr):
    taps = core.col0["od_conv_w_2"]
    with core.stage("link") as (block, link):
        @block.vector
        def _(dve):
            for k in range(KT):
                bias = columns(core, "od_conv_b_2")[:, k:k + 1]
                tap = [core.cols[:, taps + w * KT + k:taps + w * KT + k + 1] for w in range(4)]
                dve.tensor_scalar(xr[:, k, :], raw[:, k, 0:NX], tap[0], bias, ALU.mult, ALU.add).then_inc(link, 1)
                for w in (1, 2, 3):
                    dve.wait_ge(link, 4 * k + w)
                    dve.scalar_tensor_tensor(out=xr[:, k, :], in0=raw[:, k, w:w + NX], scalar=tap[w],
                                             in1=xr[:, k, :], op0=ALU.mult, op1=ALU.add).then_inc(link, 1)


def lru(core, xr, gate, y, last_load):
    with ExitStack() as own, core.stage("softened", "gates", "act_done", "dve_done", "link") as (
            block, softened, gates, act_done, dve_done, link):
        soft = core.sb(own, "softplus_lam", 3, KT)
        r = core.sb(own, "lru_r", 2, NX)
        i = core.sb(own, "lru_i", 2, NX)
        a = core.sb(own, "lru_a", 2, NX)
        th = core.sb(own, "lru_tanh", 2, NX)
        de = core.sb(own, "lru_den", 2, NX)
        lam = columns(core, "od_lam_2")
        tiles = LD // P

        @block.sync
        def _(sp):
            core.ring.feed(sp, last_load)

        @block.tensor
        def _(pe):
            core.ring.wait(pe, "od_a")
            core.ring.wait(pe, "od_x")
            for k in range(KT):
                h, e = k // tiles, k % tiles
                if k >= 4:
                    pe.wait_ge(act_done, 4 + 4 * (k - 4) + 2)
                for n, name in enumerate(("od_a", "od_x")):
                    w = core.ring.view(name)
                    for q in range(tiles):
                        last = pe.matmul(core.bank[2 * (k % 4) + n][:], w[:, h * tiles + q, e * P:(e + 1) * P],
                                         xr[:, h * tiles + q, :], start=(q == 0), stop=(q == tiles - 1))
                last.then_inc(gates, 1)
            pe.wait_ge(gates, KT)
            pe.sem_inc(core.ring.used, 2)

        @block.vector
        def _(dve):
            dve.scalar_tensor_tensor(out=soft[:, 0, :], in0=lam, scalar=-1.0, in1=lam, op0=ALU.mult,
                                     op1=ALU.max).then_inc(softened, 1)
            dve.tensor_scalar(soft[:, 1, :], lam, -1.0, 0.0, ALU.mult, ALU.max).then_inc(softened, 1)
            dve.wait_ge(act_done, 2)
            dve.wait_ge(softened, 2)
            dve.tensor_tensor(soft[:, 1, :], soft[:, 1, :], soft[:, 0, :], ALU.add).then_inc(softened, 1)
            dve.wait_ge(softened, 3)
            dve.tensor_scalar(soft[:, 2, :], soft[:, 1, :], -LRU_C, None, ALU.mult).then_inc(softened, 1)
            links = [0]

            def linked(instruction):
                links[0] += 1
                instruction.then_inc(link, 1)
                dve.wait_ge(link, links[0])

            for k in range(KT):
                b = k % 2
                R, I, A, TH, DE = (v[:, b, :] for v in (r, i, a, th, de))
                dve.wait_ge(act_done, 4 + 4 * k + 2)
                dve.wait_ge(softened, 4)
                dve.tensor_scalar(R, R, soft[:, 2, k:k + 1], None, ALU.mult).then_inc(dve_done, 1)
                dve.wait_ge(act_done, 4 + 4 * k + 4)
                linked(dve.tensor_scalar(DE, TH, -1.0, 1.0, ALU.mult, ALU.add))
                linked(dve.reciprocal(DE, DE))
                dve.scalar_tensor_tensor(out=TH, in0=TH, scalar=-2.0, in1=DE, op0=ALU.mult,
                                         op1=ALU.mult).then_inc(dve_done, 1)
                linked(dve.tensor_tensor(I, I, xr[:, k, :], ALU.mult))
                dve.wait_ge(softened, 5 + k)
                linked(dve.tensor_tensor(I, I, TH, ALU.mult))
                linked(dve.tensor_tensor_scan(DE, A, I, 0.0, ALU.mult, ALU.add))
                dve.tensor_tensor(y[:, k, :], DE, gate[:, k, :], ALU.mult).then_inc(dve_done, 1)

        @block.scalar
        def _(act):
            act.wait_ge(softened, 1)
            act.activation(soft[:, 0, :], soft[:, 0, :], ACT.Exp, scale=-1.0).then_inc(act_done, 1)
            act.wait_ge(act_done, 1)
            act.activation(soft[:, 0, :], soft[:, 0, :], ACT.Ln, bias=core.ones[:, 0:1]).then_inc(act_done, 1)
            act.wait_ge(softened, 4)
            act.sem_inc(act_done, 2)
            for k in range(KT):
                b = k % 2
                act.wait_ge(gates, k + 1)
                if k >= 2:
                    act.wait_ge(dve_done, 3 * (k - 1))
                act.activation(r[:, b, :], core.bank[2 * (k % 4)][:], ACT.Sigmoid,
                               bias=columns(core, "od_b_a_2")[:, k:k + 1]).then_inc(act_done, 1)
                act.activation(i[:, b, :], core.bank[2 * (k % 4) + 1][:], ACT.Sigmoid,
                               bias=columns(core, "od_b_x_2")[:, k:k + 1]).then_inc(act_done, 1)
                act.wait_ge(dve_done, 3 * k + 1)
                act.activation(a[:, b, :], r[:, b, :], ACT.Exp).then_inc(act_done, 1)
                act.activation(th[:, b, :], r[:, b, :], ACT.Tanh).then_inc(act_done, 1)
                act.wait_ge(dve_done, 3 * k + 2)
                act.activation(th[:, b, :], th[:, b, :], ACT.Sqrt).then_inc(softened, 1)




def route(core, hT, sets, layer, slotT, gateT, last_load):
    nt = sum(len(tiles) for tiles, _ in sets)
    with ExitStack() as own, core.stage("summed", "dve_done", "exped", "turned", "link", "back") as (
            block, summed, dve_done, exped, turned, link, back):
        ex = core.sb(own, "route_exp", nt, NE)
        mx = core.sb(own, "route_max", nt)
        sm = core.sb(own, "route_sum", nt)
        affT = core.sb(own, "affinity_rows", nt * P)
        left = core.sb(own, "affinity_left", 2, nt * P)
        best = core.sb(own, "best", 8)
        taken = core.sb(own, "taken", nt * P)
        place = core.sb(own, "place", nt * P)
        acc = core.bank[0][:, 0:nt * NE].rearrange("p (t e) -> p t e", e=NE)
        name = f"router{layer}"
        runs = [(a, min(a + 4, nt)) for a in range(0, nt, 4)]

        @block.sync
        def _(sp):
            core.ring.feed(sp, last_load)

        @block.tensor
        def _(pe):
            core.ring.wait(pe, name)
            w = core.ring.view(name)
            for t in range(nt):
                for k in range(KT):
                    last = pe.matmul(acc[:, t, :], hT[:, k, t * P:(t + 1) * P], w[:, k, :],
                                     start=(k == 0), stop=(k == KT - 1))
            last.then_inc(core.ring.used, 1)
            pe.wait_ge(dve_done, 1)
            for n, (a, b) in enumerate(runs):
                for t in range(a, b):
                    last = pe.transpose(core.bank[1 + n][0:NE, (t - a) * P:(t - a + 1) * P], gateT[:, t, :],
                                        core.ident[:])
            last.then_inc(turned, 1)
            pe.wait_ge(dve_done, 2)
            for t in range(nt):
                last = pe.transpose(core.bank[3][:, t * NE:(t + 1) * NE], place[0:NE, t * P:(t + 1) * P],
                                    core.ident[0:NE, 0:NE])
            last.then_inc(back, 1)

        @block.vector
        def _(dve):
            links = [0]

            def linked(instruction):
                links[0] += 1
                instruction.then_inc(link, 1)
                dve.wait_ge(link, links[0])

            core.ring.done(dve, name)
            linked(dve.tensor_reduce(mx[:], acc, AX.X, ALU.max))
            linked(dve.tensor_tensor(ex[:], acc, mx[:].unsqueeze(2).to_broadcast([P, nt, NE]), ALU.subtract))
            dve.wait_ge(exped, 1)
            linked(dve.tensor_reduce(sm[:], ex[:], AX.X, ALU.add))
            linked(dve.reciprocal(sm[:], sm[:]))
            dve.tensor_tensor(gateT[:, 0:nt, :], ex[:], sm[:].unsqueeze(2).to_broadcast([P, nt, NE]),
                              ALU.mult).then_inc(dve_done, 1)
            dve.wait_ge(turned, 1)
            for n, (a, b) in enumerate(runs):
                linked(dve.tensor_copy(affT[0:NE, a * P:b * P], core.bank[1 + n][0:NE, 0:(b - a) * P]))
            at = 0
            for tiles, cap in sets:
                cols = slice(at, at + len(tiles) * P)
                source = affT[0:NE, cols]
                for n in range(cap // 8):
                    linked(dve.max(best[0:NE, :], source))
                    target = left[0:NE, n % 2, cols]
                    linked(dve.match_replace(target, best[0:NE, :], source, -1.0))
                    source = target
                linked(dve.tensor_scalar(taken[0:NE, cols], source, 0.0, None, ALU.is_lt))
                ones = core.ones[0:NE, 0:1].to_broadcast([NE, len(tiles) * P])
                linked(dve.tensor_tensor_scan(place[0:NE, cols], ones, taken[0:NE, cols], 0.0, ALU.mult, ALU.add))
                linked(dve.tensor_tensor(place[0:NE, cols], place[0:NE, cols], taken[0:NE, cols], ALU.mult))
                at += len(tiles) * P
            dve.tensor_scalar(place[0:NE, :], place[0:NE, :], -1.0, None, ALU.add).then_inc(dve_done, 1)
            dve.wait_ge(back, 1)
            dve.tensor_copy(slotT[:, 0:nt, :], core.bank[3][:, 0:nt * NE].rearrange("p (t e) -> p t e", e=NE))

        @block.scalar
        def _(act):
            act.wait_ge(link, 2)
            act.activation(ex[:], ex[:], ACT.Exp).then_inc(exped, 1)


PAIR = 2
LOADS_E = 6


def expert_load(core, layer, expert, kind):
    h = kind // 2 if kind < 4 else kind - 4
    if kind < 4:
        w = core.dram["moe_w_up" if kind % 2 else "moe_w_gate"][layer][expert]
        return by_k(w, h * 512, (h + 1) * 512)
    return by_k(core.dram["moe_w_down"][layer][expert], 0, D, h * 512, (h + 1) * 512)


def moe(core, xn, X, sets, layer, slotT, gateT, out_gate, last_load):
    nc, ring = core.nc, core.ring
    cap_all = sum(c for _, _, c, _ in sets)
    nt = sum(len(t) for _, t, _, _ in sets)
    R = ring.slots
    per = PAIR * LOADS_E
    assert per % R == 0
    n0 = ring.index[f"moe{layer}_0_0"]
    scat = [(si, t) for si, (_, tiles, _, _) in enumerate(sets) for t in tiles]
    PEM = [f"gather{k}" for k in range(KT)] + [f"turn{si}" for si in range(len(sets))]
    PEM += [f"scatter{n}" for n in range(2 * len(scat))]
    HAND = ["slots", "picks", "weighted"] + [f"xs{k}" for k in range(KT)]
    HAND += [name for e in range(PAIR) for name in (f"hid{e}0", f"hid{e}1", f"y{e}")]
    HAND += [f"x{n}" for n in range(2 * len(scat))]
    ACM = [f"turn{si}" for si in range(len(sets))] + [f"silu{e}{h}" for e in range(PAIR) for h in range(2)]
    with ExitStack() as own, core.stage("pe_done", "dve_done", "act_done", "slot_free") as (
            block, pe_done, dve_done, act_done, slot_free):
        pem, dvm, acm = Marks(pe_done, *PEM), Marks(dve_done, *HAND), Marks(act_done, *ACM)
        sl_now = core.sb(own, "slots_now", nt, PAIR)
        ga_now = core.sb(own, "gates_now", nt, PAIR)
        pick, weight, turned, back = [], [], [], []
        for si, (_, tiles, cap, _) in enumerate(sets):
            pick.append(core.sb(own, f"pick{si}", len(tiles), PAIR, cap))
            weight.append(core.sb(own, f"weight{si}", len(tiles), PAIR, cap))
            turned.append(core.sb(own, f"weight_turned{si}", len(tiles) * P))
            back.append(core.sb(own, f"y_gated{si}", D))
        xs = core.sb(own, "xs", KT, PAIR, cap_all)
        sl = core.sb(own, "moe_silu", 4, cap_all)
        hid = core.sb(own, "moe_hid", KT, cap_all)
        gu = [[core.bank[2 * h + n] for n in range(2)] for h in range(2)]
        yb = [core.bank[4], core.bank[5]]
        spare = [core.bank[6], core.bank[7]]

        def wait(engine, marks, step, name):
            engine.wait_ge(marks.sem, marks.at(step, name))

        def arrived(pe, i, j):
            pe.wait_ge(ring.arrived[(n0 + j) % R], i * (16 * per // R) + 16 * ((n0 + j) // R + 1))

        def done(engine, i, j):
            engine.wait_ge(ring.used, i * per + n0 + j + 1)

        def view(j, width):
            return ring.buf[:, (n0 + j) % R, :].rearrange("p (a b) -> p a b", b=width)

        @block.sync
        def _(sp):
            assert ring.issued == n0 + R
            with sp.Fori(0, NE // PAIR - 1) as i:
                for j in range(per):
                    ahead = R + j
                    expert = i * PAIR + PAIR * (ahead // per) + (ahead % per) // LOADS_E
                    source = expert_load(core, layer, expert, ahead % LOADS_E)
                    sp.wait_ge(ring.used, i * per + n0 + j + 1)
                    sp.sem_inc(slot_free, 1)
                    slot = (n0 + ahead) % R
                    sp.dma_start(ring.buf[:, slot, :].rearrange("p (a b) -> p a b", b=source.shape[2]), source) \
                        .then_inc(ring.arrived[slot], 16)
            ring.issued += (NE // PAIR - 1) * per
            ring.feed(sp, last_load)

        @block.tensor
        def _(pe):
            pem.skip_step(pe)
            with pe.Fori(0, NE // PAIR) as i:
                step = i + 1
                wait(pe, dvm, step, "weighted")
                n_out = 2 * len(scat)
                for k in range(KT):
                    b = spare[k % 2]
                    if k >= 2:
                        wait(pe, dvm, step, f"xs{k - 2}")
                    else:
                        wait(pe, dvm, i, f"x{n_out - 2 + k}")
                    out = b[:, 0:PAIR * cap_all].rearrange("p (e c) -> p e c", e=PAIR)
                    for si, (_, tiles, cap, first) in enumerate(sets):
                        for n, t in enumerate(tiles):
                            last = pe.matmul(out[:, :, first:first + cap], xn[:, t, k * P:(k + 1) * P],
                                             pick[si][:, n, :, :], start=(n == 0), stop=(n == len(tiles) - 1))
                    last.then_inc(pe_done, 1)
                wait(pe, dvm, step, f"xs{KT - 1}")
                for si, (_, tiles, cap, _) in enumerate(sets):
                    for n, t in enumerate(tiles):
                        last = pe.transpose(spare[si][0:PAIR * cap, n * P:(n + 1) * P],
                                            weight[si][:, n, :, :].rearrange("p e c -> p (e c)"), core.ident[:])
                    last.then_inc(pe_done, 1)
                for e in range(PAIR):
                    for h in range(2):
                        for n in range(2):
                            j = e * LOADS_E + 2 * h + n
                            arrived(pe, i, j)
                            if n == 0:
                                if e == 0:
                                    wait(pe, dvm, i, f"hid1{h}")
                                    if h == 0:
                                        wait(pe, dvm, step, f"xs{KT - 1}")
                                else:
                                    wait(pe, dvm, step, f"hid0{h}")
                            w = view(j, 512)
                            for c in range(4):
                                for k in range(KT):
                                    last = pe.matmul(gu[h][n][:, c * cap_all:(c + 1) * cap_all],
                                                     w[:, k, c * P:(c + 1) * P], xs[:, k, e, :],
                                                     start=(k == 0), stop=(k == KT - 1))
                            last.then_inc(ring.used, 1)
                    wait(pe, dvm, step, f"y{e - 1}") if e else wait(pe, dvm, i, f"y{PAIR - 1}")
                    for h in range(2):
                        j = e * LOADS_E + 4 + h
                        arrived(pe, i, j)
                        wait(pe, dvm, step, f"hid{e}{h}")
                        w = view(j, D)
                        for n in range(2):
                            for q in range(4):
                                last = pe.matmul(yb[n][0:cap_all, :], hid[:, 4 * h + q, :],
                                                 w[:, q, n * 512:(n + 1) * 512], start=(h == 0 and q == 0),
                                                 stop=(h == 1 and q == 3), skip_group_check=True)
                        last.then_inc(ring.used, 1)
                wait(pe, dvm, step, f"y{PAIR - 1}")
                for n, (si, t) in enumerate(scat):
                    tiles, cap = sets[si][1], sets[si][2]
                    m = tiles.index(t)
                    for h in range(2):
                        if 2 * n + h >= 2:
                            wait(pe, dvm, step, f"x{2 * n + h - 2}")
                        else:
                            for other in range(len(sets)):
                                wait(pe, acm, step, f"turn{other}")
                        pe.matmul(spare[h][:], turned[si][0:PAIR * cap, m * P:(m + 1) * P],
                                  back[si][0:PAIR * cap, h * 512:(h + 1) * 512], start=True,
                                  stop=True).then_inc(pe_done, 1)

        @block.scalar
        def _(act):
            acm.skip_step(act)
            with act.Fori(0, NE // PAIR) as i:
                step = i + 1
                for si, (_, tiles, cap, _) in enumerate(sets):
                    wait(act, pem, step, f"turn{si}")
                    act.activation(turned[si][0:PAIR * cap, :], spare[si][0:PAIR * cap, 0:len(tiles) * P],
                                   ACT.Copy).then_inc(act_done, 1)
                for e in range(PAIR):
                    for h in range(2):
                        done(act, i, e * LOADS_E + 2 * h)
                        if e == 0 and h == 0:
                            wait(act, dvm, i, "hid11")
                        else:
                            wait(act, dvm, step, f"hid{(2 * e + h - 1) // 2}{(2 * e + h - 1) % 2}")
                        act.activation(sl[:].rearrange("p c n -> p (c n)"), gu[h][0][:, 0:4 * cap_all],
                                       ACT.Silu).then_inc(act_done, 1)

        @block.vector
        def _(dve):
            def picks(pair, now, before):
                if before is not None:
                    wait(dve, pem, before, f"turn{len(sets) - 1}")
                dve.tensor_copy(ga_now[:], gateT[:, 0:nt, bass.ds(pair * PAIR, PAIR)])
                dve.tensor_copy(sl_now[:], slotT[:, 0:nt, bass.ds(pair * PAIR, PAIR)]).then_inc(dve_done, 1)
                wait(dve, dvm, now, "slots")
                for weighted in (False, True):
                    for si, (_, tiles, cap, _) in enumerate(sets):
                        for n, t in enumerate(tiles):
                            for e in range(PAIR):
                                s, g = sl_now[:, t, e:e + 1], ga_now[:, t, e:e + 1]
                                target = (weight if weighted else pick)[si][:, n, e, :]
                                if weighted:
                                    last = dve.tensor_scalar(target, core.iota[:, 0:cap], s, g, ALU.is_equal, ALU.mult)
                                else:
                                    last = dve.tensor_scalar(target, core.iota[:, 0:cap], s, None, ALU.is_equal)
                    last.then_inc(dve_done, 1)

            dve.sem_inc(dve_done, len(HAND))
            picks(0, 1, None)
            with dve.Fori(0, NE // PAIR) as i:
                step = i + 1
                for k in range(KT):
                    wait(dve, pem, step, f"gather{k}")
                    got = spare[k % 2][:, 0:PAIR * cap_all].rearrange("p (e c) -> p e c", e=PAIR)
                    for which, _, cap, first in sets:
                        last = dve.tensor_scalar(xs[:, k, :, first:first + cap], got[:, :, first:first + cap],
                                                 core.factor[:, 1, k, which:which + 1],
                                                 core.mod[:, 3 * KT + k, which:which + 1], ALU.mult, ALU.add)
                    last.then_inc(dve_done, 1)
                for e in range(PAIR):
                    for h in range(2):
                        done(dve, i, e * LOADS_E + 2 * h + 1)
                        wait(dve, acm, step, f"silu{e}{h}")
                        if h == 0:
                            done(dve, i, e * LOADS_E - 1) if e else wait(dve, pem, i, "scatter0")
                        dve.tensor_tensor(hid[:, 4 * h:4 * h + 4, :].rearrange("p c n -> p (c n)"),
                                          sl[:].rearrange("p c n -> p (c n)"), gu[h][1][:, 0:4 * cap_all],
                                          ALU.mult).then_inc(dve_done, 1)
                    done(dve, i, e * LOADS_E + 5)
                    if e == 0:
                        wait(dve, pem, i, f"scatter{2 * len(scat) - 1}")
                    for si, (which, _, cap, first) in enumerate(sets):
                        for n in range(2):
                            last = dve.tensor_tensor(back[si][e * cap:(e + 1) * cap, n * 512:(n + 1) * 512],
                                                     yb[n][first:first + cap, :],
                                                     out_gate[first:first + cap, which, n * 512:(n + 1) * 512],
                                                     ALU.mult)
                    last.then_inc(dve_done, 1)
                for n, (si, t) in enumerate(scat):
                    for h in range(2):
                        wait(dve, pem, step, f"scatter{2 * n + h}")
                        cols = slice(h * 512, (h + 1) * 512)
                        dve.tensor_tensor(X[:, t, cols], X[:, t, cols], spare[h][:], ALU.add).then_inc(dve_done, 1)
                picks(i + 1, step + 1, step)



HG = SG // 2


def ssd_scan(core, BT, CT, XS, Y, dec, g0, last_load):
    PEM = ["rows", "cb", "y", "bturn", "state"]
    ACM = ["gap", "decay", "rowexp", "bk"]
    DVM = ["cbm", "w", "te", "out", "fade", "state"]
    POM = ["cs", "xd"]
    with ExitStack() as own, core.stage("pe_f", "pe_b", "dve_f", "dve_b", "act_f", "act_b", "pool_f", "pool_b",
                                        "cleared") as (
            block, pe_f, pe_b, dve_f, dve_b, act_f, act_b, pool_f, pool_b, cleared):
        pem = [Marks(x, *PEM) for x in (pe_f, pe_b)]
        dvm = [Marks(x, *DVM) for x in (dve_f, dve_b)]
        acm = [Marks(x, *ACM) for x in (act_f, act_b)]
        pom = [Marks(x, *POM) for x in (pool_f, pool_b)]
        G = core.sb(own, "s_gap", 2, SR, P)
        E = core.sb(own, "s_decay", 2, SR, P)
        CS = core.sb(own, "s_cs", 2, SR, P)
        CB = core.sb(own, "s_cb", 2, P)
        BK = core.sb(own, "s_bk", 2, P)
        XD = core.sb(own, "s_xd", 2, SR, SP_)
        TE = core.sb(own, "s_te", 2, SR, SP_)
        H = core.sb(own, "s_state", 2, HG, SR, SP_)
        bank = [[core.bank[4 * d + i] for i in range(4)] for d in (FWD, BWD)]
        units = [(s, g) for s in range(TT) for g in range(HG)]

        def wait(engine, marks, u, name):
            engine.wait_ge(marks.sem, marks.at(u, name))

        def skip(engine, marks, u, name, count):
            before = marks.at(u, name) - 1
            if before:
                engine.wait_ge(marks.sem, before)
            engine.sem_inc(marks.sem, count)

        def wide(x, d, t, g, n):
            return x[:, t, d, SR * (g0 + g):SR * (g0 + g + 1)].unsqueeze(2).to_broadcast([P, SR, n])

        def head(x, d, t, g, r):
            first = SR * (g0 + g) + r
            return x[:, t, d, first:first + 1]

        def over_heads(m):
            return m.unsqueeze(1).to_broadcast([P, SR, P])

        def four(b):
            return b[:].rearrange("p (r c) -> p r c", c=P)

        def heads64(b):
            return b[:, 0:SR * SP_].rearrange("p (r c) -> p r c", c=SP_)

        @block.sync
        def _(sp):
            core.ring.feed(sp, last_load)

        @block.tensor
        def _(pe):
            for u, (s, g) in enumerate(units):
                both = [(d, ORDER[d][s], slice(chunk_cols(ORDER[d][s]), chunk_cols(ORDER[d][s]) + P))
                        for d in (FWD, BWD)]
                if s >= TC:
                    for d, t, cols in both:
                        if u > TC * HG:
                            wait(pe, acm[d], u - 1, "rowexp")
                            wait(pe, dvm[d], u - 1, "cbm")
                        for r in range(SR):
                            last = pe.matmul(four(bank[d][0])[:, r, :], head(dec.g, d, t, g, r).to_broadcast([P, P]),
                                             core.tri[:, d, :], start=True, stop=True)
                        last.then_inc(pem[d].sem, 1)
                        pe.matmul(bank[d][1][:, 0:P], BT[:, g, cols], CT[:, g, cols], start=True,
                                  stop=True).then_inc(pem[d].sem, 1)
                else:
                    for d in (FWD, BWD):
                        skip(pe, pem[d], u, "rows", 3)
                for d, t, cols in both:
                    if u:
                        wait(pe, dvm[d], u - 1, "state")
                    else:
                        pe.wait_ge(cleared, 1)
                if s >= TC:
                    for d, t, cols in both:
                        wait(pe, pom[d], u, "xd")
                        wait(pe, dvm[d], u, "w")
                        for r in range(SR):
                            out = bank[d][2][:, r * SP_:(r + 1) * SP_]
                            pe.matmul(out, CS[:, d, r, :], H[:, d, g, r, :], start=True, stop=False)
                            last = pe.matmul(out, E[:, d, r, :], XD[:, d, r, :], start=False, stop=True)
                        last.then_inc(pem[d].sem, 1)
                for d, t, cols in both:
                    pe.transpose(bank[d][3][:, 0:P], BT[:, g, cols], core.ident[:]).then_inc(pem[d].sem, 1)
                for d, t, cols in both:
                    wait(pe, acm[d], u, "bk")
                    wait(pe, dvm[d], u, "te")
                    pe.matmul(bank[d][3][:, 0:SR * SP_], BK[:, d, :], TE[:, d].rearrange("p r c -> p (r c)"),
                              start=True, stop=True).then_inc(pem[d].sem, 1)

        @block.scalar
        def _(act):
            for u, (s, g) in enumerate(units):
                for d in (FWD, BWD):
                    t = ORDER[d][s]
                    if s >= TC:
                        wait(act, pem[d], u, "rows")
                        if u > TC * HG:
                            wait(act, pem[d], u - 1, "y")
                        for r in range(SR):
                            last = act.activation(G[:, d, r, :], four(bank[d][0])[:, r, :], ACT.Abs, scale=-1.0,
                                                  bias=head(dec.cum, d, t, g, r))
                        last.then_inc(acm[d].sem, 1)
                        wait(act, acm[d], u, "gap")
                        act.activation(E[:, d], G[:, d], ACT.Exp, scale=-1.0).then_inc(acm[d].sem, 1)
                        act.activation(CS[:, d], four(bank[d][0]), ACT.Exp).then_inc(acm[d].sem, 1)
                    else:
                        skip(act, acm[d], u, "gap", 3)
                for d in (FWD, BWD):
                    wait(act, pem[d], u, "bturn")
                    if u:
                        wait(act, pem[d], u - 1, "state")
                    act.activation(BK[:, d, :], bank[d][3][:, 0:P], ACT.Copy).then_inc(acm[d].sem, 1)

        @block.gpsimd
        def _(pool):
            for u, (s, g) in enumerate(units):
                for d in (FWD, BWD):
                    t = ORDER[d][s]
                    cols = slice(chunk_cols(t), chunk_cols(t) + P)
                    if s >= TC:
                        wait(pool, acm[d], u, "rowexp")
                        pool.tensor_tensor(CS[:, d], CS[:, d], over_heads(CT[:, g, cols]),
                                           ALU.mult).then_inc(pom[d].sem, 1)
                        pool.tensor_tensor(XD[:, d], XS[:, t, SR * g:SR * (g + 1), :], wide(dec.step, d, t, g, SP_),
                                           ALU.mult).then_inc(pom[d].sem, 1)
                    else:
                        skip(pool, pom[d], u, "cs", 2)

        @block.vector
        def _(dve):
            dve.memset(H[:], 0.0).then_inc(cleared, 1)
            dve.wait_ge(cleared, 1)
            for u, (s, g) in enumerate(units):
                for d in (FWD, BWD):
                    t = ORDER[d][s]
                    if s >= TC:
                        wait(dve, pem[d], u, "cb")
                        dve.tensor_tensor(CB[:, d, :], bank[d][1][:, 0:P], core.tri[:, d, :],
                                          ALU.mult).then_inc(dvm[d].sem, 1)
                        wait(dve, dvm[d], u, "cbm")
                        wait(dve, acm[d], u, "decay")
                        dve.tensor_tensor(E[:, d], E[:, d], over_heads(CB[:, d, :]), ALU.mult) \
                            .then_inc(dvm[d].sem, 1)
                    else:
                        skip(dve, dvm[d], u, "cbm", 2)
                    if u:
                        wait(dve, pem[d], u - 1, "state")
                    dve.tensor_tensor(TE[:, d], XS[:, t, SR * g:SR * (g + 1), :], wide(dec.to_end, d, t, g, SP_),
                                      ALU.mult).then_inc(dvm[d].sem, 1)
                for d in (FWD, BWD):
                    t = ORDER[d][s]
                    if s >= TC:
                        wait(dve, pem[d], u, "y")
                        other = ORDER[1 - d].index(t)
                        y = Y[:, t - TC, SR * g:SR * (g + 1), :]
                        if s < other:
                            dve.tensor_copy(y, heads64(bank[d][2])).then_inc(dvm[d].sem, 1)
                        else:
                            wait(dve, dvm[1 - d], other * HG + g, "out")
                            dve.tensor_tensor(y, y, heads64(bank[d][2]), ALU.add).then_inc(dvm[d].sem, 1)
                    else:
                        skip(dve, dvm[d], u, "out", 1)
                    if s:
                        wait(dve, dvm[d], u - HG, "state")
                    dve.tensor_tensor(H[:, d, g], H[:, d, g], wide(dec.whole, d, t, g, SP_), ALU.mult) \
                        .then_inc(dvm[d].sem, 1)
                    wait(dve, dvm[d], u, "fade")
                    wait(dve, pem[d], u, "state")
                    dve.tensor_tensor(H[:, d, g], H[:, d, g], heads64(bank[d][3]), ALU.add) \
                        .then_inc(dvm[d].sem, 1)


def vector_ops(core, ops, last_load=None):
    with core.stage("link") as (block, link):
        @block.sync
        def _(sp):
            if last_load is not None:
                core.ring.feed(sp, last_load)

        @block.vector
        def _(dve):
            for n, op in enumerate(ops):
                if n:
                    dve.wait_ge(link, n)
                op(dve).then_inc(link, 1)


def turn_all(core, src, dst, factor, KK, runs, last_load):
    with core.stage("turned", "moved") as (block, turned, moved):
        @block.sync
        def _(sp):
            core.ring.feed(sp, last_load)

        @block.tensor
        def _(pe):
            n = 0
            for k in range(KK):
                for run in runs:
                    if n >= 8:
                        pe.wait_ge(moved, n - 7)
                    for j, t in enumerate(run):
                        last = pe.transpose(core.bank[n % 8][:, j * P:(j + 1) * P], src(k, t), core.ident[:])
                    last.then_inc(turned, 1)
                    n += 1

        @block.vector
        def _(dve):
            n = 0
            for k in range(KK):
                for run in runs:
                    dve.wait_ge(turned, n + 1)
                    dve.tensor_scalar(dst(k, run), core.bank[n % 8][:, 0:len(run) * P], factor(k), None,
                                      ALU.mult).then_inc(moved, 1)
                    n += 1


def rms_rows(core, src, junk, inv, tiles, width):
    with ExitStack() as own, core.stage("squared", "scaled", "rooted") as (block, squared, scaled, rooted):
        ss = core.sb(own, "sum_squares", tiles)

        @block.scalar
        def _(act):
            for t in range(tiles):
                if t:
                    act.wait_ge(squared, t)
                act.activation(junk, src(t), ACT.Square, accum_out=ss[:, t:t + 1]).then_inc(squared, 1)
            act.wait_ge(scaled, 1)
            act.activation(ss[:], ss[:], ACT.Sqrt).then_inc(rooted, 1)

        @block.vector
        def _(dve):
            dve.wait_ge(squared, tiles)
            dve.tensor_scalar(ss[:], ss[:], 1.0 / width, EPS, ALU.mult, ALU.add).then_inc(scaled, 1)
            dve.wait_ge(rooted, 1)
            dve.reciprocal(inv, ss[:])


def head_norm(core, O, Z):
    with ExitStack() as own, core.stage("link", "rooted") as (block, link, rooted):
        sq = core.sb(own, "head_squares", TT * GH, GK)
        ss = core.sb(own, "head_sums", TT * GH)
        rows = O.rearrange("p t h c -> p (t h) c")

        @block.vector
        def _(dve):
            dve.tensor_tensor(sq[:], rows, rows, ALU.mult).then_inc(link, 1)
            dve.wait_ge(link, 1)
            dve.tensor_reduce(ss[:], sq[:], AX.X, ALU.add).then_inc(link, 1)
            dve.wait_ge(link, 2)
            dve.tensor_scalar(ss[:], ss[:], 1.0 / GK, EPS, ALU.mult, ALU.add).then_inc(link, 1)
            dve.wait_ge(rooted, 1)
            dve.reciprocal(ss[:], ss[:]).then_inc(link, 1)
            dve.wait_ge(link, 4)
            dve.tensor_tensor(rows, rows, ss[:].unsqueeze(2).to_broadcast([P, TT * GH, GK]), ALU.mult) \
                .then_inc(link, 1)
            dve.wait_ge(link, 5)
            dve.tensor_tensor(rows, rows, Z.rearrange("p t (h c) -> p (t h) c", c=GK), ALU.mult)

        @block.scalar
        def _(act):
            act.wait_ge(link, 3)
            act.activation(ss[:], ss[:], ACT.Sqrt).then_inc(rooted, 1)


def store(core, target, source):
    with core.stage("stored") as (block, stored):
        @block.sync
        def _(sp):
            sp.dma_start(target, source).then_inc(stored, 16)
            sp.wait_ge(stored, 16)




def by_k(w, a, b, r0=0, r1=None):
    r1 = w.shape[0] if r1 is None else r1
    return w[r0:r1, a:b].rearrange("(k p) n -> p k n", p=P)


def plan(core):
    ring, dram = core.ring, core.dram

    def columns_of(name, w, count, first=0, width=512):
        for j in range(count):
            a = first + j * width
            ring.plan(f"{name}{j}", by_k(w, a, min(a + width, w.shape[1])))

    def row_groups(name, w, step):
        for j in range(w.shape[1] // 512):
            for n, r in enumerate(range(0, w.shape[0], step)):
                ring.plan(f"{name}{j}_{n}", by_k(w, j * 512, (j + 1) * 512, r, min(r + step, w.shape[0])))

    def experts(layer):
        ring.plan(f"router{layer}", by_k(dram["router_w"][layer], 0, NE))
        for e in range(NE):
            for kind in range(LOADS_E):
                ring.plan(f"moe{layer}_{e}_{kind}", expert_load(core, layer, e, kind))

    def swiglu(layer):
        for j in range(-(-DFF // 512)):
            for part in ("gate", "up"):
                w = dram[f"ffn_w_{part}_2"][layer]
                ring.plan(f"ffn{layer}_{part}{j}", by_k(w, j * 512, min((j + 1) * 512, DFF)))
        row_groups(f"ffn{layer}_down", dram["ffn_w_down_2"][layer], D)

    columns_of("ada0_", dram["ada_w"][0], 12)
    w = dram["gdn_w_in"][0]
    gdn = GH * GK
    ring.plan("gdn_gates", by_k(w, 4 * gdn, 4 * gdn + 4 * GH))
    for half in range(2):
        for n, part in enumerate("qkv"):
            ring.plan(f"gdn_{part}{half}", by_k(w, n * gdn + half * 512, n * gdn + half * 512 + 512))
    columns_of("gdn_z", w, 2, 3 * gdn)
    columns_of("gdn_out", dram["gdn_w_out"][0], 2)
    experts(0)
    columns_of("ada1_", dram["ada_w"][1], 12)
    w = dram["ssd_w_in"][0]
    sn = SG * SN
    ring.plan("ssd_dt", by_k(w, 2 * SI + 2 * sn, 2 * SI + 2 * sn + 2 * SH))
    for half in range(2):
        columns_of(f"ssd_x{half}_", w, 2, SI + half * (SI // 2))
        ring.plan(f"ssd_b{half}", by_k(w, 2 * SI + half * 512, 2 * SI + half * 512 + 512))
        ring.plan(f"ssd_c{half}", by_k(w, 2 * SI + sn + half * 512, 2 * SI + sn + half * 512 + 512))
    columns_of("ssd_z", w, SI // 512)
    row_groups("ssd_out", dram["ssd_w_out"][0], D)
    experts(1)
    w = dram["ev_w_in_2"][0]
    fw = FH * FD
    ring.plan("ev_q", by_k(w, 0, fw))
    ring.plan("ev_k", by_k(w, fw, 2 * fw))
    ring.plan("ev_u", by_k(w, 3 * fw + FH, w.shape[1]))
    ring.plan("ev_v", by_k(w, 2 * fw, 3 * fw))
    ring.plan("ev_f", by_k(w, 3 * fw, 3 * fw + FH))
    ring.plan("ev_pool", dram["ev_pool_w_2"][0].rearrange("g d e -> d g e"))
    columns_of("ev_out", dram["ev_w_out_2"][0], 2)
    swiglu(0)
    columns_of("od_in", dram["od_w_in_2"][0], 4)
    for n, part in (("od_a", "od_w_a_2"), ("od_x", "od_w_x_2")):
        ring.plan(n, by_k(dram[part][0].rearrange("h d e -> (h d) e"), 0, LD))
    columns_of("od_out", dram["od_w_out_2"][0], 2)
    swiglu(1)


def tile_cols(t, first=0):
    return slice((t - first) * P, (t - first + 1) * P)


def first_norm(core, own, source, last_load):
    hT = core.sb(own, "hT", KT, T)
    with ExitStack() as inner:
        X = core.sb(inner, "X", TT, D)
        xn = core.sb(inner, "xn", TT, D)
        load_x(core, X[:], source)
        norm_turn(core, X, hT, list(range(TT)), lambda k, t: core.factor[:, 0, k, int(t < TC)].unsqueeze(1),
                  lambda k, t: core.mod[:, k, int(t < TC)].unsqueeze(1), xn, last_load)
    return hT


def gdn_layer(core):
    with ExitStack() as own:
        hT = first_norm(core, own, None, "ada0_11")
        O = core.sb(own, "gdn_o", TT, GH, GK)
        with ExitStack() as scans:
            dec = Decays(core, scans, "gdn", GH)
            dec.beta = core.sb(scans, "gdn_beta", TT, 2, GH)
            decays(core, hT, "gdn_gates", GH, core.head["gdn_dt_bias"], core.head["gdn_a_log"], dec, True,
                   "gdn_gates")
            taps, tiles = core.col0["gdn_conv_w"], 3 * GH
            for half in range(2):
                h0 = half * GQ
                with ExitStack() as scan:
                    qT = core.sb(scan, "qT", GQ, CV)
                    kT = core.sb(scan, "kT", GQ, CV)
                    V = core.sb(scan, "V", TT, GQ, P)
                    jobs = []
                    for n, (part, kind) in enumerate((("q", "unit"), ("k", "unit"), ("v", "turn"))):
                        for h in range(GQ):
                            target = ((qT[:, h, :], GK ** -0.5), (kT[:, h, :], 1.0), V[:, :, h, :])[n]
                            jobs.append((f"gdn_{part}{half}", h, n * GH + h0 + h, kind, target))
                    conv_project(core, hT, jobs,
                                 lambda w, ch: core.cols[:, taps + w * tiles + ch:taps + w * tiles + ch + 1],
                                 None, f"gdn_v{half}")
                    delta_scan(core, qT, kT, V, O[:, :, h0:h0 + GQ, :], dec, h0, f"gdn_v{half}")
        core.dump("O", O[:])
        Z = core.sb(own, "gdn_z", TT, D)
        gemm_tokens(core, lambda k, t: hT[:, k, tile_cols(t)], [[(f"gdn_z{j}", range(KT))] for j in range(2)],
                    range(TT), lambda act, linked, j, t, bank: act.activation(
                        Z[:, t, j * 512:(j + 1) * 512], bank[:], ACT.Silu), "gdn_z1", on_scalar=True)
        head_norm(core, O[:], Z[:])
        oT = hT
        runs = [range(0, TC), range(TC, TT)]
        turn_all(core, lambda k, t: O[:, t, k, :], lambda k, run: oT[:, k, run[0] * P:(run[-1] + 1) * P],
                 lambda k: columns(core, "gdn_norm_g", 0, 1), GH, runs, "gdn_z1")
        X = core.sb(own, "X", TT, D)
        gate = core.sb(own, "gate", 2, D)
        tmp = core.sb(own, "gated", 512)
        load_x(core, X[:], None)
        gate_rows(core, gate, 2)
        gemm_tokens(core, lambda k, t: oT[:, k, tile_cols(t)], [[(f"gdn_out{j}", range(KT))] for j in range(2)],
                    range(TT), add_gated(lambda t: X[:, t, :], gate, tmp), "gdn_out1")
        core.dump("X1", X[:])
        store(core, core.x_dram, X[:])


def ssd_layer(core):
    with ExitStack() as own:
        hT = first_norm(core, own, core.x_dram, "ada1_11")
        Y = core.sb(own, "ssd_y", TX, SH, SP_)
        with ExitStack() as scans:
            dec = Decays(core, scans, "ssd", SH)
            decays(core, hT, "ssd_dt", SH, core.head["ssd_dt_bias"], core.head["ssd_a_log"], dec, False, "ssd_dt")
            vector_ops(core, [lambda dve: dve.tensor_tensor(dec.to_end[:], dec.to_end[:], dec.step[:], ALU.mult)])
            taps, tiles = core.col0["ssd_conv_w"], (SI + 2 * SG * SN) // P
            for half in range(2):
                with ExitStack() as scan:
                    XS = core.sb(scan, "ssd_xs", TT, SH // 2, SP_)
                    BT = core.sb(scan, "ssd_bT", HG, CV)
                    CT = core.sb(scan, "ssd_cT", HG, CV)
                    xs = XS[:].rearrange("p t h c -> p t (h c)")
                    jobs = [(f"ssd_x{half}_{c // 4}", c % 4, half * 8 + c, "turn", xs[:, :, c * P:(c + 1) * P])
                            for c in range(8)]
                    for n, (part, target) in enumerate((("b", BT), ("c", CT))):
                        jobs += [(f"ssd_{part}{half}", c, SI // P + n * SG + half * HG + c, "plain", target[:, c, :])
                                 for c in range(HG)]
                    conv_project(core, hT, jobs,
                                 lambda w, ch: core.cols[:, taps + w * tiles + ch:taps + w * tiles + ch + 1],
                                 lambda ch: core.cols[:, core.col0["ssd_conv_b"] + ch:core.col0["ssd_conv_b"] + ch + 1],
                                 f"ssd_c{half}")
                    mine = Y[:, :, half * (SH // 2):(half + 1) * (SH // 2), :]
                    ssd_scan(core, BT, CT, XS, mine, dec, half * HG, f"ssd_c{half}")
                    skip = core.head["ssd_d"][:, half * (SH // 2):(half + 1) * (SH // 2)].unsqueeze(2) \
                        .to_broadcast([P, SH // 2, SP_])
                    ops = []
                    for t in range(TX):
                        x = XS[:, TC + t]
                        ops.append(lambda dve, x=x: dve.tensor_tensor(x, x, skip, ALU.mult))
                        ops.append(lambda dve, x=x, t=t: dve.tensor_tensor(mine[:, t], mine[:, t], x, ALU.add))
                    vector_ops(core, ops)
        core.dump("Y", Y[:])
        y = Y[:].rearrange("p t h c -> p t (h c)")
        with ExitStack() as gated:
            Z = core.sb(gated, "ssd_z", TX, SI)
            gemm_tokens(core, lambda k, t: hT[:, k, tile_cols(t)],
                        [[(f"ssd_z{j}", range(KT))] for j in range(SI // 512)], range(TC, TT),
                        lambda act, linked, j, t, bank: act.activation(
                            Z[:, t - TC, j * 512:(j + 1) * 512], bank[:], ACT.Silu), "ssd_z3", on_scalar=True)
            inv = core.sb(gated, "ssd_inv", TX)
            vector_ops(core, [lambda dve: dve.tensor_tensor(y, y, Z[:], ALU.mult)])
            rms_rows(core, lambda t: y[:, t, :], Z[:, 0, :], inv[:], TX, SI)
            vector_ops(core, [lambda dve, t=t: dve.tensor_scalar(y[:, t, :], y[:, t, :], inv[:, t:t + 1], None,
                                                                 ALU.mult) for t in range(TX)])
        yT = core.sb(own, "ssd_yT", SI // P, NX)
        turn_all(core, lambda k, t: y[:, t, k * P:(k + 1) * P], lambda k, run: yT[:, k, :],
                 lambda k: columns(core, "ssd_norm_g", 0, SI // P)[:, k:k + 1], SI // P, [range(TX)], "ssd_z3")
        X = core.sb(own, "X", TX, D)
        gate = core.sb(own, "gate", 2, D)
        tmp = core.sb(own, "gated", 512)
        load_x(core, X[:], core.x_dram[:, TC:TT, :])
        gate_rows(core, gate, 2)
        groups = [[(f"ssd_out{j}_{n}", range(n * KT, (n + 1) * KT)) for n in range(SI // D)] for j in range(2)]
        gemm_tokens(core, lambda k, t: yT[:, k, tile_cols(t, TC)], groups, range(TC, TT),
                    add_gated(lambda t: X[:, t - TC, :], gate, tmp), "ssd_out1_1")
        core.dump("X3", X[:])
        store(core, core.x_dram[:, TC:TT, :], X[:])


def moe_layer(core, layer, X, tiles):
    nt = len(tiles)
    split = [(0, [i for i, t in enumerate(tiles) if t >= TC], CAPX, 0)]
    if nt == TT:
        split.append((1, [i for i, t in enumerate(tiles) if t < TC], CAPC, CAPX))
    before = "gdn_out1" if layer == 0 else "ssd_out1_1"
    with ExitStack() as own:
        xn = core.sb(own, "xn", nt, D)
        slotT = core.sb(own, "slots", nt, NE + PAIR)
        gateT = core.sb(own, "affinities", nt, NE + PAIR)
        with ExitStack() as routing:
            hT = core.sb(routing, "hT", KT, nt * P)
            vector_ops(core, [lambda dve: dve.memset(slotT[:], -1.0), lambda dve: dve.memset(gateT[:], 0.0)])
            norm_turn(core, X, hT, tiles, lambda k, t: core.factor[:, 1, k, int(t < TC)].unsqueeze(1),
                      lambda k, t: core.mod[:, 3 * KT + k, int(t < TC)].unsqueeze(1), xn, before)
            order = [s for s in reversed(split)]
            route(core, hT, [(s[1], s[2]) for s in order], layer, slotT[:, :, 0:NE], gateT[:, :, 0:NE],
                  f"router{layer}")
        core.dump(f"slots{layer}", slotT[:])
        core.dump(f"gates{layer}", gateT[:])
        gate = core.sb(own, "gate", 2, D)
        gate_rows(core, gate, 5)
        moe(core, xn, X, split, layer, slotT, gateT, gate, f"moe{layer}_{NE - 1}_{LOADS_E - 1}")


def plain_norm(core, X, hT, xn, name, layer, last_load):
    norm_turn(core, X, hT, list(range(TC, TT)), lambda k, t: columns(core, name, layer)[:, k:k + 1], None, xn,
              last_load)


def swiglu_layer(core, X, layer, before):
    with ExitStack() as own:
        hT = core.sb(own, "hT", KT, NX)
        M = core.sb(own, "mixed", TX, D)
        plain_norm(core, X, hT, M, "ffn_pre_g_2", layer, before)
        hid = core.sb(own, "hidden", DFF // P, NX)
        n = -(-DFF // 512)
        loads = [(f"ffn{layer}_gate{j}", f"ffn{layer}_up{j}", 4 * j, min(4, DFF // P - 4 * j)) for j in range(n)]
        swiglu_up(core, hT, hid, loads, f"ffn{layer}_up{n - 1}")
        steps = -(-DFF // D)
        groups = [[(f"ffn{layer}_down{j}_{r}", range(r * KT, min((r + 1) * KT, DFF // P))) for r in range(steps)]
                  for j in range(2)]
        gemm_tokens(core, lambda k, t: hid[:, k, tile_cols(t)], groups, range(TX),
                    lambda dve, linked, j, t, bank: dve.tensor_copy(M[:, t, j * 512:(j + 1) * 512], bank[:]),
                    f"ffn{layer}_down1_{steps - 1}")
        add_normed(core, X, M, core.dram["ffn_post_g_2"][layer], None)


def even_layer(core, X):
    with ExitStack() as own:
        hT = core.sb(own, "hT", KT, NX)
        M = core.sb(own, "mixed", TX, D)
        plain_norm(core, X, hT, M, "mix_pre_g_2", 0, f"moe1_{NE - 1}_{LOADS_E - 1}")
        catT = core.sb(own, "mixedT", KT, NX)
        with ExitStack() as inner:
            QT = core.sb(inner, "qT", 4, NX)
            KTt = core.sb(inner, "kT", 4, NX)
            U = core.sb(inner, "u", len(WINDOWS), WINDOWS[-1] + NX)
            V = core.sb(inner, "v", TX, FH * FD)
            nlf = core.sb(inner, "neg_log_f", TX, FH)
            vector_ops(core, [lambda dve: dve.memset(U[:, :, 0:WINDOWS[-1]], 0.0)])
            jobs = [("ev_q", c, QT[:, c, :], ACT.Copy) for c in range(4)]
            jobs += [("ev_k", c, KTt[:, c, :], ACT.Copy) for c in range(4)]
            jobs += [("ev_u", c, U[:, c, WINDOWS[-1]:], ACT.Copy) for c in range(4)]
            project_channels(core, hT, jobs, "ev_u")
            gemm_tokens(core, lambda k, t: hT[:, k, tile_cols(t)], [[("ev_v", range(KT))]], range(TX),
                        lambda dve, linked, j, t, bank: dve.tensor_copy(V[:, t, :], bank[:]), "ev_v")
            forget_gate(core, hT, nlf, "ev_f")
            pool_mix(core, U, catT[:, 4:8, :], "ev_pool")
            forgetting_attention(core, QT, KTt, V, nlf, catT[:, 0:4, :], "ev_pool")
        gemm_tokens(core, lambda k, t: catT[:, k, tile_cols(t)], [[(f"ev_out{j}", range(KT))] for j in range(2)],
                    range(TX), lambda dve, linked, j, t, bank: dve.tensor_copy(
                        M[:, t, j * 512:(j + 1) * 512], bank[:]), "ev_out1")
        add_normed(core, X, M, core.dram["mix_post_g_2"][0], None)


def odd_layer(core, X):
    with ExitStack() as own:
        hT = core.sb(own, "hT", KT, NX)
        M = core.sb(own, "mixed", TX, D)
        plain_norm(core, X, hT, M, "mix_pre_g_2", 1, "ffn0_down1_2")
        gate = core.sb(own, "lru_gate", KT, NX)
        raw = core.sb(own, "lru_raw", KT, 3 + NX)
        xr = core.sb(own, "lru_x", KT, NX)
        y = core.sb(own, "lru_y", KT, NX)
        vector_ops(core, [lambda dve: dve.memset(raw[:, :, 0:3], 0.0)])
        jobs = [(f"od_in{c // 4}", c % 4, gate[:, c, :], ACT.Gelu_apprx_tanh) for c in range(KT)]
        jobs += [(f"od_in{2 + c // 4}", c % 4, raw[:, c, 3:], ACT.Copy) for c in range(KT)]
        project_channels(core, hT, jobs, "od_in3")
        lru_conv(core, raw, xr)
        lru(core, xr, gate, y, "od_x")
        gemm_tokens(core, lambda k, t: y[:, k, tile_cols(t)], [[(f"od_out{j}", range(KT))] for j in range(2)],
                    range(TX), lambda dve, linked, j, t, bank: dve.tensor_copy(
                        M[:, t, j * 512:(j + 1) * 512], bank[:]), "od_out1")
        add_normed(core, X, M, core.dram["mix_post_g_2"][1], None)


def final_norm(core, X):
    with ExitStack() as own:
        junk = core.sb(own, "squares", D)
        inv = core.sb(own, "inverse_rms", TX)
        gain = core.sb(own, "gain_row", D)
        load_x(core, gain[:], core.dram["final_norm_g"].partition_broadcast(P))
        rms_rows(core, lambda t: X[:, t, :], junk[:], inv[:], TX, D)
        vector_ops(core, [lambda dve, t=t: dve.scalar_tensor_tensor(
            out=X[:, t, :], in0=X[:, t, :], scalar=inv[:, t:t + 1], in1=gain[:], op0=ALU.mult, op1=ALU.mult)
            for t in range(TX)])


def program(nc, dram, out, dumps=None):
    with ExitStack() as ctx:
        core = Core(nc, ctx, dram)
        core.dumps = dumps
        core.ring = Ring(nc, ctx, 3)
        core.mod = core.sb(ctx, "mod", 48, 2)
        core.factor = core.sb(ctx, "factor", 2, KT, 2)
        core.x_dram = nc.dram_tensor("residual", (P, TT, D), F32, kind="Internal").ap()
        plan(core)
        constants(core)
        ada(core, 0)
        gdn_layer(core)
        with ExitStack() as own:
            X = core.sb(own, "X", TT, D)
            load_x(core, X[:], core.x_dram)
            moe_layer(core, 0, X, list(range(TT)))
            core.dump("X2", X[:])
            store(core, core.x_dram, X[:])
        ada(core, 1)
        ssd_layer(core)
        with ExitStack() as own:
            X = core.sb(own, "X", TX, D)
            load_x(core, X[:], core.x_dram[:, TC:TT, :])
            moe_layer(core, 1, X, list(range(TC, TT)))
            core.dump("X4", X[:])
            final_norm(core, X)
            even_layer(core, X)
            core.dump("X5", X[:])
            swiglu_layer(core, X, 0, "ev_out1")
            odd_layer(core, X)
            core.dump("X6", X[:])
            swiglu_layer(core, X, 1, "od_out1")
            store(core, out.rearrange("o (t p) n -> p (o t) n", p=P), X[:])


INPUTS = ["x", "c", "ctx", "c_ctx", "ada_w", "ada_b", "norm1_g", "norm2_g", "router_w", "moe_w_gate",
          "moe_w_up", "moe_w_down", "gdn_w_in", "gdn_conv_w", "gdn_a_log", "gdn_dt_bias", "gdn_norm_g",
          "gdn_w_out", "ssd_w_in", "ssd_conv_w", "ssd_conv_b", "ssd_a_log", "ssd_dt_bias", "ssd_d",
          "ssd_norm_g", "ssd_w_out", "final_norm_g", "mix_pre_g_2", "mix_post_g_2", "ffn_pre_g_2",
          "ffn_post_g_2", "ffn_w_gate_2", "ffn_w_up_2", "ffn_w_down_2", "ev_w_in_2", "ev_b_f_2",
          "ev_pool_w_2", "ev_pool_scale_2", "ev_w_out_2", "od_w_in_2", "od_conv_w_2", "od_conv_b_2",
          "od_w_a_2", "od_b_a_2", "od_w_x_2", "od_b_x_2", "od_lam_2", "od_w_out_2"]


def kernel(**inputs):
    import concourse.bacc as bacc
    from concourse.bass_utils import run_bass_kernel_spmd

    nc = bacc.Bacc("TRN2", target_bir_lowering=False, num_devices=1)
    arrays, dram = {}, {}
    for name in INPUTS:
        a = np.ascontiguousarray(inputs[name])
        arrays[f"in_{name}"] = a
        dram[name] = nc.dram_tensor(f"in_{name}", a.shape, F32, kind="ExternalInput").ap()
    out = nc.dram_tensor("out", (1, NX, D), F32, kind="ExternalOutput").ap()
    program(nc, dram, out)
    result = run_bass_kernel_spmd(nc, [arrays], core_ids=[0])
    return result.results[0]["out"]
```

```python
from contextlib import ExitStack, contextmanager

import numpy as np

import concourse.bass as bass
from concourse import mybir

F32 = mybir.dt.float32
ALU = mybir.AluOpType
ACT = mybir.ActivationFunctionType
AX = mybir.AxisListType

P = 128
D = 1024
KT = D // P
NX, NC = 512, 256
T = NX + NC
TC, TX = NC // P, NX // P
TT = TC + TX
EPS = 1e-6
SLOT = 4096

GH, GK = 8, 128
SH, SP_, SG, SN = 32, 64, 8, 128
SR = SH // SG
SI = SH * SP_
NE, FF = 16, 1024
CAPX, CAPC = 2 * NX // NE, 2 * NC // NE
CAP = CAPX + CAPC
FH, FD = 8, 64
WINDOWS = (2, 4, 8, 16)
DFF = 2816
LH, LD = 4, 256
LRU_C = 8.0

FWD, BWD = 0, 1
ORDER = (tuple(range(TT)), tuple(reversed(range(TC))) + tuple(reversed(range(TC, TT))))


class Marks:

    def __init__(self, sem, *names):
        self.sem, self.names = sem, names

    def skip_step(self, engine):
        engine.sem_inc(self.sem, len(self.names))

    def at(self, step, name):
        return step * len(self.names) + self.names.index(name) + 1


class Ring:

    def __init__(self, nc, ctx, slots):
        self.slots = slots
        self.buf = ctx.enter_context(nc.sbuf_tensor("weight_ring", [P, slots, SLOT], F32))
        self.extra = None
        self.arrived = [nc.alloc_semaphore(name=f"weights_arrived_{s}") for s in range(2 * slots)]
        self.used = nc.alloc_semaphore(name="weights_used")
        self.loads, self.index, self.issued = [], {}, 0
        self.slot, self.before, self.times = [], [], []
        self.last, self.count, self.wide = {}, {}, 0

    def plan(self, name, source, wide=False):
        n = len(self.loads)
        slot = n % self.slots
        if wide:
            if self.wide % (2 * self.slots) >= self.slots:
                slot += self.slots
            self.wide += 1
        self.index[name] = n
        self.loads.append(source)
        self.slot.append(slot)
        self.before.append(self.last.get(slot))
        self.count[slot] = self.count.get(slot, 0) + 1
        self.times.append(self.count[slot])
        self.last[slot] = n

    def place(self, slot):
        return self.buf[:, slot, :] if slot < self.slots else self.extra[:, slot - self.slots, :]

    def part(self, slot, shape):
        flat = self.place(slot)[:, 0:int(np.prod(shape[1:]))]
        return flat.rearrange("p (a b) -> p a b", b=shape[2]) if len(shape) == 3 else flat

    def view(self, name):
        n = self.index[name]
        return self.part(self.slot[n], self.loads[n].shape)

    def wait(self, pe, name):
        n = self.index[name]
        pe.wait_ge(self.arrived[self.slot[n]], 16 * self.times[n])

    def done(self, engine, name):
        engine.wait_ge(self.used, self.index[name] + 1)

    def feed(self, sp, last):
        end = -1 if last is None else self.index[last]
        while self.issued < len(self.loads):
            n = self.issued
            before, slot = self.before[n], self.slot[n]
            if (before is not None and before > end) or (slot >= self.slots and self.extra is None):
                break
            if before is not None:
                sp.wait_ge(self.used, before + 1)
            source = self.loads[n]
            sp.dma_start(self.part(slot, source.shape), source).then_inc(self.arrived[slot], 16)
            self.issued += 1


class Core:

    def __init__(self, nc, ctx, dram):
        self.nc, self.ctx, self.dram = nc, ctx, dram
        self.bank = [ctx.enter_context(nc.psum_tensor(f"bank{i}", [P, 512], F32)) for i in range(8)]
        self.stages, self.buffers = 0, 0

    def sb(self, ctx, name, *shape):
        self.buffers += 1
        return ctx.enter_context(self.nc.sbuf_tensor(f"{name}_b{self.buffers}", [P, *shape], F32))

    @contextmanager
    def stage(self, *names):
        self.stages += 1
        sems = [self.nc.alloc_semaphore(name=f"{n}_s{self.stages}") for n in names]
        with self.nc.Block() as block:
            yield (block, *sems)
        self.nc.clear_and_free_semaphores(sems)
        self.nc.all_engine_barrier()



VECTORS = [("c", 1), ("c_ctx", 1), ("norm1_g", 2), ("norm2_g", 2), ("ada_b", 2), ("gdn_conv_w", 3),
           ("gdn_norm_g", 1), ("ssd_conv_w", 3), ("ssd_conv_b", 1), ("ssd_norm_g", 1),
           ("mix_pre_g_2", 2), ("ffn_pre_g_2", 2), ("ev_pool_scale_2", 1), ("od_conv_w_2", 4),
           ("od_conv_b_2", 1), ("od_b_a_2", 1), ("od_b_x_2", 1), ("od_lam_2", 1)]
HEADED = ["gdn_a_log", "gdn_dt_bias", "ssd_a_log", "ssd_dt_bias", "ssd_d", "ev_b_f_2"]
LEVELS = [1, 2, 4, 8, 16, 32, 64]


def flat_rows(ap):
    names = " ".join("abcdef"[:len(ap.shape)])
    flat = ap.rearrange(f"{names} -> ({names})") if len(ap.shape) > 1 else ap
    return flat.rearrange("(r p) -> r p", p=P)


def constants(core):
    nc, ctx, dram = core.nc, core.ctx, core.dram
    core.ident = core.sb(ctx, "ident", P)
    core.ones = core.sb(ctx, "ones", P)
    core.tri = core.sb(ctx, "tri", 2, P)
    core.strict = core.sb(ctx, "strict", 2, P)
    core.level = core.sb(ctx, "level", len(LEVELS), P)
    core.iota = core.sb(ctx, "iota", 2 * CAPX)
    core.zero = core.sb(ctx, "zero", 1)
    core.eps = core.sb(ctx, "eps", 1)
    pieces, at = {}, 0
    for name, _ in VECTORS:
        n = int(np.prod(dram[name].shape)) // P
        pieces[name] = (at, n)
        at += n
    groups = -(-at // P)
    core.cols = core.sb(ctx, "cols", groups * P)
    core.col0 = {name: first for name, (first, _) in pieces.items()}
    width = {n: int(np.prod(dram[n].shape)) for n in HEADED}
    heads = core.sb(ctx, "heads", sum(width.values()))
    core.head, first = {}, 0
    for n in HEADED:
        core.head[n] = heads[:, first:first + width[n]]
        first += width[n]
    core.c2 = core.sb(ctx, "c2", KT, 2)
    copies = []
    for name, (first, n) in pieces.items():
        source, done = flat_rows(dram[name]), 0
        while done < n:
            g, r = (first + done) // P, (first + done) % P
            k = min(n - done, P - r)
            copies.append((g, r, source[done:done + k, :]))
            done += k
    with ExitStack() as own:
        rows = core.sb(own, "vector_rows", groups, P)
        with core.stage("rows_loaded", "rows_blank", "made", "turned", "copied") as (
                block, rows_loaded, rows_blank, made, turned, copied):
            @block.sync
            def _(sp):
                sp.wait_ge(rows_blank, 1)
                for g, r, source in copies:
                    sp.dma_start(rows[r:r + source.shape[0], g, :], source).then_inc(rows_loaded, 16)
                for n in HEADED:
                    letters = " ".join("abcd"[:len(dram[n].shape)])
                    source = dram[n].rearrange(f"{letters} -> ({letters})")
                    sp.dma_start(core.head[n], source.partition_broadcast(P)).then_inc(rows_loaded, 16)
                core.ring.feed(sp, None)

            @block.gpsimd
            def _(pool):
                pool.memset(core.ident[:], 0.0)
                pool.memset(core.strict[:], 0.0)
                pool.memset(core.zero[:], 0.0)
                pool.memset(core.eps[:], EPS)
                pool.memset(core.level[:], 1.0)
                pool.memset(core.ones[:], 1.0)
                pool.memset(core.tri[:], 1.0)
                pool.iota(core.iota[:], [[1, 2 * CAPX]], base=0, channel_multiplier=0,
                          allow_small_or_imprecise_dtypes=True).then_inc(made, 1)
                pool.wait_ge(made, 1)
                pool.affine_select(out=core.ident[:], in_=core.ident[:], pattern=[[-1, P]],
                                   compare_op=ALU.not_equal, fill=1.0, base=0, channel_multiplier=1)
                for d, sign in ((FWD, 1), (BWD, -1)):
                    for t, fill in ((core.tri, 0.0), (core.strict, 1.0)):
                        pool.affine_select(out=t[:, d, :], in_=t[:, d, :], pattern=[[sign, P]],
                                           compare_op=ALU.is_ge, fill=fill, base=0, channel_multiplier=-sign)
                for n, s in enumerate(LEVELS):
                    view = core.level[:, n, :].rearrange("p (b s) -> p b s", s=2 * s)
                    last = pool.affine_select(out=view, in_=view, pattern=[[-2 * s, P // (2 * s)], [0, 2 * s]],
                                              compare_op=ALU.is_ge, fill=0.0, base=0, channel_multiplier=1)
                last.then_inc(made, 1)
                pool.wait_ge(made, 2)
                for n, s in enumerate(LEVELS):
                    view = core.level[:, n, :].rearrange("p (b s) -> p b s", s=2 * s)
                    last = pool.affine_select(out=view, in_=view, pattern=[[2 * s, P // (2 * s)], [0, 2 * s]],
                                              compare_op=ALU.is_ge, fill=0.0, base=2 * s - 1,
                                              channel_multiplier=-1)
                last.then_inc(made, 1)

            @block.vector
            def _(dve):
                dve.memset(rows[:], 0.0).then_inc(rows_blank, 1)
                dve.wait_ge(made, 3)
                for n in reversed(range(1, len(LEVELS))):
                    dve.tensor_tensor(core.level[:, n, :], core.level[:, n, :], core.level[:, n - 1, :],
                                      ALU.subtract)
                dve.tensor_tensor(core.level[:, 0, :], core.level[:, 0, :], core.ident[:], ALU.subtract)
                dve.wait_ge(turned, 1)
                dve.tensor_copy(core.cols[:], core.bank[0][:, 0:groups * P]).then_inc(copied, 1)

            @block.tensor
            def _(pe):
                pe.wait_ge(made, 3)
                pe.wait_ge(rows_loaded, 16 * (len(copies) + len(HEADED)))
                for g in range(groups):
                    last = pe.transpose(core.bank[0][:, g * P:(g + 1) * P], rows[:, g, :], core.ident[:])
                last.then_inc(turned, 1)

            @block.scalar
            def _(act):
                act.wait_ge(copied, 1)
                for i, name in enumerate(("c", "c_ctx")):
                    first = core.col0[name]
                    act.activation(core.c2[:, :, i], core.cols[:, first:first + KT], ACT.Silu)


def columns(core, name, index=0, count=KT):
    first = core.col0[name] + index * count
    return core.cols[:, first:first + count]




def ada(core, layer):
    mod = core.mod
    tiles = 6 * D // 512
    with ExitStack() as own, core.stage("moved", "m", "turned") as (block, moved, m, turned):
        rows = core.sb(own, "ada_rows", 6 * D)

        @block.sync
        def _(sp):
            core.ring.feed(sp, f"ada{layer}_{tiles - 1}")

        @block.tensor
        def _(pe):
            def turn(j):
                pe.wait_ge(moved, j + 1)
                for c in range(4 * j, 4 * j + 4):
                    last = pe.transpose(core.bank[7][:, 2 * c:2 * c + 2], rows[0:2, c * P:(c + 1) * P],
                                        core.ident[0:2, 0:2])
                if j == tiles - 1:
                    last.then_inc(turned, 1)

            for j in range(tiles):
                name = f"ada{layer}_{j}"
                core.ring.wait(pe, name)
                w = core.ring.view(name)
                if j >= 4:
                    pe.wait_ge(moved, j - 3)
                for k in range(KT):
                    last = pe.matmul(core.bank[j % 4][0:2, :], core.c2[:, k, :], w[:, k, :],
                                     start=(k == 0), stop=(k == KT - 1))
                last.then_inc(core.ring.used, 1)
                if j >= 1:
                    turn(j - 1)
            turn(tiles - 1)

        @block.vector
        def _(dve):
            for j in range(tiles):
                core.ring.done(dve, f"ada{layer}_{j}")
                dve.tensor_copy(rows[0:2, j * 512:(j + 1) * 512], core.bank[j % 4][0:2, :]).then_inc(moved, 1)
            dve.wait_ge(turned, 1)
            bias = core.cols[:, core.col0["ada_b"] + 48 * layer:core.col0["ada_b"] + 48 * layer + 48]
            dve.tensor_tensor(mod[:], core.bank[7][:, 0:96].rearrange("p (c i) -> p c i", i=2),
                              bias.unsqueeze(2).to_broadcast([P, 48, 2]), ALU.add).then_inc(m, 1)
            dve.wait_ge(m, 1)
            for n, (norm, chunk) in enumerate((("norm1_g", 1), ("norm2_g", 4))):
                g = columns(core, norm, layer).unsqueeze(2).to_broadcast([P, KT, 2])
                dve.scalar_tensor_tensor(out=core.factor[:, n, :, :], in0=mod[:, chunk * KT:(chunk + 1) * KT, :],
                                         scalar=1.0, in1=g, op0=ALU.add, op1=ALU.mult)


def gate_rows(core, gate, chunk, last_load=None, beside=()):
    with core.stage("spread", "loaded") as (block, spread, loaded):
        @block.sync
        def _(sp):
            if last_load is not None:
                core.ring.feed(sp, last_load)
            for target, source in beside:
                sp.dma_start(target, source).then_inc(loaded, 16)
            if beside:
                sp.wait_ge(loaded, 16 * len(beside))

        @block.tensor
        def _(pe):
            for i in range(2):
                for h in range(2):
                    for k in range(4):
                        m = core.mod[:, chunk * KT + 4 * h + k, i:i + 1]
                        last = pe.matmul(core.bank[2 * i + h][:, k * P:(k + 1) * P], m.to_broadcast([P, P]),
                                         core.ident[:], start=True, stop=True)
                    last.then_inc(spread, 1)

        @block.vector
        def _(dve):
            for i in range(2):
                for h in range(2):
                    dve.wait_ge(spread, 2 * i + h + 1)
                    dve.tensor_copy(gate[:, i, h * 512:(h + 1) * 512], core.bank[2 * i + h][:])




def norm_turn(core, X, hT, tiles, factor, shift, xn, last_load):
    nt = len(tiles)
    with ExitStack() as own, core.stage("squared", "rooted", "scaled", "turned", "moved") as (
            block, squared, rooted, scaled, turned, moved):
        ss = core.sb(own, "sum_squares", nt)
        rms = core.sb(own, "rms", nt)
        inv = core.sb(own, "inverse_rms", nt)
        runs = [r for r in (tiles[0:TC], tiles[TC:]) if r] if nt == TT else [tiles]

        @block.sync
        def _(sp):
            core.ring.feed(sp, last_load)

        @block.scalar
        def _(act):
            for i, t in enumerate(tiles):
                last = act.activation(xn[:, i, :], X[:, i, :], ACT.Square, accum_out=ss[:, i:i + 1])
            last.then_inc(squared, 1)
            act.wait_ge(scaled, 1)
            act.activation(rms[:], ss[:], ACT.Sqrt).then_inc(rooted, 1)

        @block.vector
        def _(dve):
            dve.wait_ge(squared, 1)
            dve.tensor_scalar(ss[:], ss[:], 1.0 / D, EPS, ALU.mult, ALU.add).then_inc(scaled, 1)
            dve.wait_ge(rooted, 1)
            dve.reciprocal(inv[:], rms[:]).then_inc(scaled, 1)
            dve.wait_ge(scaled, 2)
            for i in range(nt):
                dve.tensor_scalar(xn[:, i, :], X[:, i, :], inv[:, i:i + 1], None, ALU.mult).then_inc(scaled, 1)
            n = 0
            for k in range(KT):
                at = 0
                for run in runs:
                    w = len(run) * P
                    dve.wait_ge(turned, n + 1)
                    b = shift(k, run[0]) if shift else core.zero[:, 0:1]
                    dve.tensor_scalar(hT[:, k, at:at + w], core.bank[n % 8][:, 0:w], factor(k, run[0]), b,
                                      ALU.mult, ALU.add).then_inc(moved, 1)
                    at += w
                    n += 1

        @block.tensor
        def _(pe):
            n = 0
            pe.wait_ge(scaled, 2 + nt)
            for k in range(KT):
                i = 0
                for run in runs:
                    if n >= 8:
                        pe.wait_ge(moved, n - 7)
                    for j in range(len(run)):
                        last = pe.transpose(core.bank[n % 8][:, j * P:(j + 1) * P],
                                            xn[:, i, k * P:(k + 1) * P], core.ident[:])
                        i += 1
                    last.then_inc(turned, 1)
                    n += 1


def input_parts(core, X):
    return [(X[:, a:b, :], ap.rearrange("o (t p) n -> p (o t) n", p=P))
            for a, b, ap in ((0, TC, core.dram["ctx"]), (TC, TT, core.dram["x"]))]


def load_x(core, X, source):
    with core.stage("loaded") as (block, loaded):
        @block.sync
        def _(sp):
            parts = input_parts(core, X) if source is None else [(X, source)]
            for target, part in parts:
                sp.dma_start(target, part).then_inc(loaded, 16)
            sp.wait_ge(loaded, 16 * len(parts))



CV = T + 2
SEQ0 = NC + 2


def chunk_cols(t):
    return t * P + (0 if t < TC else 2)


def conv_project(core, hT, jobs, taps, bias, last_load):
    nc = core.nc
    with ExitStack() as own, core.stage("projected", "padded", "convolved", "activated", "squared",
                                        "posted", "rooted", "link", "stored") as (
            block, projected, padded, convolved, activated, squared, posted, rooted, link, stored):
        raw = core.sb(own, "conv_in", 2, CV + 2)
        cv = core.sb(own, "conv_out", 2, CV)
        sl = core.sb(own, "conv_silu", 2, CV)
        sq = core.sb(own, "conv_square", CV)
        rt = core.sb(own, "conv_root", CV)
        half = T // 2
        N = len(jobs)
        turn_runs = ((0, 4), (4, TT))

        @block.sync
        def _(sp):
            core.ring.feed(sp, last_load)

        @block.gpsimd
        def _(pool):
            pool.memset(raw[:, :, 0:1], 0.0)
            pool.memset(raw[:, :, NC + 1:NC + 3], 0.0)
            pool.memset(raw[:, :, CV + 1:CV + 2], 0.0).then_inc(stored, 1)

        @block.tensor
        def _(pe):
            def post(n):
                _, _, _, kind, _ = jobs[n]
                if kind == "unit":
                    pe.wait_ge(squared, n + 1)
                    if n >= 2:
                        pe.wait_ge(link, 2 * (n - 1))
                    for h in range(2):
                        last = pe.matmul(core.bank[4 + 2 * (n % 2) + h][:, 0:CV // 2], core.ones[:],
                                         sq[:, h * (CV // 2):(h + 1) * (CV // 2)], start=True, stop=True)
                    last.then_inc(posted, 1)
                elif kind == "turn":
                    pe.wait_ge(activated, n + 1)
                    if n >= 2:
                        pe.wait_ge(link, 2 * (n - 1))
                    for h, (a, b) in enumerate(turn_runs):
                        for t in range(a, b):
                            last = pe.transpose(core.bank[4 + 2 * (n % 2) + h][:, (t - a) * P:(t - a + 1) * P],
                                                sl[:, n % 2, chunk_cols(t):chunk_cols(t) + P], core.ident[:])
                    last.then_inc(posted, 1)

            names = [j[0] for j in jobs]
            for n, (name, c, _, _, _) in enumerate(jobs):
                if n == 0 or names[n - 1] != name:
                    core.ring.wait(pe, name)
                w = core.ring.view(name)
                if n >= 2:
                    pe.wait_ge(padded, n - 1)
                for h in range(2):
                    acc = core.bank[2 * (n % 2) + h][:, 0:half]
                    for k in range(KT):
                        last = pe.matmul(acc, w[:, k, c * P:(c + 1) * P], hT[:, k, h * half:(h + 1) * half],
                                         start=(k == 0), stop=(k == KT - 1))
                last.then_inc(projected, 1)
                if n == N - 1 or names[n + 1] != name:
                    pe.wait_ge(projected, n + 1)
                    pe.sem_inc(core.ring.used, 1)
                if n >= 1:
                    post(n - 1)
            post(N - 1)

        @block.scalar
        def _(act):
            act.wait_ge(stored, 1)
            for n, (_, _, ch, kind, target) in enumerate(jobs):
                act.wait_ge(projected, n + 1)
                if n >= 2:
                    act.wait_ge(convolved, 3 * (n - 1))
                a, b = core.bank[2 * (n % 2)], core.bank[2 * (n % 2) + 1]
                r = raw[:, n % 2, :]
                act.activation(r[:, 1:1 + NC], a[:, 0:NC], ACT.Copy)
                act.activation(r[:, SEQ0 + 1:SEQ0 + 1 + half - NC], a[:, NC:half], ACT.Copy)
                act.activation(r[:, SEQ0 + 1 + half - NC:CV + 1], b[:, 0:half], ACT.Copy).then_inc(padded, 1)
                act.wait_ge(convolved, 3 * (n + 1))
                if n >= 2 and kind != "plain":
                    act.wait_ge(link, 2 * (n - 1))
                out = target if kind == "plain" else sl[:, n % 2, :]
                act.activation(out, cv[:, n % 2, :], ACT.Silu,
                               bias=bias(ch) if bias else 0.0).then_inc(activated, 1)
                if kind == "unit":
                    act.wait_ge(posted, n + 1)
                    if n >= 1:
                        act.wait_ge(link, 2 * n)
                    for h in range(2):
                        w = CV // 2
                        last = act.activation(rt[:, h * w:(h + 1) * w], core.bank[4 + 2 * (n % 2) + h][:, 0:w],
                                              ACT.Sqrt, bias=core.eps[:, 0:1])
                    last.then_inc(rooted, 1)

        @block.vector
        def _(dve):
            for n, (_, _, ch, kind, target) in enumerate(jobs):
                r, y = raw[:, n % 2, :], cv[:, n % 2, :]
                dve.wait_ge(padded, n + 1)
                if n >= 2:
                    dve.wait_ge(activated, n - 1)
                dve.tensor_scalar(y, r[:, 1:CV + 1], taps(1, ch), None, ALU.mult).then_inc(convolved, 1)
                dve.wait_ge(convolved, 3 * n + 1)
                dve.scalar_tensor_tensor(out=y, in0=r[:, 0:CV], scalar=taps(0, ch), in1=y, op0=ALU.mult,
                                         op1=ALU.add).then_inc(convolved, 1)
                dve.wait_ge(convolved, 3 * n + 2)
                dve.scalar_tensor_tensor(out=y, in0=r[:, 2:CV + 2], scalar=taps(2, ch), in1=y, op0=ALU.mult,
                                         op1=ALU.add).then_inc(convolved, 1)
                if kind == "unit":
                    goal, scale = target
                    x = sl[:, n % 2, :]
                    dve.wait_ge(activated, n + 1)
                    if n >= 1:
                        dve.wait_ge(posted, n)
                    dve.tensor_tensor(sq[:], x, x, ALU.mult).then_inc(squared, 1)
                    dve.wait_ge(rooted, n + 1)
                    dve.reciprocal(rt[:], rt[:]).then_inc(link, 1)
                    dve.wait_ge(link, 2 * n + 1)
                    dve.scalar_tensor_tensor(out=goal, in0=x, scalar=scale, in1=rt[:], op0=ALU.mult,
                                             op1=ALU.mult).then_inc(link, 1)
                elif kind == "turn":
                    dve.wait_ge(posted, n + 1)
                    for h, (a, b) in enumerate(turn_runs):
                        view = core.bank[4 + 2 * (n % 2) + h][:, 0:(b - a) * P]
                        dve.tensor_copy(target[:, a:b, :], view.rearrange("p (t c) -> p t c", c=P)).then_inc(link, 1)




class Decays:

    def __init__(self, core, ctx, tag, heads):
        self.heads = heads
        self.step = core.sb(ctx, f"{tag}_step", TT, 2, heads)
        self.g = core.sb(ctx, f"{tag}_g", TT, 2, heads)
        self.cum = core.sb(ctx, f"{tag}_cum", TT, 2, heads)
        self.from_start = core.sb(ctx, f"{tag}_from_start", TT, 2, heads)
        self.to_end = core.sb(ctx, f"{tag}_to_end", TT, 2, heads)
        self.whole = core.sb(ctx, f"{tag}_whole", TT, 2, heads)


def decays(core, hT, load, H, bias, a_log, dec, with_beta, last_load):
    n = 2 * H
    first = n if with_beta else 0
    width = first + n
    with ExitStack() as own, core.stage("projected", "dve_done", "act_done", "summed") as (
            block, projected, dve_done, act_done, summed):
        x = core.sb(own, "gate_x", TT, n)
        ax = core.sb(own, "gate_abs", TT, n)
        ex = core.sb(own, "gate_exp", TT, n)
        a = core.sb(own, "gate_a", n)
        acc = core.bank[0][:, 0:TT * width].rearrange("p (t n) -> p t n", n=width)
        step, g, cum = (v[:].rearrange("p t d h -> p t (d h)") for v in (dec.step, dec.g, dec.cum))
        sums = core.bank[1][:, 0:TT * n].rearrange("p (t d h) -> p t d h", d=2, h=H)
        wholes = core.bank[2][:, 0:TT * n].rearrange("p (t n) -> p t n", n=n)
        to_end, whole = (v[:].rearrange("p t d h -> p t (d h)") for v in (dec.to_end, dec.whole))

        @block.sync
        def _(sp):
            core.ring.feed(sp, last_load)

        @block.tensor
        def _(pe):
            core.ring.wait(pe, load)
            w = core.ring.view(load)
            for t in range(TT):
                for k in range(KT):
                    last = pe.matmul(acc[:, t, :], hT[:, k, t * P:(t + 1) * P], w[:, k, :],
                                     start=(k == 0), stop=(k == KT - 1))
            last.then_inc(core.ring.used, 1)
            pe.wait_ge(dve_done, 5)
            for t in range(TT):
                for d in (FWD, BWD):
                    pe.matmul(sums[:, t, d, :], core.tri[:, d, :], dec.g[:, t, d, :], start=True, stop=True)
                last = pe.matmul(wholes[:, t, :], core.ones[:], g[:, t, :], start=True, stop=True)
            last.then_inc(summed, 1)

        @block.vector
        def _(dve):
            core.ring.done(dve, load)
            dve.tensor_tensor(x[:], acc[:, :, first:width], bias.unsqueeze(1).to_broadcast([P, TT, n]),
                              ALU.add).then_inc(dve_done, 1)
            dve.wait_ge(dve_done, 1)
            dve.scalar_tensor_tensor(out=ax[:], in0=x[:], scalar=-1.0, in1=x[:], op0=ALU.mult,
                                     op1=ALU.max).then_inc(dve_done, 1)
            dve.tensor_scalar(x[:], x[:], 0.0, None, ALU.max).then_inc(dve_done, 1)
            dve.wait_ge(act_done, 3)
            dve.wait_ge(dve_done, 3)
            dve.tensor_tensor(step, x[:], ex[:], ALU.add).then_inc(dve_done, 1)
            dve.wait_ge(dve_done, 4)
            dve.scalar_tensor_tensor(out=g, in0=step, scalar=-1.0, in1=a[:].unsqueeze(1).to_broadcast([P, TT, n]),
                                     op0=ALU.mult, op1=ALU.mult).then_inc(dve_done, 1)
            dve.wait_ge(summed, 1)
            dve.tensor_copy(dec.cum[:], sums).then_inc(dve_done, 1)
            dve.wait_ge(dve_done, 6)
            dve.tensor_tensor(ex[:], wholes, cum, ALU.subtract).then_inc(dve_done, 1)

        @block.scalar
        def _(act):
            act.activation(a[:], a_log, ACT.Exp).then_inc(act_done, 1)
            act.wait_ge(dve_done, 2)
            act.activation(ex[:], ax[:], ACT.Exp, scale=-1.0).then_inc(act_done, 1)
            act.wait_ge(act_done, 2)
            act.activation(ex[:], ex[:], ACT.Ln, bias=core.ones[:, 0:1]).then_inc(act_done, 1)
            act.wait_ge(dve_done, 7)
            act.activation(dec.from_start[:], dec.cum[:], ACT.Exp)
            act.activation(to_end, ex[:], ACT.Exp)
            act.activation(whole, wholes, ACT.Exp)
            if with_beta:
                beta = dec.beta[:].rearrange("p t d h -> p t (d h)")
                act.activation(beta, acc[:, :, 0:n], ACT.Sigmoid)



GQ = 4


def delta_scan(core, qT, kT, V, O, dec, h0, last_load):
    nc = core.nc
    PEM = ["gram", "qk", "turn1", "kturn", "ks"]
    for s in LEVELS[1:]:
        PEM += [f"ct{s}", f"u{s}"] + ([f"v{s}"] if s != LEVELS[-1] else [])
    PEM += ["new", "o", "state"]
    BESIDE = {2: ["eks", "rest"], 4: ["rb", "kend"], 8: ["qs"]}
    DVM = ["ge", "low", "attn", "u1", "v1"]
    for s in LEVELS[1:]:
        DVM += [f"u{s}"] + ([f"v{s}"] if s != LEVELS[-1] else []) + BESIDE.get(s, [])
    DVM += ["out", "fade", "state"]
    ACM = ["gap", "decay", "rowexp"] + [f"ct{s}" for s in LEVELS[1:]] + ["new"]
    POM = ["attn", "a1"] + [f"a{s}" for s in LEVELS[1:]]
    with ExitStack() as own, core.stage("pe_f", "pe_b", "dve_f", "dve_b", "act_f", "act_b", "pool_f", "pool_b",
                                        "rows_f", "rows_b", "cleared") as (
            block, pe_f, pe_b, dve_f, dve_b, act_f, act_b, pool_f, pool_b, rows_f, rows_b, cleared):
        rows = [Marks(x, "rows") for x in (rows_f, rows_b)]
        pem = [Marks(x, *PEM) for x in (pe_f, pe_b)]
        dvm = [Marks(x, *DVM) for x in (dve_f, dve_b)]
        acm = [Marks(x, *ACM) for x in (act_f, act_b)]
        pom = [Marks(x, *POM) for x in (pool_f, pool_b)]
        E = core.sb(own, "d_decay", 2, GQ, P)
        L = core.sb(own, "d_low", 2, GQ, P)
        A = core.sb(own, "d_level", 2, 2, GQ, P)
        U = core.sb(own, "d_u", 2, GQ, P)
        W = core.sb(own, "d_v", 2, GQ, P)
        C = core.sb(own, "d_ct", 2, GQ, P)
        G = core.sb(own, "d_gap", 2, GQ, P)
        QS = core.sb(own, "d_qs", 2, GQ, P)
        KE = core.sb(own, "d_kend", 2, GQ, P)
        AT = core.sb(own, "d_attn", 2, GQ, P)
        R, NW = E, C
        S = core.sb(own, "d_state", 2, GQ, P)
        B = [[core.bank[4 * d + i][:].rearrange("p (h c) -> p h c", c=P) for i in range(4)] for d in (FWD, BWD)]
        flat = "p h c -> p (h c)"

        def wide(x, d, t):
            return x[:, t, d, h0:h0 + GQ].unsqueeze(2).to_broadcast([P, GQ, P])

        def over_heads(m):
            return m.unsqueeze(1).to_broadcast([P, GQ, P])

        def steps():
            for s in range(TT):
                yield s

        def wait(engine, marks, s, name):
            engine.wait_ge(marks.sem, marks.at(s, name))

        @block.sync
        def _(sp):
            core.ring.feed(sp, last_load)

        @block.gpsimd
        def _(pool):
            for s in steps():
                for d in (FWD, BWD):
                    wait(pool, dvm[d], s, "attn")
                    if s:
                        wait(pool, pem[d], s - 1, "o")
                    pool.tensor_tensor(AT[:, d], G[:, d], over_heads(core.tri[:, d, :]), ALU.mult) \
                        .then_inc(pom[d].sem, 1)
                for n, size in enumerate(LEVELS):
                    for d in (FWD, BWD):
                        if n > 2:
                            wait(pool, pem[d], s, f"ct{LEVELS[n - 2]}")
                        elif n == 2:
                            wait(pool, pem[d], s, "turn1")
                            wait(pool, dvm[d], s, "v1")
                        elif s:
                            wait(pool, pem[d], s - 1, f"ct{LEVELS[-1 - n]}")
                        wait(pool, dvm[d], s, "low")
                        pool.tensor_tensor(A[:, d, n % 2], L[:, d], over_heads(core.level[:, n, :]), ALU.mult) \
                            .then_inc(pom[d].sem, 1)

        @block.tensor
        def _(pe):
            def each(d, s, name, out, lhsT, rhs):
                for h in range(GQ):
                    last = pe.matmul(out[:, h, :], lhsT(h), rhs(h), start=True, stop=True)
                last.then_inc(pem[d].sem, 1)

            def cumulated(s):
                for d in (FWD, BWD):
                    t = ORDER[d][s]
                    if s:
                        wait(pe, acm[d], s - 1, "rowexp")
                        wait(pe, dvm[d], s - 1, "kend")
                    for h in range(GQ):
                        last = pe.matmul(B[d][0][:, h, :], dec.g[:, t, d, h0 + h:h0 + h + 1].to_broadcast([P, P]),
                                         core.tri[:, d, :], start=True, stop=True)
                    last.then_inc(rows[d].sem, 1)

            cumulated(0)
            for s in steps():
                for d in (FWD, BWD):
                    t = ORDER[d][s]
                    cols = slice(chunk_cols(t), chunk_cols(t) + P)
                    if s:
                        wait(pe, dvm[d], s - 1, "out")
                    each(d, s, "gram", B[d][1], lambda h: kT[:, h, cols], lambda h: kT[:, h, cols])
                    each(d, s, "qk", B[d][2], lambda h: kT[:, h, cols], lambda h: qT[:, h, cols])
                for d in (FWD, BWD):
                    wait(pe, pom[d], s, "a1")
                    wait(pe, dvm[d], s, "ge")
                    for h in range(GQ):
                        last = pe.transpose(B[d][1][:, h, :], A[:, d, 0, h, :], core.ident[:])
                    last.then_inc(pem[d].sem, 1)
                for d in (FWD, BWD):
                    t = ORDER[d][s]
                    cols = slice(chunk_cols(t), chunk_cols(t) + P)
                    wait(pe, acm[d], s, "rowexp")
                    for h in range(GQ):
                        last = pe.transpose(B[d][0][:, h, :], kT[:, h, cols], core.ident[:])
                    last.then_inc(pem[d].sem, 1)
                    if s:
                        wait(pe, dvm[d], s - 1, "state")
                    else:
                        pe.wait_ge(cleared, 1)
                    each(d, s, "ks", B[d][3], lambda h: kT[:, h, cols], lambda h: S[:, d, h, :])
                for n, size in enumerate(LEVELS):
                    if n == 0:
                        continue
                    below = LEVELS[n - 1]
                    for d in (FWD, BWD):
                        wait(pe, pom[d], s, f"a{size}")
                        wait(pe, dvm[d], s, f"v{below}")
                        if n == 1:
                            wait(pe, dvm[d], s, "attn")
                        each(d, s, "ct", B[d][2], lambda h: A[:, d, n % 2, h, :], lambda h: U[:, d, h, :])
                    for d in (FWD, BWD):
                        wait(pe, acm[d], s, f"ct{size}")
                        each(d, s, "u", B[d][1], lambda h: W[:, d, h, :], lambda h: C[:, d, h, :])
                        if size != LEVELS[-1]:
                            each(d, s, "v", B[d][2], lambda h: C[:, d, h, :], lambda h: W[:, d, h, :])
                if s + 1 < TT:
                    cumulated(s + 1)
                for d in (FWD, BWD):
                    wait(pe, dvm[d], s, "rb")
                    wait(pe, dvm[d], s, f"u{LEVELS[-1]}")
                    each(d, s, "new", B[d][1], lambda h: U[:, d, h, :], lambda h: R[:, d, h, :])
                for d in (FWD, BWD):
                    wait(pe, acm[d], s, "new")
                    wait(pe, pom[d], s, "attn")
                    wait(pe, dvm[d], s, "qs")
                    for h in range(GQ):
                        pe.matmul(B[d][2][:, h, :], QS[:, d, h, :], S[:, d, h, :], start=True, stop=False)
                        last = pe.matmul(B[d][2][:, h, :], AT[:, d, h, :], NW[:, d, h, :], start=False, stop=True)
                    last.then_inc(pem[d].sem, 1)
                    each(d, s, "state", B[d][3], lambda h: KE[:, d, h, :], lambda h: NW[:, d, h, :])

        @block.scalar
        def _(act):
            for s in steps():
                for d in (FWD, BWD):
                    t = ORDER[d][s]
                    wait(act, rows[d], s, "rows")
                    if s:
                        wait(act, pom[d], s - 1, "attn")
                        wait(act, pem[d], s - 1, "new")
                    for h in range(GQ):
                        last = act.activation(G[:, d, h, :], B[d][0][:, h, :], ACT.Abs, scale=-1.0,
                                              bias=dec.cum[:, t, d, h0 + h:h0 + h + 1])
                    last.then_inc(acm[d].sem, 1)
                    wait(act, acm[d], s, "gap")
                    act.activation(E[:, d], G[:, d], ACT.Exp, scale=-1.0).then_inc(acm[d].sem, 1)
                    if s:
                        wait(act, pem[d], s - 1, "o")
                    act.activation(QS[:, d], B[d][0], ACT.Exp).then_inc(acm[d].sem, 1)
                for size in LEVELS[1:]:
                    for d in (FWD, BWD):
                        wait(act, pem[d], s, f"ct{size}")
                        act.activation(C[:, d], B[d][2], ACT.Copy).then_inc(acm[d].sem, 1)
                for d in (FWD, BWD):
                    wait(act, pem[d], s, "new")
                    if s:
                        wait(act, pem[d], s - 1, "state")
                    act.activation(NW[:, d], B[d][1], ACT.Copy).then_inc(acm[d].sem, 1)

        @block.vector
        def _(dve):
            def beside(d, s, size):
                t = ORDER[d][s]
                cols = slice(chunk_cols(t), chunk_cols(t) + P)
                if size == 2:
                    wait(dve, pem[d], s, "ks")
                    dve.tensor_tensor(R[:, d], B[d][3], wide(dec.from_start, d, t), ALU.mult) \
                        .then_inc(dvm[d].sem, 1)
                    wait(dve, dvm[d], s, "eks")
                    dve.tensor_tensor(R[:, d], V[:, t], R[:, d], ALU.subtract).then_inc(dvm[d].sem, 1)
                elif size == 4:
                    wait(dve, dvm[d], s, "rest")
                    dve.tensor_tensor(R[:, d], R[:, d], wide(dec.beta, d, t), ALU.mult).then_inc(dvm[d].sem, 1)
                    wait(dve, pem[d], s, "kturn")
                    if s:
                        wait(dve, pem[d], s - 1, "state")
                    dve.tensor_tensor(KE[:, d], B[d][0], wide(dec.to_end, d, t), ALU.mult) \
                        .then_inc(dvm[d].sem, 1)
                elif size == 8:
                    wait(dve, acm[d], s, "rowexp")
                    dve.tensor_tensor(QS[:, d], QS[:, d], qT[:, :, cols], ALU.mult).then_inc(dvm[d].sem, 1)

            dve.memset(S[:], 0.0).then_inc(cleared, 1)
            for s in steps():
                for d in (FWD, BWD):
                    t = ORDER[d][s]
                    wait(dve, acm[d], s, "decay")
                    wait(dve, pem[d], s, "gram")
                    if s:
                        wait(dve, pom[d], s - 1, f"a{LEVELS[-1]}")
                    dve.tensor_tensor(L[:, d], B[d][1], E[:, d], ALU.mult).then_inc(dvm[d].sem, 1)
                    wait(dve, dvm[d], s, "ge")
                    for h in range(GQ):
                        last = dve.scalar_tensor_tensor(out=L[:, d, h, :], in0=L[:, d, h, :],
                                                        scalar=dec.beta[:, t, d, h0 + h:h0 + h + 1],
                                                        in1=core.strict[:, d, :], op0=ALU.mult, op1=ALU.mult)
                    last.then_inc(dvm[d].sem, 1)
                    wait(dve, pem[d], s, "qk")
                    dve.tensor_tensor(G[:, d], B[d][2], E[:, d], ALU.mult).then_inc(dvm[d].sem, 1)
                for d in (FWD, BWD):
                    wait(dve, pem[d], s, "turn1")
                    if s:
                        wait(dve, pem[d], s - 1, "new")
                    dve.scalar_tensor_tensor(out=U[:, d], in0=B[d][1], scalar=-1.0, in1=over_heads(core.ident[:]),
                                             op0=ALU.mult, op1=ALU.add).then_inc(dvm[d].sem, 1)
                    wait(dve, pom[d], s, "a1")
                    dve.scalar_tensor_tensor(out=W[:, d], in0=A[:, d, 0], scalar=-1.0,
                                             in1=over_heads(core.ident[:]), op0=ALU.mult,
                                             op1=ALU.add).then_inc(dvm[d].sem, 1)
                for size in LEVELS[1:]:
                    for d in (FWD, BWD):
                        wait(dve, pem[d], s, f"u{size}")
                        wait(dve, dvm[d], s, f"v{size // 2}")
                        dve.tensor_tensor(U[:, d], U[:, d], B[d][1], ALU.subtract).then_inc(dvm[d].sem, 1)
                        if size != LEVELS[-1]:
                            wait(dve, pem[d], s, f"v{size}")
                            dve.tensor_tensor(W[:, d], W[:, d], B[d][2], ALU.subtract).then_inc(dvm[d].sem, 1)
                    for d in (FWD, BWD):
                        beside(d, s, size)
                for d in (FWD, BWD):
                    t = ORDER[d][s]
                    wait(dve, pem[d], s, "o")
                    other = ORDER[1 - d].index(t)
                    if s < other or (s == other and d == FWD):
                        dve.tensor_copy(O[:, t], B[d][2]).then_inc(dvm[d].sem, 1)
                    else:
                        wait(dve, dvm[1 - d], other, "out")
                        dve.tensor_tensor(O[:, t], O[:, t], B[d][2], ALU.add).then_inc(dvm[d].sem, 1)
                    dve.tensor_tensor(S[:, d], S[:, d], wide(dec.whole, d, t), ALU.mult).then_inc(dvm[d].sem, 1)
                    wait(dve, pem[d], s, "state")
                    wait(dve, dvm[d], s, "fade")
                    dve.tensor_tensor(S[:, d], S[:, d], B[d][3], ALU.add).then_inc(dvm[d].sem, 1)




def gemm_tokens(core, lhs, groups, tiles, evac, last_load, on_scalar=False):
    nt = len(tiles)
    with core.stage("summed", "moved", "link") as (block, summed, moved, link):
        @block.sync
        def _(sp):
            core.ring.feed(sp, last_load)

        @block.tensor
        def _(pe):
            for j, group in enumerate(groups):
                for n, (load, ks) in enumerate(group):
                    core.ring.wait(pe, load)
                    w = core.ring.view(load)
                    width = w.shape[2]
                    for i, t in enumerate(tiles):
                        b = (j * nt + i)
                        if n == 0 and b >= 8:
                            pe.wait_ge(moved, b - 7)
                        for q, k in enumerate(ks):
                            last = pe.matmul(core.bank[b % 8][:, 0:width], lhs(k, t), w[:, q, :],
                                             start=(n == 0 and q == 0), stop=(n == len(group) - 1 and q == len(ks) - 1))
                        if n == len(group) - 1 and i < nt - 1:
                            last.then_inc(summed, 1)
                    last.then_inc(core.ring.used, 1)

        @(block.scalar if on_scalar else block.vector)
        def _(dve):
            links = [0]

            def linked(instruction):
                links[0] += 1
                instruction.then_inc(link, 1)
                dve.wait_ge(link, links[0])

            for j, group in enumerate(groups):
                for i, t in enumerate(tiles):
                    if i < nt - 1:
                        dve.wait_ge(summed, j * (nt - 1) + i + 1)
                    else:
                        core.ring.done(dve, group[-1][0])
                    if not on_scalar and j * nt + i:
                        dve.wait_ge(moved, j * nt + i)
                    evac(dve, linked, j, t, core.bank[(j * nt + i) % 8]).then_inc(moved, 1)


def add_gated(X, gate, tmp, width=512):
    def evac(dve, linked, j, t, bank):
        cols = slice(j * width, (j + 1) * width)
        g = gate[:, int(t < TC), cols]
        linked(dve.tensor_tensor(tmp[:, 0:width], bank[:, 0:width], g, ALU.mult))
        return dve.tensor_tensor(X(t)[:, cols], X(t)[:, cols], tmp[:, 0:width], ALU.add)
    return evac




def swiglu_up(core, hT, hid, loads, last_load):
    with ExitStack() as own, core.stage("gated", "upped", "activated", "stored", "used") as (
            block, gated, upped, activated, stored, used):
        sl = core.sb(own, "swiglu_silu", 4, NX)
        hidden = [f0 + c for _, _, f0, n in loads for c in range(n)]

        @block.sync
        def _(sp):
            core.ring.feed(sp, last_load)

        @block.tensor
        def _(pe):
            for g, u, f0, tiles in loads:
                for name, first_bank, sem in ((g, 0, gated), (u, 4, upped)):
                    core.ring.wait(pe, name)
                    w = core.ring.view(name)
                    for c in range(tiles):
                        f = f0 + c
                        if f >= 4:
                            pe.wait_ge(stored, f - 3)
                        for k in range(KT):
                            last = pe.matmul(core.bank[first_bank + f % 4][:], w[:, k, c * P:(c + 1) * P],
                                             hT[:, k, :], start=(k == 0), stop=(k == KT - 1))
                        last.then_inc(sem, 1)
                    pe.wait_ge(sem, f0 + tiles)
                    pe.sem_inc(core.ring.used, 1)

        @block.scalar
        def _(act):
            for f in hidden:
                act.wait_ge(gated, f + 1)
                if f >= 4:
                    act.wait_ge(stored, f - 3)
                act.activation(sl[:, f % 4, :], core.bank[f % 4][:], ACT.Silu).then_inc(activated, 1)

        @block.vector
        def _(dve):
            for f in hidden:
                dve.wait_ge(activated, f + 1)
                dve.wait_ge(upped, f + 1)
                dve.tensor_tensor(hid[:, f, :], sl[:, f % 4, :], core.bank[4 + f % 4][:],
                                  ALU.mult).then_inc(stored, 1)


def project_channels(core, hT, jobs, last_load):
    with core.stage("summed", "moved") as (block, summed, moved):
        names = [j[0] for j in jobs]

        @block.sync
        def _(sp):
            core.ring.feed(sp, last_load)

        @block.tensor
        def _(pe):
            for n, (name, c, _, _) in enumerate(jobs):
                core.ring.wait(pe, name)
                w = core.ring.view(name)
                if n >= 8:
                    pe.wait_ge(moved, n - 7)
                for k in range(KT):
                    last = pe.matmul(core.bank[n % 8][:], w[:, k, c * P:(c + 1) * P], hT[:, k, :],
                                     start=(k == 0), stop=(k == KT - 1))
                last.then_inc(summed, 1)
                if n == len(jobs) - 1 or names[n + 1] != name:
                    pe.wait_ge(summed, n + 1)
                    pe.sem_inc(core.ring.used, 1)

        @block.scalar
        def _(act):
            for n, (_, _, target, function) in enumerate(jobs):
                act.wait_ge(summed, n + 1)
                act.activation(target, core.bank[n % 8][:], function).then_inc(moved, 1)


def add_normed(core, X, M, gain_source):
    with ExitStack() as own, core.stage("gain_loaded", "squared", "rooted", "scaled") as (
            block, gain_loaded, squared, rooted, scaled):
        gain = core.sb(own, "gain_row", D)
        ss = core.sb(own, "sum_squares", TX)
        junk = core.sb(own, "squares", D)
        rms = core.sb(own, "rms", TX)
        inv = core.sb(own, "inverse_rms", TX)

        @block.sync
        def _(sp):
            sp.dma_start(gain[:], gain_source.partition_broadcast(P)).then_inc(gain_loaded, 16)

        @block.scalar
        def _(act):
            for i in range(TX):
                if i:
                    act.wait_ge(squared, i)
                act.activation(junk[:], M[:, i, :], ACT.Square, accum_out=ss[:, i:i + 1]).then_inc(squared, 1)
            act.wait_ge(scaled, 1)
            act.activation(rms[:], ss[:], ACT.Sqrt).then_inc(rooted, 1)

        @block.vector
        def _(dve):
            dve.wait_ge(squared, TX)
            dve.tensor_scalar(ss[:], ss[:], 1.0 / D, EPS, ALU.mult, ALU.add).then_inc(scaled, 1)
            dve.wait_ge(rooted, 1)
            dve.reciprocal(inv[:], rms[:]).then_inc(scaled, 1)
            dve.wait_ge(scaled, 2)
            dve.wait_ge(gain_loaded, 16)
            for i in range(TX):
                dve.scalar_tensor_tensor(out=M[:, i, :], in0=M[:, i, :], scalar=inv[:, i:i + 1], in1=gain[:],
                                         op0=ALU.mult, op1=ALU.mult).then_inc(scaled, 1)
            for i in range(TX):
                dve.wait_ge(scaled, 3 + i)
                dve.tensor_tensor(X[:, i, :], X[:, i, :], M[:, i, :], ALU.add)




def pool_mix(core, U, uT, last_load):
    groups, lead = len(WINDOWS), WINDOWS[-1]
    with ExitStack() as own, core.stage("made", "summed", "mixed", "counted") as (
            block, made, summed, mixed, counted):
        Ws = core.sb(own, "pool_window", 2, lead + NX)
        pooled = core.sb(own, "pooled", groups, NX)
        inv = core.sb(own, "inverse_count", groups, NX)
        t1 = core.sb(own, "token_number", NX)

        @block.sync
        def _(sp):
            core.ring.feed(sp, last_load)

        @block.gpsimd
        def _(pool):
            pool.iota(t1[:], [[1, NX]], base=1, channel_multiplier=0,
                      allow_small_or_imprecise_dtypes=True).then_inc(counted, 1)

        @block.vector
        def _(dve):
            links = [0]

            def linked(instruction):
                links[0] += 1
                instruction.then_inc(made, 1)
                dve.wait_ge(made, links[0])

            dve.wait_ge(counted, 1)
            for g, window in enumerate(WINDOWS):
                linked(dve.tensor_scalar(inv[:, g, :], t1[:], float(window), None, ALU.min))
            linked(dve.reciprocal(inv[:], inv[:]))
            for g, window in enumerate(WINDOWS):
                source, size, n = U[:, g, :], 1, 0
                while size < window:
                    target = Ws[:, n % 2, :]
                    linked(dve.tensor_copy(target[:, 0:size], source[:, 0:size]))
                    linked(dve.tensor_tensor(target[:, size:], source[:, size:], source[:, 0:lead + NX - size],
                                             ALU.add))
                    source, size, n = target, 2 * size, n + 1
                linked(dve.tensor_tensor(pooled[:, g, :], source[:, lead:], inv[:, g, :], ALU.mult))
                dve.tensor_tensor(pooled[:, g, :], pooled[:, g, :], U[:, g, lead:], ALU.subtract) \
                    .then_inc(summed, 1)
            for g in range(groups):
                if g < groups - 1:
                    dve.wait_ge(mixed, g + 1)
                else:
                    core.ring.done(dve, "ev_pool")
                scale = core.cols[:, core.col0["ev_pool_scale_2"] + g:core.col0["ev_pool_scale_2"] + g + 1]
                dve.tensor_scalar(uT[:, g, :], core.bank[g][:], scale, None, ALU.mult)

        @block.tensor
        def _(pe):
            core.ring.wait(pe, "ev_pool")
            w = core.ring.view("ev_pool")
            for g in range(groups):
                pe.wait_ge(summed, g + 1)
                last = pe.matmul(core.bank[g][:], w[:, g, :], pooled[:, g, :], start=True, stop=True)
                last.then_inc(mixed if g < groups - 1 else core.ring.used, 1)




def forget_gate(core, hT, nlf, last_load):
    bias = core.head["ev_b_f_2"]
    with ExitStack() as own, core.stage("dve_done", "act_done") as (block, dve_done, act_done):
        x = core.sb(own, "f_x", TX, FH)
        ax = core.sb(own, "f_abs", TX, FH)
        acc = core.bank[0][:, 0:TX * FH].rearrange("p (t h) -> p t h", h=FH)

        @block.sync
        def _(sp):
            core.ring.feed(sp, last_load)

        @block.tensor
        def _(pe):
            core.ring.wait(pe, "ev_f")
            w = core.ring.view("ev_f")
            for t in range(TX):
                for k in range(KT):
                    last = pe.matmul(acc[:, t, :], hT[:, k, t * P:(t + 1) * P], w[:, k, :],
                                     start=(k == 0), stop=(k == KT - 1))
            last.then_inc(core.ring.used, 1)

        @block.vector
        def _(dve):
            core.ring.done(dve, "ev_f")
            dve.tensor_tensor(x[:], acc, bias.unsqueeze(1).to_broadcast([P, TX, FH]), ALU.add).then_inc(dve_done, 1)
            dve.wait_ge(dve_done, 1)
            dve.scalar_tensor_tensor(out=ax[:], in0=x[:], scalar=-1.0, in1=x[:], op0=ALU.mult,
                                     op1=ALU.max).then_inc(dve_done, 1)
            dve.tensor_scalar(x[:], x[:], -1.0, 0.0, ALU.mult, ALU.max).then_inc(dve_done, 1)
            dve.wait_ge(act_done, 2)
            dve.wait_ge(dve_done, 3)
            dve.tensor_tensor(nlf[:], x[:], ax[:], ALU.add)

        @block.scalar
        def _(act):
            act.wait_ge(dve_done, 2)
            act.activation(ax[:], ax[:], ACT.Exp, scale=-1.0).then_inc(act_done, 1)
            act.wait_ge(act_done, 1)
            act.activation(ax[:], ax[:], ACT.Ln, bias=core.ones[:, 0:1]).then_inc(act_done, 1)


def forgetting_attention(core, QT, KT_, V, nlf, aT, last_load):
    scale = FD ** -0.5
    units = [(h, t) for h in range(FH) for t in range(TX)]
    with ExitStack() as own, core.stage("crow", "crow_moved", "scored", "dve_done", "exped", "normed", "turned",
                                        "moved", "out", "stored", "inverted") as (
            block, crow, crow_moved, scored, dve_done, exped, normed, turned, moved, out, stored, inverted):
        NCR = core.sb(own, "neg_c_rows", 2, NX)
        Sc = core.sb(own, "scores", 2, NX)
        Pr = core.sb(own, "probs", 2, NX)
        mx = core.sb(own, "row_max", 2, 1)
        nm = core.sb(own, "neg_max", 2, 1)
        sm = core.sb(own, "row_sum", 2, 1)
        ri = core.sb(own, "row_inverse", 2, 1)
        PT = core.sb(own, "probs_turned", 2, TX, NX)

        @block.sync
        def _(sp):
            core.ring.feed(sp, last_load)

        @block.tensor
        def _(pe):
            def rows(h):
                if h >= 1:
                    pe.wait_ge(crow_moved, h)
                for t in range(TX):
                    for j in range(t + 1):
                        last = pe.matmul(core.bank[0][:, t * P:(t + 1) * P],
                                         nlf[:, j, h:h + 1].to_broadcast([P, P]),
                                         core.tri[:, FWD, :] if j == t else core.ones[:],
                                         start=(j == 0), stop=(j == t))
                last.then_inc(crow, 1)

            def score(u):
                h, t = units[u]
                part = slice((h % 2) * FD, (h % 2 + 1) * FD)
                if u >= 2:
                    pe.wait_ge(dve_done, 4 * (u - 2) + 1)
                pe.matmul(core.bank[1 + u % 2][:, 0:(t + 1) * P], QT[part, h // 2, t * P:(t + 1) * P],
                          KT_[part, h // 2, 0:(t + 1) * P], start=True, stop=True).then_inc(scored, 1)

            def turn(u):
                h, t = units[u]
                pe.wait_ge(normed, u + 1)
                if u >= 2:
                    pe.wait_ge(moved, u - 1)
                for j in range(t + 1):
                    last = pe.transpose(core.bank[3 + u % 2][:, j * P:(j + 1) * P], Pr[:, u % 2, j * P:(j + 1) * P],
                                        core.ident[:])
                last.then_inc(turned, 1)

            def values(h):
                pe.wait_ge(moved, TX * (h + 1))
                if h >= 2:
                    pe.wait_ge(stored, h - 1)
                acc = core.bank[5 + h % 2][0:FD, :]
                for t in range(TX):
                    for j in range(t + 1):
                        last = pe.matmul(acc[:, t * P:(t + 1) * P], V[:, j, h * FD:(h + 1) * FD],
                                         PT[:, h % 2, j, t * P:(t + 1) * P], start=(j == 0), stop=(j == t))
                last.then_inc(out, 1)

            rows(0)
            for u in range(len(units)):
                score(u)
                if u >= 1:
                    turn(u - 1)
                if u % TX == TX - 1 and u // TX + 1 < FH:
                    rows(u // TX + 1)
                if u % TX == 1 and u >= TX:
                    values(u // TX - 1)
            turn(len(units) - 1)
            values(FH - 1)

        @block.scalar
        def _(act):
            def store(h):
                act.wait_ge(out, h + 1)
                act.activation(aT[(h % 2) * FD:(h % 2 + 1) * FD, h // 2, :], core.bank[5 + h % 2][0:FD, :],
                               ACT.Copy).then_inc(stored, 1)

            def move(u):
                h, t = units[u]
                act.wait_ge(turned, u + 1)
                if h >= 2:
                    act.wait_ge(out, h - 1)
                act.activation(PT[:, h % 2, 0:t + 1, t * P:(t + 1) * P],
                               core.bank[3 + u % 2][:, 0:(t + 1) * P].rearrange("p (j c) -> p j c", c=P),
                               ACT.Copy).then_inc(moved, 1)

            for u, (h, t) in enumerate(units):
                w = (t + 1) * P
                if t == 0:
                    act.wait_ge(crow, h + 1)
                    if h >= 2:
                        act.wait_ge(dve_done, 4 * ((h - 1) * TX - 1) + 1)
                    act.activation(NCR[:, h % 2, :], core.bank[0][:], ACT.Copy).then_inc(crow_moved, 1)
                act.wait_ge(dve_done, 4 * u + 4)
                if u >= 2:
                    act.wait_ge(turned, u - 1)
                act.activation(Pr[:, u % 2, 0:w], Sc[:, u % 2, 0:w], ACT.Exp, bias=nm[:, u % 2, :],
                               accum_out=sm[:, u % 2, :]).then_inc(exped, 1)
                if u >= 1:
                    move(u - 1)
                if u % TX == 2 and u >= TX:
                    store(u // TX - 1)
            move(len(units) - 1)
            store(FH - 1)

        @block.gpsimd
        def _(pool):
            for u, (h, t) in enumerate(units):
                pool.wait_ge(dve_done, 4 * u + 1)
                diagonal = Sc[:, u % 2, t * P:(t + 1) * P]
                pool.affine_select(out=diagonal, in_=diagonal, pattern=[[-1, P]], compare_op=ALU.is_ge,
                                   fill=-3.0e38, base=0, channel_multiplier=1).then_inc(dve_done, 1)

        @block.vector
        def _(dve):
            for u, (h, t) in enumerate(units):
                w = (t + 1) * P
                dve.wait_ge(scored, u + 1)
                dve.wait_ge(crow_moved, h + 1)
                if u >= 2:
                    dve.wait_ge(exped, u - 1)
                dve.scalar_tensor_tensor(out=Sc[:, u % 2, 0:w], in0=core.bank[1 + u % 2][:, 0:w], scalar=scale,
                                         in1=NCR[:, h % 2, 0:w], op0=ALU.mult, op1=ALU.add).then_inc(dve_done, 1)
                dve.wait_ge(dve_done, 4 * u + 2)
                dve.tensor_reduce(mx[:, u % 2, :], Sc[:, u % 2, 0:w], AX.X, ALU.max).then_inc(dve_done, 1)
                dve.wait_ge(dve_done, 4 * u + 3)
                dve.tensor_scalar(nm[:, u % 2, :], mx[:, u % 2, :], -1.0, None, ALU.mult).then_inc(dve_done, 1)
                dve.wait_ge(exped, u + 1)
                dve.reciprocal(ri[:, u % 2, :], sm[:, u % 2, :]).then_inc(inverted, 1)
                dve.wait_ge(inverted, u + 1)
                dve.tensor_scalar(Pr[:, u % 2, 0:w], Pr[:, u % 2, 0:w], ri[:, u % 2, :], None,
                                  ALU.mult).then_inc(normed, 1)




def lru_conv(core, raw, xr):
    taps = core.col0["od_conv_w_2"]
    with core.stage("link") as (block, link):
        @block.vector
        def _(dve):
            for k in range(KT):
                bias = columns(core, "od_conv_b_2")[:, k:k + 1]
                tap = [core.cols[:, taps + w * KT + k:taps + w * KT + k + 1] for w in range(4)]
                dve.tensor_scalar(xr[:, k, :], raw[:, k, 0:NX], tap[0], bias, ALU.mult, ALU.add).then_inc(link, 1)
                for w in (1, 2, 3):
                    dve.wait_ge(link, 4 * k + w)
                    dve.scalar_tensor_tensor(out=xr[:, k, :], in0=raw[:, k, w:w + NX], scalar=tap[w],
                                             in1=xr[:, k, :], op0=ALU.mult, op1=ALU.add).then_inc(link, 1)


def lru(core, xr, gate, y, last_load):
    with ExitStack() as own, core.stage("softened", "gates", "act_done", "dve_done", "link") as (
            block, softened, gates, act_done, dve_done, link):
        soft = core.sb(own, "softplus_lam", 3, KT)
        r = core.sb(own, "lru_r", 2, NX)
        i = core.sb(own, "lru_i", 2, NX)
        a = core.sb(own, "lru_a", 2, NX)
        th = core.sb(own, "lru_tanh", 2, NX)
        de = core.sb(own, "lru_den", 2, NX)
        lam = columns(core, "od_lam_2")
        tiles = LD // P

        @block.sync
        def _(sp):
            core.ring.feed(sp, last_load)

        @block.tensor
        def _(pe):
            core.ring.wait(pe, "od_a")
            core.ring.wait(pe, "od_x")
            for k in range(KT):
                h, e = k // tiles, k % tiles
                if k >= 4:
                    pe.wait_ge(act_done, 4 + 4 * (k - 4) + 2)
                for n, name in enumerate(("od_a", "od_x")):
                    w = core.ring.view(name)
                    for q in range(tiles):
                        last = pe.matmul(core.bank[2 * (k % 4) + n][:], w[:, h * tiles + q, e * P:(e + 1) * P],
                                         xr[:, h * tiles + q, :], start=(q == 0), stop=(q == tiles - 1))
                last.then_inc(gates, 1)
            pe.wait_ge(gates, KT)
            pe.sem_inc(core.ring.used, 2)

        @block.vector
        def _(dve):
            dve.scalar_tensor_tensor(out=soft[:, 0, :], in0=lam, scalar=-1.0, in1=lam, op0=ALU.mult,
                                     op1=ALU.max).then_inc(softened, 1)
            dve.tensor_scalar(soft[:, 1, :], lam, -1.0, 0.0, ALU.mult, ALU.max).then_inc(softened, 1)
            dve.wait_ge(act_done, 2)
            dve.wait_ge(softened, 2)
            dve.tensor_tensor(soft[:, 1, :], soft[:, 1, :], soft[:, 0, :], ALU.add).then_inc(softened, 1)
            dve.wait_ge(softened, 3)
            dve.tensor_scalar(soft[:, 2, :], soft[:, 1, :], -LRU_C, None, ALU.mult).then_inc(softened, 1)
            links = [0]

            def linked(instruction):
                links[0] += 1
                instruction.then_inc(link, 1)
                dve.wait_ge(link, links[0])

            for k in range(KT):
                b = k % 2
                R, I, A, TH, DE = (v[:, b, :] for v in (r, i, a, th, de))
                dve.wait_ge(act_done, 4 + 4 * k + 2)
                dve.wait_ge(softened, 4)
                dve.tensor_scalar(R, R, soft[:, 2, k:k + 1], None, ALU.mult).then_inc(dve_done, 1)
                dve.wait_ge(act_done, 4 + 4 * k + 4)
                linked(dve.tensor_scalar(DE, TH, -1.0, 1.0, ALU.mult, ALU.add))
                linked(dve.reciprocal(DE, DE))
                dve.scalar_tensor_tensor(out=TH, in0=TH, scalar=-2.0, in1=DE, op0=ALU.mult,
                                         op1=ALU.mult).then_inc(dve_done, 1)
                linked(dve.tensor_tensor(I, I, xr[:, k, :], ALU.mult))
                dve.wait_ge(softened, 5 + k)
                linked(dve.tensor_tensor(I, I, TH, ALU.mult))
                linked(dve.tensor_tensor_scan(DE, A, I, 0.0, ALU.mult, ALU.add))
                dve.tensor_tensor(y[:, k, :], DE, gate[:, k, :], ALU.mult).then_inc(dve_done, 1)

        @block.scalar
        def _(act):
            act.wait_ge(softened, 1)
            act.activation(soft[:, 0, :], soft[:, 0, :], ACT.Exp, scale=-1.0).then_inc(act_done, 1)
            act.wait_ge(act_done, 1)
            act.activation(soft[:, 0, :], soft[:, 0, :], ACT.Ln, bias=core.ones[:, 0:1]).then_inc(act_done, 1)
            act.wait_ge(softened, 4)
            act.sem_inc(act_done, 2)
            for k in range(KT):
                b = k % 2
                act.wait_ge(gates, k + 1)
                if k >= 2:
                    act.wait_ge(dve_done, 3 * (k - 1))
                act.activation(r[:, b, :], core.bank[2 * (k % 4)][:], ACT.Sigmoid,
                               bias=columns(core, "od_b_a_2")[:, k:k + 1]).then_inc(act_done, 1)
                act.activation(i[:, b, :], core.bank[2 * (k % 4) + 1][:], ACT.Sigmoid,
                               bias=columns(core, "od_b_x_2")[:, k:k + 1]).then_inc(act_done, 1)
                act.wait_ge(dve_done, 3 * k + 1)
                act.activation(a[:, b, :], r[:, b, :], ACT.Exp).then_inc(act_done, 1)
                act.activation(th[:, b, :], r[:, b, :], ACT.Tanh).then_inc(act_done, 1)
                act.wait_ge(dve_done, 3 * k + 2)
                act.activation(th[:, b, :], th[:, b, :], ACT.Sqrt).then_inc(softened, 1)




def route(core, hT, sets, layer, slotT, gateT, last_load):
    nt = sum(len(tiles) for tiles, _ in sets)
    with ExitStack() as own, core.stage("summed", "dve_done", "exped", "turned", "link", "back") as (
            block, summed, dve_done, exped, turned, link, back):
        ex = core.sb(own, "route_exp", nt, NE)
        mx = core.sb(own, "route_max", nt)
        sm = core.sb(own, "route_sum", nt)
        affT = core.sb(own, "affinity_rows", nt * P)
        left = core.sb(own, "affinity_left", 2, nt * P)
        best = core.sb(own, "best", 8)
        taken = core.sb(own, "taken", nt * P)
        place = core.sb(own, "place", nt * P)
        acc = core.bank[0][:, 0:nt * NE].rearrange("p (t e) -> p t e", e=NE)
        name = f"router{layer}"
        runs = [(a, min(a + 4, nt)) for a in range(0, nt, 4)]

        @block.sync
        def _(sp):
            core.ring.feed(sp, last_load)

        @block.tensor
        def _(pe):
            core.ring.wait(pe, name)
            w = core.ring.view(name)
            for t in range(nt):
                for k in range(KT):
                    last = pe.matmul(acc[:, t, :], hT[:, k, t * P:(t + 1) * P], w[:, k, :],
                                     start=(k == 0), stop=(k == KT - 1))
            last.then_inc(core.ring.used, 1)
            pe.wait_ge(dve_done, 1)
            for n, (a, b) in enumerate(runs):
                for t in range(a, b):
                    last = pe.transpose(core.bank[1 + n][0:NE, (t - a) * P:(t - a + 1) * P], gateT[:, t, :],
                                        core.ident[:])
            last.then_inc(turned, 1)
            pe.wait_ge(dve_done, 2)
            for t in range(nt):
                last = pe.transpose(core.bank[3][:, t * NE:(t + 1) * NE], place[0:NE, t * P:(t + 1) * P],
                                    core.ident[0:NE, 0:NE])
            last.then_inc(back, 1)

        @block.vector
        def _(dve):
            links = [0]

            def linked(instruction):
                links[0] += 1
                instruction.then_inc(link, 1)
                dve.wait_ge(link, links[0])

            core.ring.done(dve, name)
            linked(dve.tensor_reduce(mx[:], acc, AX.X, ALU.max))
            linked(dve.tensor_tensor(ex[:], acc, mx[:].unsqueeze(2).to_broadcast([P, nt, NE]), ALU.subtract))
            dve.wait_ge(exped, 1)
            linked(dve.tensor_reduce(sm[:], ex[:], AX.X, ALU.add))
            linked(dve.reciprocal(sm[:], sm[:]))
            dve.tensor_tensor(gateT[:, 0:nt, :], ex[:], sm[:].unsqueeze(2).to_broadcast([P, nt, NE]),
                              ALU.mult).then_inc(dve_done, 1)
            dve.wait_ge(turned, 1)
            for n, (a, b) in enumerate(runs):
                linked(dve.tensor_copy(affT[0:NE, a * P:b * P], core.bank[1 + n][0:NE, 0:(b - a) * P]))
            at = 0
            for tiles, cap in sets:
                cols = slice(at, at + len(tiles) * P)
                source = affT[0:NE, cols]
                for n in range(cap // 8):
                    linked(dve.max(best[0:NE, :], source))
                    target = left[0:NE, n % 2, cols]
                    linked(dve.match_replace(target, best[0:NE, :], source, -1.0))
                    source = target
                linked(dve.tensor_scalar(taken[0:NE, cols], source, 0.0, None, ALU.is_lt))
                ones = core.ones[0:NE, 0:1].to_broadcast([NE, len(tiles) * P])
                linked(dve.tensor_tensor_scan(place[0:NE, cols], ones, taken[0:NE, cols], 0.0, ALU.mult, ALU.add))
                linked(dve.tensor_tensor(place[0:NE, cols], place[0:NE, cols], taken[0:NE, cols], ALU.mult))
                at += len(tiles) * P
            dve.tensor_scalar(place[0:NE, :], place[0:NE, :], -1.0, None, ALU.add).then_inc(dve_done, 1)
            dve.wait_ge(back, 1)
            dve.tensor_copy(slotT[:, 0:nt, :], core.bank[3][:, 0:nt * NE].rearrange("p (t e) -> p t e", e=NE))

        @block.scalar
        def _(act):
            act.wait_ge(link, 2)
            act.activation(ex[:], ex[:], ACT.Exp).then_inc(exped, 1)


PAIR = 2
LOADS_E = 6


def expert_load(core, layer, expert, kind):
    h = kind // 2 if kind < 4 else kind - 4
    if kind < 4:
        w = core.dram["moe_w_up" if kind % 2 else "moe_w_gate"][layer][expert]
        return by_k(w, h * 512, (h + 1) * 512)
    return by_k(core.dram["moe_w_down"][layer][expert], 0, D, h * 512, (h + 1) * 512)


def moe(core, xn, X, sets, layer, slotT, gateT, out_gate, last_load):
    nc, ring = core.nc, core.ring
    cap_all = sum(c for _, _, c, _ in sets)
    nt = sum(len(t) for _, t, _, _ in sets)
    R = 2 * ring.slots
    per = PAIR * LOADS_E
    assert per % R == 0
    n0 = ring.index[f"moe{layer}_0_0"]
    scat = [(si, t) for si, (_, tiles, _, _) in enumerate(sets) for t in tiles]
    n_out = 2 * len(scat)
    PEM = [f"turn{si}" for si in range(len(sets))] + [f"gather{k}" for k in range(KT)]
    PEM += [f"scatter{n}" for n in range(n_out)]
    HAND = ["hid00", "slots", "picks", "weighted", "hid01", "y0", "hid10", "hid11", "y1"]
    HAND += [f"xs{k}" for k in range(KT)] + [f"x{n}" for n in range(n_out)]
    ACM = [f"turn{si}" for si in range(len(sets))] + [f"silu{e}{h}" for e in range(PAIR) for h in range(2)]
    with ExitStack() as own, core.stage("pe_done", "dve_done", "act_done", "slot_free") as (
            block, pe_done, dve_done, act_done, slot_free):
        pem, dvm, acm = Marks(pe_done, *PEM), Marks(dve_done, *HAND), Marks(act_done, *ACM)
        sl_now = core.sb(own, "slots_now", nt, PAIR)
        ga_now = core.sb(own, "gates_now", nt, PAIR)
        pick, weight, turned, back = [], [], [], []
        for si, (_, tiles, cap, _) in enumerate(sets):
            pick.append(core.sb(own, f"pick{si}", len(tiles), PAIR, cap))
            weight.append(core.sb(own, f"weight{si}", len(tiles), PAIR, cap))
            turned.append(core.sb(own, f"weight_turned{si}", len(tiles) * P))
            back.append(core.sb(own, f"y_gated{si}", D))
        xs = core.sb(own, "xs", KT, PAIR, cap_all)
        sl = core.sb(own, "moe_silu", 4, cap_all)
        hid = core.sb(own, "moe_hid", KT, cap_all)
        gu = [[core.bank[2 * h + n] for n in range(2)] for h in range(2)]
        yb = [core.bank[4], core.bank[5]]
        spare = [core.bank[6], core.bank[7]]
        gathered = spare + gu[0]

        def wait(engine, marks, step, name):
            engine.wait_ge(marks.sem, marks.at(step, name))

        def arrived(pe, i, j):
            pe.wait_ge(ring.arrived[ring.slot[n0 + j]], i * (16 * per // R) + 16 * ring.times[n0 + j])

        def done(engine, i, j):
            engine.wait_ge(ring.used, i * per + n0 + j + 1)

        def view(j, width):
            return ring.part(ring.slot[n0 + j], (P, SLOT // width, width))

        @block.sync
        def _(sp):
            assert ring.issued == n0 + R
            with sp.Fori(0, NE // PAIR - 1) as i:
                for j in range(per):
                    ahead = R + j
                    expert = i * PAIR + PAIR * (ahead // per) + (ahead % per) // LOADS_E
                    source = expert_load(core, layer, expert, ahead % LOADS_E)
                    sp.wait_ge(ring.used, i * per + n0 + j + 1)
                    sp.sem_inc(slot_free, 1)
                    slot = ring.slot[n0 + ahead]
                    sp.dma_start(ring.part(slot, source.shape), source).then_inc(ring.arrived[slot], 16)
            ring.issued += (NE // PAIR - 1) * per
            ring.feed(sp, last_load)

        @block.tensor
        def _(pe):
            def gather(step, banks_free):
                wait(pe, dvm, step, "picks")
                for k in range(KT):
                    b = gathered[k % 4]
                    if k >= 4:
                        wait(pe, dvm, step, f"xs{k - 4}")
                    elif k == 0 or k == 2:
                        banks_free(k)
                    out = b[:, 0:PAIR * cap_all].rearrange("p (e c) -> p e c", e=PAIR)
                    for si, (_, tiles, cap, first) in enumerate(sets):
                        for n, t in enumerate(tiles):
                            last = pe.matmul(out[:, :, first:first + cap], xn[:, t, k * P:(k + 1) * P],
                                             pick[si][:, n, :, :], start=(n == 0), stop=(n == len(tiles) - 1))
                    last.then_inc(pe_done, 1)

            pe.sem_inc(pe_done, len(sets))
            gather(0, lambda k: None)
            pe.wait_ge(pe_done, pem.at(0, f"gather{KT - 1}"))
            pe.sem_inc(pe_done, n_out)
            with pe.Fori(0, NE // PAIR) as i:
                step = i + 1
                wait(pe, dvm, i, "weighted")
                wait(pe, dvm, i, f"xs{KT - 1}")
                for si, (_, tiles, cap, _) in enumerate(sets):
                    for n, t in enumerate(tiles):
                        last = pe.transpose(spare[si][0:PAIR * cap, n * P:(n + 1) * P],
                                            weight[si][:, n, :, :].rearrange("p e c -> p (e c)"), core.ident[:])
                    last.then_inc(pe_done, 1)
                for e in range(PAIR):
                    for h in range(2):
                        for n in range(2):
                            j = e * LOADS_E + 2 * h + n
                            arrived(pe, i, j)
                            if n == 0:
                                if e:
                                    wait(pe, dvm, step, f"hid0{h}")
                                elif h:
                                    wait(pe, dvm, i, f"x{n_out - 1}")
                            w = view(j, 512)
                            for c in range(4):
                                for k in range(KT):
                                    last = pe.matmul(gu[h][n][:, c * cap_all:(c + 1) * cap_all],
                                                     w[:, k, c * P:(c + 1) * P], xs[:, k, e, :],
                                                     start=(k == 0), stop=(k == KT - 1))
                            last.then_inc(ring.used, 1)
                    wait(pe, dvm, step, f"y{e - 1}") if e else wait(pe, dvm, i, f"y{PAIR - 1}")
                    for h in range(2):
                        j = e * LOADS_E + 4 + h
                        arrived(pe, i, j)
                        wait(pe, dvm, step, f"hid{e}{h}")
                        w = view(j, D)
                        for n in range(2):
                            for q in range(4):
                                last = pe.matmul(yb[n][0:cap_all, :], hid[:, 4 * h + q, :],
                                                 w[:, q, n * 512:(n + 1) * 512], start=(h == 0 and q == 0),
                                                 stop=(h == 1 and q == 3), skip_group_check=True)
                        last.then_inc(ring.used, 1)

                def banks_free(k):
                    if k == 2:
                        wait(pe, dvm, step, "hid10")
                    else:
                        for other in range(len(sets)):
                            wait(pe, acm, step, f"turn{other}")

                gather(step, banks_free)
                wait(pe, dvm, step, "y1")
                for n, (si, t) in enumerate(scat):
                    tiles, cap = sets[si][1], sets[si][2]
                    m = tiles.index(t)
                    for h in range(2):
                        if 2 * n + h >= 2:
                            wait(pe, dvm, step, f"x{2 * n + h - 2}")
                        pe.matmul(gu[1][h][:], turned[si][0:PAIR * cap, m * P:(m + 1) * P],
                                  back[si][0:PAIR * cap, h * 512:(h + 1) * 512], start=True,
                                  stop=True).then_inc(pe_done, 1)

        @block.scalar
        def _(act):
            acm.skip_step(act)
            with act.Fori(0, NE // PAIR) as i:
                step = i + 1
                for si, (_, tiles, cap, _) in enumerate(sets):
                    wait(act, pem, step, f"turn{si}")
                    act.activation(turned[si][0:PAIR * cap, :], spare[si][0:PAIR * cap, 0:len(tiles) * P],
                                   ACT.Copy).then_inc(act_done, 1)
                for e in range(PAIR):
                    for h in range(2):
                        done(act, i, e * LOADS_E + 2 * h)
                        if e == 0 and h == 0:
                            wait(act, dvm, i, "hid11")
                        else:
                            wait(act, dvm, step, f"hid{(2 * e + h - 1) // 2}{(2 * e + h - 1) % 2}")
                        act.activation(sl[:].rearrange("p c n -> p (c n)"), gu[h][0][:, 0:4 * cap_all],
                                       ACT.Silu).then_inc(act_done, 1)

        @block.vector
        def _(dve):
            def picks(pair, now, before):
                if before is not None:
                    wait(dve, pem, before, f"turn{len(sets) - 1}")
                dve.tensor_copy(ga_now[:], gateT[:, 0:nt, bass.ds(pair * PAIR, PAIR)])
                dve.tensor_copy(sl_now[:], slotT[:, 0:nt, bass.ds(pair * PAIR, PAIR)]).then_inc(dve_done, 1)
                wait(dve, dvm, now, "slots")
                for weighted in (False, True):
                    for si, (_, tiles, cap, _) in enumerate(sets):
                        for n, t in enumerate(tiles):
                            for e in range(PAIR):
                                s, g = sl_now[:, t, e:e + 1], ga_now[:, t, e:e + 1]
                                target = (weight if weighted else pick)[si][:, n, e, :]
                                if weighted:
                                    last = dve.tensor_scalar(target, core.iota[:, 0:cap], s, g, ALU.is_equal, ALU.mult)
                                else:
                                    last = dve.tensor_scalar(target, core.iota[:, 0:cap], s, None, ALU.is_equal)
                    last.then_inc(dve_done, 1)

            def tokens(step):
                for k in range(KT):
                    wait(dve, pem, step, f"gather{k}")
                    got = gathered[k % 4][:, 0:PAIR * cap_all].rearrange("p (e c) -> p e c", e=PAIR)
                    for which, _, cap, first in sets:
                        last = dve.tensor_scalar(xs[:, k, :, first:first + cap], got[:, :, first:first + cap],
                                                 core.factor[:, 1, k, which:which + 1],
                                                 core.mod[:, 3 * KT + k, which:which + 1], ALU.mult, ALU.add)
                    last.then_inc(dve_done, 1)

            dve.sem_inc(dve_done, HAND.index("slots"))
            picks(0, 0, None)
            dve.wait_ge(dve_done, dvm.at(0, "weighted"))
            dve.sem_inc(dve_done, HAND.index("xs0") - HAND.index("weighted") - 1)
            tokens(0)
            dve.wait_ge(dve_done, dvm.at(0, f"xs{KT - 1}"))
            dve.sem_inc(dve_done, n_out)
            with dve.Fori(0, NE // PAIR) as i:
                step = i + 1
                for e in range(PAIR):
                    for h in range(2):
                        done(dve, i, e * LOADS_E + 2 * h + 1)
                        wait(dve, acm, step, f"silu{e}{h}")
                        if h == 0:
                            done(dve, i, e * LOADS_E - 1)
                        dve.tensor_tensor(hid[:, 4 * h:4 * h + 4, :].rearrange("p c n -> p (c n)"),
                                          sl[:].rearrange("p c n -> p (c n)"), gu[h][1][:, 0:4 * cap_all],
                                          ALU.mult).then_inc(dve_done, 1)
                        if e == 0 and h == 0:
                            picks(i + 1, step, step)
                    done(dve, i, e * LOADS_E + 5)
                    if e == 0:
                        wait(dve, pem, i, f"scatter{2 * len(scat) - 1}")
                    for si, (which, _, cap, first) in enumerate(sets):
                        for n in range(2):
                            last = dve.tensor_tensor(back[si][e * cap:(e + 1) * cap, n * 512:(n + 1) * 512],
                                                     yb[n][first:first + cap, :],
                                                     out_gate[first:first + cap, which, n * 512:(n + 1) * 512],
                                                     ALU.mult)
                    last.then_inc(dve_done, 1)
                tokens(step)
                for n, (si, t) in enumerate(scat):
                    for h in range(2):
                        wait(dve, pem, step, f"scatter{2 * n + h}")
                        cols = slice(h * 512, (h + 1) * 512)
                        dve.tensor_tensor(X[:, t, cols], X[:, t, cols], gu[1][h][:], ALU.add).then_inc(dve_done, 1)



HG = SG // 2


def ssd_scan(core, BT, CT, XS, Y, dec, g0, last_load):
    PE_BACK, DVE_BACK = ["bturn", "state"], ["te", "fade", "state"]
    PE_FRONT, ACT_FRONT, DVE_FRONT, POOL_FRONT = ["rows", "cb"], ["gap", "decay", "rowexp"], ["cbm", "w"], ["cs", "xd"]
    with ExitStack() as own, core.stage(
            "pe_front_f", "pe_front_b", "pe_y_f", "pe_y_b", "pe_back_f", "pe_back_b", "act_front_f", "act_front_b",
            "act_bk_f", "act_bk_b", "dve_front_f", "dve_front_b", "dve_out_f", "dve_out_b", "dve_back_f",
            "dve_back_b", "pool_f", "pool_b", "cleared") as (
            block, pe_front_f, pe_front_b, pe_y_f, pe_y_b, pe_back_f, pe_back_b, act_front_f, act_front_b,
            act_bk_f, act_bk_b, dve_front_f, dve_front_b, dve_out_f, dve_out_b, dve_back_f,
            dve_back_b, pool_f, pool_b, cleared):
        pef = [Marks(x, *PE_FRONT) for x in (pe_front_f, pe_front_b)]
        pey = [Marks(x, "y") for x in (pe_y_f, pe_y_b)]
        peb = [Marks(x, *PE_BACK) for x in (pe_back_f, pe_back_b)]
        acf = [Marks(x, *ACT_FRONT) for x in (act_front_f, act_front_b)]
        acb = [Marks(x, "bk") for x in (act_bk_f, act_bk_b)]
        dvf = [Marks(x, *DVE_FRONT) for x in (dve_front_f, dve_front_b)]
        dvo = [Marks(x, "out") for x in (dve_out_f, dve_out_b)]
        dvb = [Marks(x, *DVE_BACK) for x in (dve_back_f, dve_back_b)]
        pof = [Marks(x, *POOL_FRONT) for x in (pool_f, pool_b)]
        G = core.sb(own, "s_gap", 2, SR, P)
        E = core.sb(own, "s_decay", 2, 2, SR, P)
        CS = core.sb(own, "s_cs", 2, 2, SR, P)
        CB = core.sb(own, "s_cb", 2, P)
        BK = core.sb(own, "s_bk", 2, P)
        XD = core.sb(own, "s_xd", 2, 2, SR, SP_)
        TE = core.sb(own, "s_te", 2, SR, SP_)
        H = core.sb(own, "s_state", 2, HG, SR, SP_)
        bank = [[core.bank[4 * d + i] for i in range(4)] for d in (FWD, BWD)]
        units = [(s, g) for s in range(TT) for g in range(HG)]
        first = TC * HG

        def wait(engine, marks, u, name):
            engine.wait_ge(marks.sem, marks.at(u, name))

        def place(u, d):
            s, g = units[u]
            t = ORDER[d][s]
            return t, g, slice(chunk_cols(t), chunk_cols(t) + P)

        def wide(x, d, t, g, n):
            return x[:, t, d, SR * (g0 + g):SR * (g0 + g + 1)].unsqueeze(2).to_broadcast([P, SR, n])

        def head(x, d, t, g, r):
            at = SR * (g0 + g) + r
            return x[:, t, d, at:at + 1]

        def over_heads(m):
            return m.unsqueeze(1).to_broadcast([P, SR, P])

        def four(b):
            return b[:].rearrange("p (r c) -> p r c", c=P)

        def heads64(b):
            return b[:, 0:SR * SP_].rearrange("p (r c) -> p r c", c=SP_)

        @block.sync
        def _(sp):
            core.ring.feed(sp, last_load)

        @block.tensor
        def _(pe):
            def front(u):
                f = u - first
                for d in (FWD, BWD):
                    t, g, cols = place(u, d)
                    if f:
                        wait(pe, acf[d], f - 1, "rowexp")
                    for r in range(SR):
                        last = pe.matmul(four(bank[d][0])[:, r, :], head(dec.g, d, t, g, r).to_broadcast([P, P]),
                                         core.tri[:, d, :], start=True, stop=True)
                    last.then_inc(pef[d].sem, 1)
                for d in (FWD, BWD):
                    t, g, cols = place(u, d)
                    wait(pe, acb[d], u - 1, "bk")
                    pe.matmul(bank[d][1][:, 0:P], BT[:, g, cols], CT[:, g, cols], start=True,
                              stop=True).then_inc(pef[d].sem, 1)

            for u, (s, g) in enumerate(units):
                f = u - first
                for d in (FWD, BWD):
                    _, _, cols = place(u, d)
                    if f >= 0:
                        wait(pe, dvf[d], f, "cbm")
                    elif u:
                        wait(pe, acb[d], u - 1, "bk")
                    pe.transpose(bank[d][1][:, 0:P], BT[:, g, cols], core.ident[:]).then_inc(peb[d].sem, 1)
                if first <= u + 1 < len(units):
                    front(u + 1)
                for d in (FWD, BWD):
                    if f >= 0:
                        wait(pe, pof[d], f, "xd")
                        wait(pe, dvf[d], f, "w")
                        wait(pe, dvb[d], u - HG, "state")
                        if f:
                            wait(pe, dvo[d], f - 1, "out")
                        for r in range(SR):
                            out = bank[d][2][:, r * SP_:(r + 1) * SP_]
                            pe.matmul(out, CS[:, d, f % 2, r, :], H[:, d, g, r, :], start=True, stop=False)
                            last = pe.matmul(out, E[:, d, f % 2, r, :], XD[:, d, f % 2, r, :], start=False, stop=True)
                        last.then_inc(pey[d].sem, 1)
                for d in (FWD, BWD):
                    wait(pe, acb[d], u, "bk")
                    wait(pe, dvb[d], u, "te")
                    if u:
                        wait(pe, dvb[d], u - 1, "state")
                    pe.matmul(bank[d][3][:, 0:SR * SP_], BK[:, d, :], TE[:, d].rearrange("p r c -> p (r c)"),
                              start=True, stop=True).then_inc(peb[d].sem, 1)

        @block.scalar
        def _(act):
            for u in range(len(units)):
                for d in (FWD, BWD):
                    wait(act, peb[d], u, "bturn")
                    if u:
                        wait(act, peb[d], u - 1, "state")
                    act.activation(BK[:, d, :], bank[d][1][:, 0:P], ACT.Copy).then_inc(acb[d].sem, 1)
                f = u + 1 - first
                if f < 0 or u + 1 == len(units):
                    continue
                for d in (FWD, BWD):
                    t, g, _ = place(u + 1, d)
                    wait(act, pef[d], f, "rows")
                    for r in range(SR):
                        last = act.activation(G[:, d, r, :], four(bank[d][0])[:, r, :], ACT.Abs, scale=-1.0,
                                              bias=head(dec.cum, d, t, g, r))
                    last.then_inc(acf[d].sem, 1)
                    wait(act, acf[d], f, "gap")
                    if f >= 2:
                        wait(act, pey[d], f - 2, "y")
                    act.activation(E[:, d, f % 2], G[:, d], ACT.Exp, scale=-1.0).then_inc(acf[d].sem, 1)
                    act.activation(CS[:, d, f % 2], four(bank[d][0]), ACT.Exp).then_inc(acf[d].sem, 1)

        @block.gpsimd
        def _(pool):
            for f in range(len(units) - first):
                for d in (FWD, BWD):
                    t, g, cols = place(first + f, d)
                    wait(pool, acf[d], f, "rowexp")
                    pool.tensor_tensor(CS[:, d, f % 2], CS[:, d, f % 2], over_heads(CT[:, g, cols]),
                                       ALU.mult).then_inc(pof[d].sem, 1)
                    if f >= 2:
                        wait(pool, pey[d], f - 2, "y")
                    pool.tensor_tensor(XD[:, d, f % 2], XS[:, t, SR * g:SR * (g + 1), :],
                                       wide(dec.step, d, t, g, SP_), ALU.mult).then_inc(pof[d].sem, 1)

        @block.vector
        def _(dve):
            dve.memset(H[:], 0.0).then_inc(cleared, 1)
            dve.wait_ge(cleared, 1)
            for u, (s, g) in enumerate(units):
                for d in (FWD, BWD):
                    t, _, _ = place(u, d)
                    if u:
                        wait(dve, peb[d], u - 1, "state")
                    dve.tensor_tensor(TE[:, d], XS[:, t, SR * g:SR * (g + 1), :], wide(dec.to_end, d, t, g, SP_),
                                      ALU.mult).then_inc(dvb[d].sem, 1)
                f = u + 1 - first
                if f >= 0 and u + 1 < len(units):
                    for d in (FWD, BWD):
                        wait(dve, pef[d], f, "cb")
                        dve.tensor_tensor(CB[:, d, :], bank[d][1][:, 0:P], core.tri[:, d, :],
                                          ALU.mult).then_inc(dvf[d].sem, 1)
                        wait(dve, dvf[d], f, "cbm")
                        wait(dve, acf[d], f, "decay")
                        dve.tensor_tensor(E[:, d, f % 2], E[:, d, f % 2], over_heads(CB[:, d, :]), ALU.mult) \
                            .then_inc(dvf[d].sem, 1)
                f = u - first
                for d in (FWD, BWD):
                    t, _, _ = place(u, d)
                    if f >= 0:
                        wait(dve, pey[d], f, "y")
                        other = ORDER[1 - d].index(t)
                        y = Y[:, t - TC, SR * g:SR * (g + 1), :]
                        if s < other:
                            dve.tensor_copy(y, heads64(bank[d][2])).then_inc(dvo[d].sem, 1)
                        else:
                            wait(dve, dvo[1 - d], (other - TC) * HG + g, "out")
                            dve.tensor_tensor(y, y, heads64(bank[d][2]), ALU.add).then_inc(dvo[d].sem, 1)
                    if s:
                        wait(dve, dvb[d], u - HG, "state")
                    dve.tensor_tensor(H[:, d, g], H[:, d, g], wide(dec.whole, d, t, g, SP_), ALU.mult) \
                        .then_inc(dvb[d].sem, 1)
                    wait(dve, dvb[d], u, "fade")
                    wait(dve, peb[d], u, "state")
                    dve.tensor_tensor(H[:, d, g], H[:, d, g], heads64(bank[d][3]), ALU.add) \
                        .then_inc(dvb[d].sem, 1)


def vector_ops(core, ops, last_load=None):
    with core.stage("link") as (block, link):
        @block.sync
        def _(sp):
            if last_load is not None:
                core.ring.feed(sp, last_load)

        @block.vector
        def _(dve):
            for n, op in enumerate(ops):
                if n:
                    dve.wait_ge(link, n)
                op(dve).then_inc(link, 1)


def turn_all(core, src, dst, factor, KK, runs, last_load):
    with core.stage("turned", "moved") as (block, turned, moved):
        @block.sync
        def _(sp):
            core.ring.feed(sp, last_load)

        @block.tensor
        def _(pe):
            n = 0
            for k in range(KK):
                for run in runs:
                    if n >= 8:
                        pe.wait_ge(moved, n - 7)
                    for j, t in enumerate(run):
                        last = pe.transpose(core.bank[n % 8][:, j * P:(j + 1) * P], src(k, t), core.ident[:])
                    last.then_inc(turned, 1)
                    n += 1

        @block.vector
        def _(dve):
            n = 0
            for k in range(KK):
                for run in runs:
                    dve.wait_ge(turned, n + 1)
                    dve.tensor_scalar(dst(k, run), core.bank[n % 8][:, 0:len(run) * P], factor(k), None,
                                      ALU.mult).then_inc(moved, 1)
                    n += 1


def rms_rows(core, src, junk, inv, tiles, width):
    with ExitStack() as own, core.stage("squared", "scaled", "rooted") as (block, squared, scaled, rooted):
        ss = core.sb(own, "sum_squares", tiles)

        @block.scalar
        def _(act):
            for t in range(tiles):
                if t:
                    act.wait_ge(squared, t)
                act.activation(junk, src(t), ACT.Square, accum_out=ss[:, t:t + 1]).then_inc(squared, 1)
            act.wait_ge(scaled, 1)
            act.activation(ss[:], ss[:], ACT.Sqrt).then_inc(rooted, 1)

        @block.vector
        def _(dve):
            dve.wait_ge(squared, tiles)
            dve.tensor_scalar(ss[:], ss[:], 1.0 / width, EPS, ALU.mult, ALU.add).then_inc(scaled, 1)
            dve.wait_ge(rooted, 1)
            dve.reciprocal(inv, ss[:])


def head_norm(core, O, Z):
    with ExitStack() as own, core.stage("link", "rooted") as (block, link, rooted):
        sq = core.sb(own, "head_squares", TT * GH, GK)
        ss = core.sb(own, "head_sums", TT * GH)
        rows = O.rearrange("p t h c -> p (t h) c")

        @block.vector
        def _(dve):
            dve.tensor_tensor(sq[:], rows, rows, ALU.mult).then_inc(link, 1)
            dve.wait_ge(link, 1)
            dve.tensor_reduce(ss[:], sq[:], AX.X, ALU.add).then_inc(link, 1)
            dve.wait_ge(link, 2)
            dve.tensor_scalar(ss[:], ss[:], 1.0 / GK, EPS, ALU.mult, ALU.add).then_inc(link, 1)
            dve.wait_ge(rooted, 1)
            dve.reciprocal(ss[:], ss[:]).then_inc(link, 1)
            dve.wait_ge(link, 4)
            dve.tensor_tensor(rows, rows, ss[:].unsqueeze(2).to_broadcast([P, TT * GH, GK]), ALU.mult) \
                .then_inc(link, 1)
            dve.wait_ge(link, 5)
            dve.tensor_tensor(rows, rows, Z.rearrange("p t (h c) -> p (t h) c", c=GK), ALU.mult)

        @block.scalar
        def _(act):
            act.wait_ge(link, 3)
            act.activation(ss[:], ss[:], ACT.Sqrt).then_inc(rooted, 1)


def store(core, target, source):
    with core.stage("stored") as (block, stored):
        @block.sync
        def _(sp):
            sp.dma_start(target, source).then_inc(stored, 16)
            sp.wait_ge(stored, 16)




def by_k(w, a, b, r0=0, r1=None):
    r1 = w.shape[0] if r1 is None else r1
    return w[r0:r1, a:b].rearrange("(k p) n -> p k n", p=P)


def plan(core):
    ring, dram = core.ring, core.dram

    def columns_of(name, w, count, first=0, width=512):
        for j in range(count):
            a = first + j * width
            ring.plan(f"{name}{j}", by_k(w, a, min(a + width, w.shape[1])))

    def row_groups(name, w, step):
        for j in range(w.shape[1] // 512):
            for n, r in enumerate(range(0, w.shape[0], step)):
                ring.plan(f"{name}{j}_{n}", by_k(w, j * 512, (j + 1) * 512, r, min(r + step, w.shape[0])))

    def experts(layer):
        ring.plan(f"router{layer}", by_k(dram["router_w"][layer], 0, NE))
        for e in range(NE):
            for kind in range(LOADS_E):
                ring.plan(f"moe{layer}_{e}_{kind}", expert_load(core, layer, e, kind), wide=True)

    def swiglu(layer):
        for j in range(-(-DFF // 512)):
            for part in ("gate", "up"):
                w = dram[f"ffn_w_{part}_2"][layer]
                ring.plan(f"ffn{layer}_{part}{j}", by_k(w, j * 512, min((j + 1) * 512, DFF)))
        row_groups(f"ffn{layer}_down", dram["ffn_w_down_2"][layer], D)

    columns_of("ada0_", dram["ada_w"][0], 12)
    w = dram["gdn_w_in"][0]
    gdn = GH * GK
    ring.plan("gdn_gates", by_k(w, 4 * gdn, 4 * gdn + 4 * GH))
    for half in range(2):
        for n, part in enumerate("qkv"):
            ring.plan(f"gdn_{part}{half}", by_k(w, n * gdn + half * 512, n * gdn + half * 512 + 512))
    columns_of("gdn_z", w, 2, 3 * gdn)
    columns_of("gdn_out", dram["gdn_w_out"][0], 2)
    experts(0)
    columns_of("ada1_", dram["ada_w"][1], 12)
    w = dram["ssd_w_in"][0]
    sn = SG * SN
    ring.plan("ssd_dt", by_k(w, 2 * SI + 2 * sn, 2 * SI + 2 * sn + 2 * SH))
    for half in range(2):
        columns_of(f"ssd_x{half}_", w, 2, SI + half * (SI // 2))
        ring.plan(f"ssd_b{half}", by_k(w, 2 * SI + half * 512, 2 * SI + half * 512 + 512))
        ring.plan(f"ssd_c{half}", by_k(w, 2 * SI + sn + half * 512, 2 * SI + sn + half * 512 + 512))
    columns_of("ssd_z", w, SI // 512)
    row_groups("ssd_out", dram["ssd_w_out"][0], D)
    experts(1)
    w = dram["ev_w_in_2"][0]
    fw = FH * FD
    ring.plan("ev_q", by_k(w, 0, fw))
    ring.plan("ev_k", by_k(w, fw, 2 * fw))
    ring.plan("ev_u", by_k(w, 3 * fw + FH, w.shape[1]))
    ring.plan("ev_v", by_k(w, 2 * fw, 3 * fw))
    ring.plan("ev_f", by_k(w, 3 * fw, 3 * fw + FH))
    ring.plan("ev_pool", dram["ev_pool_w_2"][0].rearrange("g d e -> d g e"))
    columns_of("ev_out", dram["ev_w_out_2"][0], 2)
    swiglu(0)
    columns_of("od_in", dram["od_w_in_2"][0], 4)
    for n, part in (("od_a", "od_w_a_2"), ("od_x", "od_w_x_2")):
        ring.plan(n, by_k(dram[part][0].rearrange("h d e -> (h d) e"), 0, LD))
    columns_of("od_out", dram["od_w_out_2"][0], 2)
    swiglu(1)


def tile_cols(t, first=0):
    return slice((t - first) * P, (t - first + 1) * P)


def first_norm(core, own, source, last_load):
    hT = core.sb(own, "hT", KT, T)
    with ExitStack() as inner:
        X = core.sb(inner, "X", TT, D)
        xn = core.sb(inner, "xn", TT, D)
        load_x(core, X[:], source)
        norm_turn(core, X, hT, list(range(TT)), lambda k, t: core.factor[:, 0, k, int(t < TC)].unsqueeze(1),
                  lambda k, t: core.mod[:, k, int(t < TC)].unsqueeze(1), xn, last_load)
    return hT


def gdn_layer(core):
    with ExitStack() as own:
        hT = first_norm(core, own, None, "ada0_11")
        O = core.sb(own, "gdn_o", TT, GH, GK)
        with ExitStack() as scans:
            dec = Decays(core, scans, "gdn", GH)
            dec.beta = core.sb(scans, "gdn_beta", TT, 2, GH)
            decays(core, hT, "gdn_gates", GH, core.head["gdn_dt_bias"], core.head["gdn_a_log"], dec, True,
                   "gdn_gates")
            taps, tiles = core.col0["gdn_conv_w"], 3 * GH
            for half in range(2):
                h0 = half * GQ
                with ExitStack() as scan:
                    qT = core.sb(scan, "qT", GQ, CV)
                    kT = core.sb(scan, "kT", GQ, CV)
                    V = core.sb(scan, "V", TT, GQ, P)
                    jobs = []
                    for n, (part, kind) in enumerate((("q", "unit"), ("k", "unit"), ("v", "turn"))):
                        for h in range(GQ):
                            target = ((qT[:, h, :], GK ** -0.5), (kT[:, h, :], 1.0), V[:, :, h, :])[n]
                            jobs.append((f"gdn_{part}{half}", h, n * GH + h0 + h, kind, target))
                    conv_project(core, hT, jobs,
                                 lambda w, ch: core.cols[:, taps + w * tiles + ch:taps + w * tiles + ch + 1],
                                 None, f"gdn_v{half}")
                    delta_scan(core, qT, kT, V, O[:, :, h0:h0 + GQ, :], dec, h0, f"gdn_v{half}")
        Z = core.sb(own, "gdn_z", TT, D)
        gemm_tokens(core, lambda k, t: hT[:, k, tile_cols(t)], [[(f"gdn_z{j}", range(KT))] for j in range(2)],
                    range(TT), lambda act, linked, j, t, bank: act.activation(
                        Z[:, t, j * 512:(j + 1) * 512], bank[:], ACT.Silu), "gdn_z1", on_scalar=True)
        head_norm(core, O[:], Z[:])
        oT = hT
        runs = [range(0, TC), range(TC, TT)]
        turn_all(core, lambda k, t: O[:, t, k, :], lambda k, run: oT[:, k, run[0] * P:(run[-1] + 1) * P],
                 lambda k: columns(core, "gdn_norm_g", 0, 1), GH, runs, "gdn_z1")
        X = core.sb(own, "X", TT, D)
        gate = core.sb(own, "gate", 2, D)
        tmp = core.sb(own, "gated", 512)
        gate_rows(core, gate, 2, beside=input_parts(core, X[:]))
        gemm_tokens(core, lambda k, t: oT[:, k, tile_cols(t)], [[(f"gdn_out{j}", range(KT))] for j in range(2)],
                    range(TT), add_gated(lambda t: X[:, t, :], gate, tmp), "gdn_out1")
        store(core, core.x_dram, X[:])


def ssd_layer(core):
    with ExitStack() as own:
        hT = first_norm(core, own, core.x_dram, "ada1_11")
        Y = core.sb(own, "ssd_y", TX, SH, SP_)
        with ExitStack() as scans:
            dec = Decays(core, scans, "ssd", SH)
            decays(core, hT, "ssd_dt", SH, core.head["ssd_dt_bias"], core.head["ssd_a_log"], dec, False, "ssd_dt")
            vector_ops(core, [lambda dve: dve.tensor_tensor(dec.to_end[:], dec.to_end[:], dec.step[:], ALU.mult)])
            taps, tiles = core.col0["ssd_conv_w"], (SI + 2 * SG * SN) // P
            for half in range(2):
                with ExitStack() as scan:
                    XS = core.sb(scan, "ssd_xs", TT, SH // 2, SP_)
                    BT = core.sb(scan, "ssd_bT", HG, CV)
                    CT = core.sb(scan, "ssd_cT", HG, CV)
                    xs = XS[:].rearrange("p t h c -> p t (h c)")
                    jobs = [(f"ssd_x{half}_{c // 4}", c % 4, half * 8 + c, "turn", xs[:, :, c * P:(c + 1) * P])
                            for c in range(8)]
                    for n, (part, target) in enumerate((("b", BT), ("c", CT))):
                        jobs += [(f"ssd_{part}{half}", c, SI // P + n * SG + half * HG + c, "plain", target[:, c, :])
                                 for c in range(HG)]
                    conv_project(core, hT, jobs,
                                 lambda w, ch: core.cols[:, taps + w * tiles + ch:taps + w * tiles + ch + 1],
                                 lambda ch: core.cols[:, core.col0["ssd_conv_b"] + ch:core.col0["ssd_conv_b"] + ch + 1],
                                 f"ssd_c{half}")
                    mine = Y[:, :, half * (SH // 2):(half + 1) * (SH // 2), :]
                    ssd_scan(core, BT, CT, XS, mine, dec, half * HG, f"ssd_c{half}")
                    skip = core.head["ssd_d"][:, half * (SH // 2):(half + 1) * (SH // 2)].unsqueeze(2) \
                        .to_broadcast([P, SH // 2, SP_])
                    ops = []
                    for t in range(TX):
                        x = XS[:, TC + t]
                        ops.append(lambda dve, x=x: dve.tensor_tensor(x, x, skip, ALU.mult))
                        ops.append(lambda dve, x=x, t=t: dve.tensor_tensor(mine[:, t], mine[:, t], x, ALU.add))
                    vector_ops(core, ops)
        y = Y[:].rearrange("p t h c -> p t (h c)")
        with ExitStack() as gated:
            Z = core.sb(gated, "ssd_z", TX, SI)
            gemm_tokens(core, lambda k, t: hT[:, k, tile_cols(t)],
                        [[(f"ssd_z{j}", range(KT))] for j in range(SI // 512)], range(TC, TT),
                        lambda act, linked, j, t, bank: act.activation(
                            Z[:, t - TC, j * 512:(j + 1) * 512], bank[:], ACT.Silu), "ssd_z3", on_scalar=True)
            inv = core.sb(gated, "ssd_inv", TX)
            vector_ops(core, [lambda dve: dve.tensor_tensor(y, y, Z[:], ALU.mult)])
            rms_rows(core, lambda t: y[:, t, :], Z[:, 0, :], inv[:], TX, SI)
            vector_ops(core, [lambda dve, t=t: dve.tensor_scalar(y[:, t, :], y[:, t, :], inv[:, t:t + 1], None,
                                                                 ALU.mult) for t in range(TX)])
        yT = core.sb(own, "ssd_yT", SI // P, NX)
        turn_all(core, lambda k, t: y[:, t, k * P:(k + 1) * P], lambda k, run: yT[:, k, :],
                 lambda k: columns(core, "ssd_norm_g", 0, SI // P)[:, k:k + 1], SI // P, [range(TX)], "ssd_z3")
        X = core.sb(own, "X", TX, D)
        gate = core.sb(own, "gate", 2, D)
        tmp = core.sb(own, "gated", 512)
        gate_rows(core, gate, 2, beside=[(X[:], core.x_dram[:, TC:TT, :])])
        groups = [[(f"ssd_out{j}_{n}", range(n * KT, (n + 1) * KT)) for n in range(SI // D)] for j in range(2)]
        gemm_tokens(core, lambda k, t: yT[:, k, tile_cols(t, TC)], groups, range(TC, TT),
                    add_gated(lambda t: X[:, t - TC, :], gate, tmp), "ssd_out1_1")
        store(core, core.x_dram[:, TC:TT, :], X[:])


def moe_layer(core, layer, X, tiles):
    nt = len(tiles)
    split = [(0, [i for i, t in enumerate(tiles) if t >= TC], CAPX, 0)]
    if nt == TT:
        split.append((1, [i for i, t in enumerate(tiles) if t < TC], CAPC, CAPX))
    before = "gdn_out1" if layer == 0 else "ssd_out1_1"
    with ExitStack() as own:
        xn = core.sb(own, "xn", nt, D)
        slotT = core.sb(own, "slots", nt, NE + PAIR)
        gateT = core.sb(own, "affinities", nt, NE + PAIR)
        with ExitStack() as routing:
            hT = core.sb(routing, "hT", KT, nt * P)
            vector_ops(core, [lambda dve: dve.memset(slotT[:], -1.0), lambda dve: dve.memset(gateT[:], 0.0)])
            norm_turn(core, X, hT, tiles, lambda k, t: core.factor[:, 1, k, int(t < TC)].unsqueeze(1),
                      lambda k, t: core.mod[:, 3 * KT + k, int(t < TC)].unsqueeze(1), xn, before)
            order = [s for s in reversed(split)]
            route(core, hT, [(s[1], s[2]) for s in order], layer, slotT[:, :, 0:NE], gateT[:, :, 0:NE],
                  f"router{layer}")
        gate = core.sb(own, "gate", 2, D)
        core.ring.extra = core.sb(own, "weight_ring_extra", core.ring.slots, SLOT)
        gate_rows(core, gate, 5, f"router{layer}")
        moe(core, xn, X, split, layer, slotT, gateT, gate, f"moe{layer}_{NE - 1}_{LOADS_E - 1}")
        core.ring.extra = None


def plain_norm(core, X, hT, xn, name, layer, last_load):
    norm_turn(core, X, hT, list(range(TC, TT)), lambda k, t: columns(core, name, layer)[:, k:k + 1], None, xn,
              last_load)


def swiglu_layer(core, X, layer, before):
    with ExitStack() as own:
        hT = core.sb(own, "hT", KT, NX)
        M = core.sb(own, "mixed", TX, D)
        plain_norm(core, X, hT, M, "ffn_pre_g_2", layer, before)
        hid = core.sb(own, "hidden", DFF // P, NX)
        n = -(-DFF // 512)
        loads = [(f"ffn{layer}_gate{j}", f"ffn{layer}_up{j}", 4 * j, min(4, DFF // P - 4 * j)) for j in range(n)]
        swiglu_up(core, hT, hid, loads, f"ffn{layer}_up{n - 1}")
        steps = -(-DFF // D)
        groups = [[(f"ffn{layer}_down{j}_{r}", range(r * KT, min((r + 1) * KT, DFF // P))) for r in range(steps)]
                  for j in range(2)]
        gemm_tokens(core, lambda k, t: hid[:, k, tile_cols(t)], groups, range(TX),
                    lambda dve, linked, j, t, bank: dve.tensor_copy(M[:, t, j * 512:(j + 1) * 512], bank[:]),
                    f"ffn{layer}_down1_{steps - 1}")
        add_normed(core, X, M, core.dram["ffn_post_g_2"][layer])


def even_layer(core, X):
    with ExitStack() as own:
        hT = core.sb(own, "hT", KT, NX)
        M = core.sb(own, "mixed", TX, D)
        plain_norm(core, X, hT, M, "mix_pre_g_2", 0, f"moe1_{NE - 1}_{LOADS_E - 1}")
        catT = core.sb(own, "mixedT", KT, NX)
        with ExitStack() as inner:
            QT = core.sb(inner, "qT", 4, NX)
            KTt = core.sb(inner, "kT", 4, NX)
            U = core.sb(inner, "u", len(WINDOWS), WINDOWS[-1] + NX)
            V = core.sb(inner, "v", TX, FH * FD)
            nlf = core.sb(inner, "neg_log_f", TX, FH)
            vector_ops(core, [lambda dve: dve.memset(U[:, :, 0:WINDOWS[-1]], 0.0)])
            jobs = [("ev_q", c, QT[:, c, :], ACT.Copy) for c in range(4)]
            jobs += [("ev_k", c, KTt[:, c, :], ACT.Copy) for c in range(4)]
            jobs += [("ev_u", c, U[:, c, WINDOWS[-1]:], ACT.Copy) for c in range(4)]
            project_channels(core, hT, jobs, "ev_u")
            gemm_tokens(core, lambda k, t: hT[:, k, tile_cols(t)], [[("ev_v", range(KT))]], range(TX),
                        lambda dve, linked, j, t, bank: dve.tensor_copy(V[:, t, :], bank[:]), "ev_v")
            forget_gate(core, hT, nlf, "ev_f")
            pool_mix(core, U, catT[:, 4:8, :], "ev_pool")
            forgetting_attention(core, QT, KTt, V, nlf, catT[:, 0:4, :], "ev_pool")
        gemm_tokens(core, lambda k, t: catT[:, k, tile_cols(t)], [[(f"ev_out{j}", range(KT))] for j in range(2)],
                    range(TX), lambda dve, linked, j, t, bank: dve.tensor_copy(
                        M[:, t, j * 512:(j + 1) * 512], bank[:]), "ev_out1")
        add_normed(core, X, M, core.dram["mix_post_g_2"][0])


def odd_layer(core, X):
    with ExitStack() as own:
        hT = core.sb(own, "hT", KT, NX)
        M = core.sb(own, "mixed", TX, D)
        plain_norm(core, X, hT, M, "mix_pre_g_2", 1, "ffn0_down1_2")
        gate = core.sb(own, "lru_gate", KT, NX)
        raw = core.sb(own, "lru_raw", KT, 3 + NX)
        xr = core.sb(own, "lru_x", KT, NX)
        y = core.sb(own, "lru_y", KT, NX)
        vector_ops(core, [lambda dve: dve.memset(raw[:, :, 0:3], 0.0)])
        jobs = [(f"od_in{c // 4}", c % 4, gate[:, c, :], ACT.Gelu_apprx_tanh) for c in range(KT)]
        jobs += [(f"od_in{2 + c // 4}", c % 4, raw[:, c, 3:], ACT.Copy) for c in range(KT)]
        project_channels(core, hT, jobs, "od_in3")
        lru_conv(core, raw, xr)
        lru(core, xr, gate, y, "od_x")
        gemm_tokens(core, lambda k, t: y[:, k, tile_cols(t)], [[(f"od_out{j}", range(KT))] for j in range(2)],
                    range(TX), lambda dve, linked, j, t, bank: dve.tensor_copy(
                        M[:, t, j * 512:(j + 1) * 512], bank[:]), "od_out1")
        add_normed(core, X, M, core.dram["mix_post_g_2"][1])


def final_norm(core, X):
    with ExitStack() as own:
        junk = core.sb(own, "squares", D)
        inv = core.sb(own, "inverse_rms", TX)
        gain = core.sb(own, "gain_row", D)
        load_x(core, gain[:], core.dram["final_norm_g"].partition_broadcast(P))
        rms_rows(core, lambda t: X[:, t, :], junk[:], inv[:], TX, D)
        vector_ops(core, [lambda dve, t=t: dve.scalar_tensor_tensor(
            out=X[:, t, :], in0=X[:, t, :], scalar=inv[:, t:t + 1], in1=gain[:], op0=ALU.mult, op1=ALU.mult)
            for t in range(TX)])


def program(nc, dram, out):
    with ExitStack() as ctx:
        core = Core(nc, ctx, dram)
        core.ring = Ring(nc, ctx, 3)
        core.mod = core.sb(ctx, "mod", 48, 2)
        core.factor = core.sb(ctx, "factor", 2, KT, 2)
        core.x_dram = nc.dram_tensor("residual", (P, TT, D), F32, kind="Internal").ap()
        plan(core)
        constants(core)
        ada(core, 0)
        gdn_layer(core)
        with ExitStack() as own:
            X = core.sb(own, "X", TT, D)
            load_x(core, X[:], core.x_dram)
            moe_layer(core, 0, X, list(range(TT)))
            store(core, core.x_dram, X[:])
        ada(core, 1)
        ssd_layer(core)
        with ExitStack() as own:
            X = core.sb(own, "X", TX, D)
            load_x(core, X[:], core.x_dram[:, TC:TT, :])
            moe_layer(core, 1, X, list(range(TC, TT)))
            final_norm(core, X)
            even_layer(core, X)
            swiglu_layer(core, X, 0, "ev_out1")
            odd_layer(core, X)
            swiglu_layer(core, X, 1, "od_out1")
            store(core, out.rearrange("o (t p) n -> p (o t) n", p=P), X[:])


INPUTS = ["x", "c", "ctx", "c_ctx", "ada_w", "ada_b", "norm1_g", "norm2_g", "router_w", "moe_w_gate",
          "moe_w_up", "moe_w_down", "gdn_w_in", "gdn_conv_w", "gdn_a_log", "gdn_dt_bias", "gdn_norm_g",
          "gdn_w_out", "ssd_w_in", "ssd_conv_w", "ssd_conv_b", "ssd_a_log", "ssd_dt_bias", "ssd_d",
          "ssd_norm_g", "ssd_w_out", "final_norm_g", "mix_pre_g_2", "mix_post_g_2", "ffn_pre_g_2",
          "ffn_post_g_2", "ffn_w_gate_2", "ffn_w_up_2", "ffn_w_down_2", "ev_w_in_2", "ev_b_f_2",
          "ev_pool_w_2", "ev_pool_scale_2", "ev_w_out_2", "od_w_in_2", "od_conv_w_2", "od_conv_b_2",
          "od_w_a_2", "od_b_a_2", "od_w_x_2", "od_b_x_2", "od_lam_2", "od_w_out_2"]


def kernel(**inputs):
    import concourse.bacc as bacc
    from concourse.bass_utils import run_bass_kernel_spmd

    nc = bacc.Bacc("TRN2", target_bir_lowering=False, num_devices=1)
    arrays, dram = {}, {}
    for name in INPUTS:
        a = np.ascontiguousarray(inputs[name])
        arrays[f"in_{name}"] = a
        dram[name] = nc.dram_tensor(f"in_{name}", a.shape, F32, kind="ExternalInput").ap()
    out = nc.dram_tensor("out", (1, NX, D), F32, kind="ExternalOutput").ap()
    program(nc, dram, out)
    result = run_bass_kernel_spmd(nc, [arrays], core_ids=[0])
    return result.results[0]["out"]
```
